# Optimizing a Trainium2 kernel written in Bass

```python
import jax
import jax.numpy as jnp
from jax import lax
import numpy as np
import jax, jax.numpy as jnp

D_MODEL = 1024
BATCH = 1
SEQ = 2048
DEPTH = 1

N_GROUPS = 5
HEAD_DIM = 64
GROUP_HEADS = 4
GROUP_W = GROUP_HEADS * HEAD_DIM
MIX_W = N_GROUPS * GROUP_W
N_MEM = 256
CHUNK = 128
CONV_K = 4
RWKV_DECAY_RANK = 16
RWKV_A_RANK = 16
EPS = 1e-6

A_COLS = (GROUP_W, GROUP_W, GROUP_W)
B_COLS = (GROUP_W, GROUP_W, GROUP_W, GROUP_HEADS, GROUP_W)
C_COLS = (2 * GROUP_W, GROUP_W, GROUP_HEADS, GROUP_HEADS, GROUP_W, GROUP_W)
D_COLS = (GROUP_W, RWKV_DECAY_RANK, GROUP_W, GROUP_W, RWKV_A_RANK, GROUP_W)
M_COLS = (GROUP_W, GROUP_W)
GROUP_COLS = (sum(A_COLS), sum(B_COLS), sum(C_COLS), sum(D_COLS), sum(M_COLS))
D_W = sum(D_COLS)
IN_COLS = sum(GROUP_COLS)


def rms_norm(x, g):
    xf = x.astype(jnp.float32)
    y = xf * lax.rsqrt(jnp.mean(xf * xf, axis=-1, keepdims=True) + EPS)
    return (y * g.astype(jnp.float32)).astype(x.dtype)

def split_cols(x, widths):
    return jnp.split(x, np.cumsum(widths)[:-1].tolist(), axis=-1)

def to_heads(t):
    return t.reshape(t.shape[:-1] + (GROUP_HEADS, HEAD_DIM))

def causal_dwconv(x, w, b):
    y = lax.conv_general_dilated(
        x, w[:, None, :].astype(x.dtype), (1,), [(CONV_K - 1, 0)],
        dimension_numbers=("NWC", "WIO", "NWC"), feature_group_count=x.shape[-1])
    return y + b

def token_shift(x, mu):
    prev = jnp.pad(x, ((0, 0), (1, 0), (0, 0)))[:, :-1]
    return x + mu * (prev - x)

def spatial_gating(u, v, norm_g, w_s, b_s):
    bsz, seq, _ = u.shape
    nc = seq // CHUNK
    u = jax.nn.gelu(u)
    v = rms_norm(to_heads(jax.nn.gelu(v)), norm_g.reshape(GROUP_HEADS, HEAD_DIM))
    v = v.reshape(bsz, nc, CHUNK, GROUP_HEADS, HEAD_DIM)
    w = jnp.where(jnp.tril(jnp.ones((CHUNK, CHUNK), bool)), w_s, jnp.zeros_like(w_s))
    mixed = jnp.einsum("gts,bcsgd->bctgd", w, v) + b_s.T[:, :, None]
    return u * mixed.reshape(bsz, seq, GROUP_W)

def forgetting_attention(q, k, v, f_logit, q_g, k_g):
    bsz, seq, _ = q.shape
    nb = seq // CHUNK
    q = rms_norm(to_heads(q), q_g)
    k = rms_norm(to_heads(k), k_g)
    v = to_heads(v)
    big_f = jnp.cumsum(jax.nn.log_sigmoid(f_logit.astype(jnp.float32)), axis=1)
    big_f = big_f.transpose(0, 2, 1)
    q_blocks = q.reshape(bsz, nb, CHUNK, GROUP_HEADS, HEAD_DIM).swapaxes(0, 1)
    f_blocks = big_f.reshape(bsz, GROUP_HEADS, nb, CHUNK).transpose(2, 0, 1, 3)
    k_pos = jnp.arange(seq)
    scale = HEAD_DIM ** -0.5

    def one_block(args):
        qb, fb, start = args
        s = jnp.einsum("bthd,bshd->bhts", qb, k).astype(jnp.float32) * scale
        s = s + fb[..., :, None] - big_f[..., None, :]
        q_pos = start + jnp.arange(CHUNK)
        s = jnp.where(k_pos[None, :] <= q_pos[:, None], s, -jnp.inf)
        p = jax.nn.softmax(s, axis=-1).astype(v.dtype)
        return jnp.einsum("bhts,bshd->bthd", p, v)

    out = lax.map(one_block, (q_blocks, f_blocks, jnp.arange(nb) * CHUNK))
    return out.swapaxes(0, 1).reshape(bsz, seq, GROUP_W)

def mlstm(qk, v, i_logit, f_logit, o_logit, conv_w, conv_b, out_g):
    f32 = jnp.float32
    bsz, seq, _ = v.shape
    nc = seq // CHUNK
    q, k = jnp.split(jax.nn.silu(causal_dwconv(qk, conv_w, conv_b)), 2, axis=-1)
    q = to_heads(q).astype(f32)
    k = to_heads(k).astype(f32) * HEAD_DIM ** -0.5
    vh = to_heads(v).astype(f32)
    log_i = i_logit.astype(f32)
    log_f = jax.nn.log_sigmoid(f_logit.astype(f32))

    def chunks(t):
        return t.reshape((bsz, nc, CHUNK) + t.shape[2:]).swapaxes(0, 1)

    causal = jnp.tril(jnp.ones((CHUNK, CHUNK), bool))

    def step(carry, inp):
        c_state, n_state, m_state = carry
        qc, kc, vc, ic, fc = inp
        b = jnp.cumsum(fc, axis=1).swapaxes(1, 2)
        ic = ic.swapaxes(1, 2)
        g = b[..., -1]
        log_d = jnp.where(causal, b[..., :, None] - b[..., None, :] + ic[..., None, :], -jnp.inf)
        inter = b + m_state[..., None]
        m_t = jnp.maximum(jnp.max(log_d, axis=-1), inter)
        s = jnp.einsum("bthd,bshd->bhts", qc, kc) * jnp.exp(log_d - m_t[..., None])
        w_inter = jnp.exp(inter - m_t)
        num = (jnp.einsum("bhts,bshd->bhtd", s, vc)
               + w_inter[..., None] * jnp.einsum("bthk,bhkd->bhtd", qc, c_state))
        den = jnp.sum(s, axis=-1) + w_inter * jnp.einsum("bthk,bhk->bht", qc, n_state)
        h = num / jnp.maximum(jnp.abs(den), jnp.exp(-m_t))[..., None]
        log_w = g[..., None] - b + ic
        m_new = jnp.maximum(g + m_state, jnp.max(log_w, axis=-1))
        w_new = jnp.exp(log_w - m_new[..., None])
        carry_decay = jnp.exp(g + m_state - m_new)
        c_state = carry_decay[..., None, None] * c_state + jnp.einsum("bhs,bshk,bshd->bhkd", w_new, kc, vc)
        n_state = carry_decay[..., None] * n_state + jnp.einsum("bhs,bshk->bhk", w_new, kc)
        return (c_state, n_state, m_new), h.swapaxes(1, 2)

    init = (jnp.zeros((bsz, GROUP_HEADS, HEAD_DIM, HEAD_DIM), f32),
            jnp.zeros((bsz, GROUP_HEADS, HEAD_DIM), f32),
            jnp.zeros((bsz, GROUP_HEADS), f32))
    _, h = lax.scan(step, init, (chunks(q), chunks(k), chunks(vh), chunks(log_i), chunks(log_f)))
    h = h.swapaxes(0, 1).reshape(bsz, seq, GROUP_HEADS, HEAD_DIM)
    h = jax.nn.sigmoid(to_heads(o_logit).astype(f32)) * h
    return rms_norm(h, out_g.reshape(GROUP_HEADS, HEAD_DIM)).reshape(bsz, seq, GROUP_W)

def rwkv7_time_mix(r, w_lo, k, v, a_lo, w0, w2, a0, a2, k_k, k_a, r_k, ln_g):
    f32 = jnp.float32
    bsz, seq, _ = r.shape
    r, w_lo, k, v, a_lo = (t.astype(f32) for t in (r, w_lo, k, v, a_lo))
    w_log = -jax.nn.softplus(-(w0 + jnp.tanh(w_lo) @ w2)) - 0.5
    decay = jnp.exp(-jnp.exp(w_log))
    a = jax.nn.sigmoid(a0 + a_lo @ a2)
    kk = to_heads(k * k_k)
    kk = kk / jnp.maximum(jnp.linalg.norm(kk, axis=-1, keepdims=True), 1e-12)
    k = k * (1 + (a - 1) * k_a)
    rh, dh, kh, vh, ah = (to_heads(t) for t in (r, decay, k, v, a))

    def step(state, inp):
        r_t, w_t, k_t, v_t, kk_t, a_t = inp
        sa = jnp.einsum("bhvk,bhk->bhv", state, -kk_t)
        state = (state * w_t[:, :, None, :] + sa[..., None] * (kk_t * a_t)[:, :, None, :]
                 + v_t[..., None] * k_t[:, :, None, :])
        return state, jnp.einsum("bhvk,bhk->bhv", state, r_t)

    init = jnp.zeros((bsz, GROUP_HEADS, HEAD_DIM, HEAD_DIM), f32)
    _, y = lax.scan(step, init, tuple(t.swapaxes(0, 1) for t in (rh, dh, kh, vh, kk, ah)))
    y = rms_norm(y.swapaxes(0, 1), ln_g.reshape(GROUP_HEADS, HEAD_DIM))
    y = y + jnp.sum(rh * kh * r_k, axis=-1, keepdims=True) * vh
    return y.reshape(bsz, seq, GROUP_W)

def memory_attention(q, mem_n, w_kv, q_g, k_g):
    bsz, seq, _ = q.shape
    k, v = jnp.split(mem_n @ w_kv, 2, axis=-1)
    q = rms_norm(to_heads(q), q_g)
    k = rms_norm(to_heads(k), k_g)
    v = to_heads(v)
    s = jnp.einsum("bthd,bmhd->bhtm", q, k).astype(jnp.float32) * HEAD_DIM ** -0.5
    p = jax.nn.softmax(s, axis=-1).astype(v.dtype)
    return jnp.einsum("bhtm,bmhd->bthd", p, v).reshape(bsz, seq, GROUP_W)

def hybrid_layer(x, mem, norm_g, w_in, w_out, sgu_norm_g, sgu_w, sgu_b,
                 fox_q_g, fox_k_g, fox_f_b,
                 mlstm_conv_w, mlstm_conv_b, mlstm_i_b, mlstm_f_b, mlstm_out_g,
                 rwkv_mu, rwkv_w0, rwkv_w2, rwkv_a0, rwkv_a2, rwkv_k_k, rwkv_k_a, rwkv_r_k, rwkv_ln_g,
                 mem_norm_g, mem_w_kv, mem_q_g, mem_k_g):
    h = rms_norm(x, norm_g)
    proj = h @ w_in
    pa, pb, pc, pd, pm = split_cols(proj, GROUP_COLS)

    a_u, a_v, a_z = split_cols(pa, A_COLS)
    ya = spatial_gating(a_u, a_v, sgu_norm_g, sgu_w, sgu_b)

    b_q, b_k, b_v, b_f, b_z = split_cols(pb, B_COLS)
    yb = forgetting_attention(b_q, b_k, b_v, b_f + fox_f_b, fox_q_g, fox_k_g)

    c_qk, c_v, c_i, c_f, c_o, c_z = split_cols(pc, C_COLS)
    yc = mlstm(c_qk, c_v, c_i + mlstm_i_b, c_f + mlstm_f_b, c_o, mlstm_conv_w, mlstm_conv_b, mlstm_out_g)

    d_r, d_wlo, d_k, d_v, d_alo, d_z = split_cols(token_shift(pd, rwkv_mu), D_COLS)
    yd = rwkv7_time_mix(d_r, d_wlo, d_k, d_v, d_alo, rwkv_w0, rwkv_w2, rwkv_a0, rwkv_a2,
                        rwkv_k_k, rwkv_k_a, rwkv_r_k, rwkv_ln_g)

    m_q, m_z = split_cols(pm, M_COLS)
    ym = memory_attention(m_q, rms_norm(mem, mem_norm_g), mem_w_kv, mem_q_g, mem_k_g)

    branches = [(ya, a_z), (yb, b_z), (yc, c_z), (yd, d_z), (ym, m_z)]
    mixed = jnp.concatenate([y.astype(x.dtype) * jax.nn.silu(z) for y, z in branches], axis=-1)
    return x + mixed @ w_out

def first_inputs(seed: int = 0) -> dict:
    key = jax.random.key(seed)
    ks = iter(jax.random.split(key, 32))
    f32 = jnp.float32

    def nrm(shape, scale):
        return jax.random.normal(next(ks), shape, f32) * scale

    def uni(shape, lo, hi):
        return jax.random.uniform(next(ks), shape, f32, lo, hi)

    def gain(shape):
        return 1.0 + nrm(shape, 0.1)

    L = DEPTH
    return {
        "x": nrm((BATCH, SEQ, D_MODEL), 1.0),
        "mem": nrm((BATCH, N_MEM, D_MODEL), 1.0),
        "norm_g": gain((L, D_MODEL)),
        "w_in": nrm((L, D_MODEL, IN_COLS), D_MODEL ** -0.5),
        "w_out": nrm((L, MIX_W, D_MODEL), MIX_W ** -0.5),
        "sgu_norm_g": gain((L, GROUP_W)),
        "sgu_w": nrm((L, GROUP_HEADS, CHUNK, CHUNK), 0.5 * CHUNK ** -0.5),
        "sgu_b": gain((L, GROUP_HEADS, CHUNK)),
        "fox_q_g": gain((L, HEAD_DIM)),
        "fox_k_g": gain((L, HEAD_DIM)),
        "fox_f_b": uni((L, GROUP_HEADS), 1.0, 5.0),
        "mlstm_conv_w": nrm((L, CONV_K, 2 * GROUP_W), CONV_K ** -0.5),
        "mlstm_conv_b": nrm((L, 2 * GROUP_W), 0.02),
        "mlstm_i_b": nrm((L, GROUP_HEADS), 0.1),
        "mlstm_f_b": uni((L, GROUP_HEADS), 3.0, 6.0),
        "mlstm_out_g": gain((L, GROUP_W)),
        "rwkv_mu": uni((L, D_W), 0.0, 1.0),
        "rwkv_w0": uni((L, GROUP_W), -4.0, 0.0),
        "rwkv_w2": nrm((L, RWKV_DECAY_RANK, GROUP_W), 0.5 * RWKV_DECAY_RANK ** -0.5),
        "rwkv_a0": nrm((L, GROUP_W), 0.1),
        "rwkv_a2": nrm((L, RWKV_A_RANK, GROUP_W), 0.5 * RWKV_A_RANK ** -0.5),
        "rwkv_k_k": 0.85 + nrm((L, GROUP_W), 0.05),
        "rwkv_k_a": gain((L, GROUP_W)),
        "rwkv_r_k": nrm((L, GROUP_HEADS, HEAD_DIM), 0.1),
        "rwkv_ln_g": gain((L, GROUP_W)),
        "mem_norm_g": gain((L, D_MODEL)),
        "mem_w_kv": nrm((L, D_MODEL, 2 * GROUP_W), D_MODEL ** -0.5),
        "mem_q_g": gain((L, HEAD_DIM)),
        "mem_k_g": gain((L, HEAD_DIM)),
    }

def first_block(x, mem, norm_g, w_in, w_out, sgu_norm_g, sgu_w, sgu_b,
              fox_q_g, fox_k_g, fox_f_b,
              mlstm_conv_w, mlstm_conv_b, mlstm_i_b, mlstm_f_b, mlstm_out_g,
              rwkv_mu, rwkv_w0, rwkv_w2, rwkv_a0, rwkv_a2, rwkv_k_k, rwkv_k_a, rwkv_r_k, rwkv_ln_g,
              mem_norm_g, mem_w_kv, mem_q_g, mem_k_g):
    stacked = (norm_g, w_in, w_out, sgu_norm_g, sgu_w, sgu_b,
               fox_q_g, fox_k_g, fox_f_b,
               mlstm_conv_w, mlstm_conv_b, mlstm_i_b, mlstm_f_b, mlstm_out_g,
               rwkv_mu, rwkv_w0, rwkv_w2, rwkv_a0, rwkv_a2, rwkv_k_k, rwkv_k_a, rwkv_r_k, rwkv_ln_g,
               mem_norm_g, mem_w_kv, mem_q_g, mem_k_g)
    for layer in range(DEPTH):
        x = hybrid_layer(x, mem, *[p[layer] for p in stacked])
    return x


CTX_LEN = 256
GRID_W = 64
F_WIDTH = D_MODEL // 2
F_GROUPS = 4
F_GROUP_DIM = F_WIDTH // F_GROUPS
NA_WIDTH = D_MODEL - F_WIDTH
NA_HEADS = NA_WIDTH // HEAD_DIM
MIX_WIDTH = F_WIDTH + NA_WIDTH
IN_COLS_2 = 2 * F_WIDTH + 4 * NA_WIDTH
WIN_ROWS_MAX = 8
WIN_COLS = 16
NEG_INF = -1e30


def _rms_norm(t, g):
    t32 = t.astype(jnp.float32)
    y = t32 * lax.rsqrt(jnp.mean(t32 * t32, axis=-1, keepdims=True) + EPS)
    return (y * g.astype(jnp.float32)).astype(t.dtype)

def _ada(cond, w_ada, b_ada):
    mod = jax.nn.silu(cond) @ w_ada + b_ada
    return jnp.split(mod, 3, axis=-1)

def _split_proj(p):
    f_in = p[..., :F_WIDTH]
    f_gate = p[..., F_WIDTH:2 * F_WIDTH]
    q, k, v, na_gate = jnp.split(p[..., 2 * F_WIDTH:], 4, axis=-1)
    return f_in, f_gate, q, k, v, na_gate

def _heads(t):
    return t.reshape(t.shape[0], t.shape[1], NA_HEADS, HEAD_DIM)

def _fourier(u, w_four):
    b, l, _ = u.shape
    ug = u.reshape(b, l, F_GROUPS, F_GROUP_DIM).astype(jnp.float32)
    y = jnp.real(jnp.fft.fft2(ug, axes=(1, 3))) * ((l * F_GROUP_DIM) ** -0.5)
    y = y.reshape(b, l, F_WIDTH).astype(u.dtype)
    return y @ w_four

def _ctx_attention(qc, kc, vc):
    s = jnp.einsum('bqhd,bkhd->bhqk', qc, kc, preferred_element_type=jnp.float32) * (HEAD_DIM ** -0.5)
    p = jax.nn.softmax(s, axis=-1).astype(vc.dtype)
    o = jnp.einsum('bhqk,bkhd->bqhd', p, vc)
    return o.reshape(o.shape[0], o.shape[1], NA_WIDTH)

def _neighbourhood_attention(q, k, v, kc, vc, rel_bias):
    b, l, h, d = q.shape
    rows = l // GRID_W
    wr = min(WIN_ROWS_MAX, rows)
    r_ar = jnp.arange(rows)
    rs = jnp.clip(r_ar - wr // 2, 0, rows - wr)
    row_idx = rs[:, None] + jnp.arange(wr)[None, :]
    col_ar = jnp.arange(GRID_W)
    cs = jnp.clip(col_ar - WIN_COLS // 2, 0, GRID_W - WIN_COLS)
    in_win = (col_ar[None, :] >= cs[:, None]) & (col_ar[None, :] < cs[:, None] + WIN_COLS)
    mask = jnp.broadcast_to(in_win[:, None, :], (GRID_W, wr, GRID_W)).reshape(GRID_W, wr * GRID_W)
    dr_idx = row_idx - r_ar[:, None] + (WIN_ROWS_MAX - 1)
    dc_idx = jnp.clip(col_ar[None, :] - col_ar[:, None], -(WIN_COLS - 1), WIN_COLS - 1) + (WIN_COLS - 1)
    bias = rel_bias[:, dr_idx[:, None, :, None], dc_idx[None, :, None, :]]
    bias = bias.reshape(h, rows, GRID_W, wr * GRID_W).astype(jnp.float32)
    qg = q.reshape(b, rows, GRID_W, h, d)
    k_rows = k.reshape(b, rows, GRID_W, h, d)[:, row_idx].reshape(b, rows, wr * GRID_W, h, d)
    v_rows = v.reshape(b, rows, GRID_W, h, d)[:, row_idx].reshape(b, rows, wr * GRID_W, h, d)
    scale = HEAD_DIM ** -0.5
    s_loc = jnp.einsum('brqhd,brkhd->bhrqk', qg, k_rows, preferred_element_type=jnp.float32) * scale
    s_loc = jnp.where(mask[None, None, None], s_loc + bias[None], NEG_INF)
    s_ctx = jnp.einsum('brqhd,bkhd->bhrqk', qg, kc, preferred_element_type=jnp.float32) * scale
    p = jax.nn.softmax(jnp.concatenate([s_loc, s_ctx], axis=-1), axis=-1).astype(v.dtype)
    n_loc = wr * GRID_W
    o = (jnp.einsum('bhrqk,brkhd->brqhd', p[..., :n_loc], v_rows)
         + jnp.einsum('bhrqk,bkhd->brqhd', p[..., n_loc:], vc))
    return o.reshape(b, l, NA_WIDTH)

def second_inputs(seed: int = 0) -> dict:
    key = jax.random.key(seed)
    ks = jax.random.split(key, 14)
    f32 = jnp.float32
    n = lambda k, shape: jax.random.normal(k, shape, f32)
    return {
        "x": n(ks[0], (BATCH, SEQ, D_MODEL)),
        "c": n(ks[1], (BATCH, D_MODEL)),
        "ctx": n(ks[2], (BATCH, CTX_LEN, D_MODEL)),
        "c_ctx": n(ks[3], (D_MODEL,)),
        "norm_g": 1.0 + 0.02 * n(ks[4], (DEPTH, D_MODEL)),
        "w_ada": n(ks[5], (DEPTH, D_MODEL, 3 * D_MODEL)) * D_MODEL ** -0.5,
        "b_ada": 0.02 * n(ks[6], (DEPTH, 3 * D_MODEL)),
        "w_in": n(ks[7], (DEPTH, D_MODEL, IN_COLS_2)) * D_MODEL ** -0.5,
        "w_four": n(ks[8], (DEPTH, F_WIDTH, F_WIDTH)) * F_WIDTH ** -0.5,
        "q_norm_g": 1.0 + 0.02 * n(ks[9], (DEPTH, HEAD_DIM)),
        "k_norm_g": 1.0 + 0.02 * n(ks[10], (DEPTH, HEAD_DIM)),
        "rel_bias": 0.02 * n(ks[11], (DEPTH, NA_HEADS, 2 * WIN_ROWS_MAX - 1, 2 * WIN_COLS - 1)),
        "w_out": n(ks[12], (DEPTH, MIX_WIDTH, D_MODEL)) * MIX_WIDTH ** -0.5,
    }

def second_block(x, c, ctx, c_ctx, norm_g, w_ada, b_ada, w_in, w_four, q_norm_g, k_norm_g, rel_bias, w_out):
    for l in range(DEPTH):
        last = l == DEPTH - 1
        sh_x, sc_x, g_x = [t[:, None, :] for t in _ada(c, w_ada[l], b_ada[l])]
        sh_c, sc_c, g_c = _ada(c_ctx, w_ada[l], b_ada[l])
        xn = _rms_norm(x, norm_g[l]) * (1.0 + sc_x) + sh_x
        cn = _rms_norm(ctx, norm_g[l]) * (1.0 + sc_c) + sh_c
        fx_in, fx_gate, qx, kx, vx, nx_gate = _split_proj(xn @ w_in[l])
        fc_in, fc_gate, qc, kc, vc, nc_gate = _split_proj(cn @ w_in[l])
        qx = _rms_norm(_heads(qx), q_norm_g[l])
        kx = _rms_norm(_heads(kx), k_norm_g[l])
        vx = _heads(vx)
        qc = _rms_norm(_heads(qc), q_norm_g[l])
        kc = _rms_norm(_heads(kc), k_norm_g[l])
        vc = _heads(vc)
        f_out = _fourier(fx_in, w_four[l]) * jax.nn.silu(fx_gate)
        na_out = _neighbourhood_attention(qx, kx, vx, kc, vc, rel_bias[l]) * jax.nn.silu(nx_gate)
        x_new = x + g_x * (jnp.concatenate([f_out, na_out], axis=-1) @ w_out[l])
        if not last:
            fc_out = _fourier(fc_in, w_four[l]) * jax.nn.silu(fc_gate)
            nc_out = _ctx_attention(qc, kc, vc) * jax.nn.silu(nc_gate)
            ctx = ctx + g_c * (jnp.concatenate([fc_out, nc_out], axis=-1) @ w_out[l])
        x = x_new
    return x


def setup_inputs(seed=0):
    out = dict(first_inputs(seed))
    for name, value in second_inputs(seed + 1).items():
        if name != "x":
            out[name + "_2"] = value
    return out


def reference(
    x, mem, norm_g, w_in, w_out, sgu_norm_g, sgu_w, sgu_b, fox_q_g, fox_k_g, fox_f_b,
    mlstm_conv_w, mlstm_conv_b, mlstm_i_b, mlstm_f_b, mlstm_out_g, rwkv_mu, rwkv_w0, rwkv_w2,
    rwkv_a0, rwkv_a2, rwkv_k_k, rwkv_k_a, rwkv_r_k, rwkv_ln_g, mem_norm_g, mem_w_kv, mem_q_g,
    mem_k_g, c_2, ctx_2, c_ctx_2, norm_g_2, w_ada_2, b_ada_2, w_in_2, w_four_2, q_norm_g_2,
    k_norm_g_2, rel_bias_2, w_out_2,
):
    x = first_block(
        x, mem, norm_g, w_in, w_out, sgu_norm_g, sgu_w, sgu_b, fox_q_g, fox_k_g, fox_f_b,
        mlstm_conv_w, mlstm_conv_b, mlstm_i_b, mlstm_f_b, mlstm_out_g, rwkv_mu, rwkv_w0,
        rwkv_w2, rwkv_a0, rwkv_a2, rwkv_k_k, rwkv_k_a, rwkv_r_k, rwkv_ln_g, mem_norm_g,
        mem_w_kv, mem_q_g, mem_k_g,
    )
    return second_block(
        x, c_2, ctx_2, c_ctx_2, norm_g_2, w_ada_2, b_ada_2, w_in_2, w_four_2, q_norm_g_2,
        k_norm_g_2, rel_bias_2, w_out_2,
    )


_drawn_inputs = setup_inputs


def setup_inputs(seed=0):
    import zlib

    import numpy as np

    out = dict(_drawn_inputs(seed))
    spreads = {}
    factors = {'sgu_norm_g': 8.0,
     'sgu_b': 3.372,
     'fox_q_g': 8.0,
     'fox_k_g': 7.627,
     'mlstm_conv_b': 8.0,
     'mlstm_i_b': 200.0,
     'rwkv_w2': 6.821,
     'rwkv_a0': 6.398,
     'rwkv_k_k': 200.0,
     'rwkv_k_a': 2.72,
     'mem_norm_g': 8.0,
     'mem_q_g': 8.0,
     'mem_k_g': 8.0,
     'norm_g_2': 7.07,
     'b_ada_2': 3.529,
     'q_norm_g_2': 8.0,
     'k_norm_g_2': 8.0,
     'rel_bias_2': 47.178}
    for name, (base, spread) in spreads.items():
        noise = np.random.default_rng([zlib.crc32(name.encode()), seed]).standard_normal(out[name].shape)
        drawn = base * np.exp(spread * noise) if base else spread * noise
        out[name] = jnp.asarray(drawn.astype(out[name].dtype))
    for name, factor in factors.items():
        out[name] = (out[name] * factor).astype(out[name].dtype)
    return out
```

```python
from contextlib import ExitStack

import numpy as np

import concourse.bass as bass
from concourse import mybir

F32 = mybir.dt.float32
U32 = mybir.dt.uint32
ALU = mybir.AluOpType
ACT = mybir.ActivationFunctionType
AX = mybir.AxisListType

P = 128
T = 2048
NT = T // P
DM = 1024
KB = DM // P
HD = 64
GH = 4
GW = GH * HD
NMEM = 256
EPS = 1e-6
MASKED = -1e30
BANK = 512


class Phase:

    def __init__(self, nc, name):
        self.nc, self.name, self.ctx, self.sems = nc, name, ExitStack(), []

    def sb(self, name, shape, dt=F32):
        return self.ctx.enter_context(self.nc.sbuf_tensor(f"{self.name}_{name}", shape, dt))

    def ps(self, name, shape, dt=F32):
        return self.ctx.enter_context(self.nc.psum_tensor(f"{self.name}_psum_{name}", shape, dt))

    def sem(self, name):
        s = self.ctx.enter_context(self.nc.semaphore(f"{self.name}_{name}"))
        self.sems.append(s)
        return s

    def close(self):
        for s in self.sems:
            self.nc.sync.sem_clear(s)
        self.nc.all_engine_barrier()
        self.ctx.close()


def along(column, n):
    return column.unsqueeze(2).to_broadcast([column.shape[0], column.shape[1], n])


def heads(ap, n=HD):
    return ap.rearrange("p (h d) -> p h d", d=n)


def wait_apart(eng, sem, value, taken):
    eng.wait_ge(sem, value)
    eng.sem_inc(taken, 1)


def tile_of(dram, i):
    return dram[bass.ds(i * P, P), :]


def cols_of(dram, i):
    return dram.rearrange("(b p) t -> p b t", p=P)[:, :, bass.ds(i * P, P)]


def consts_phase(nc, g):
    ph = Phase(nc, "const")
    ones_ready = ph.sem("ones_ready")
    with nc.Block() as block:
        @block.gpsimd
        def _(pool):
            nc.gpsimd.memset(g.ident[:], 0.0)
            pool.drain()
            nc.gpsimd.affine_select(out=g.ident[:], in_=g.ident[:], compare_op=ALU.not_equal, fill=1.0, base=0,
                                    pattern=[[-1, P]], channel_multiplier=1)
            nc.gpsimd.memset(g.neg_half[:], -0.5)
            nc.gpsimd.memset(g.eps[:], EPS)
            nc.gpsimd.memset(g.head_eps[:], HD * EPS)
            nc.gpsimd.memset(g.one[:], 1.0).then_inc(ones_ready, 1)
    ph.close()


def tile_pass_1(nc, d, g, hT):
    ph = Phase(nc, "p1")
    sb, ps, sem = ph.sb, ph.ps, ph.sem
    NQ = 12
    w = sb("w", [P, KB, 4 * BANK])
    xt, junk, xs = sb("xt", [P, DM]), sb("junk", [P, DM]), sb("xs", [P, DM])
    norm_gain = sb("norm_gain", [P, DM])
    x_sq, x_var, x_rstd = sb("x_sq", [P, 1]), sb("x_var", [P, 1]), sb("x_rstd", [P, 1])
    h_slot = sb("h_slot", [P, KB, P])
    uv, vn, v2 = sb("uv", [P, 2 * GW]), sb("vn", [P, GW]), sb("v2", [P, GW])
    v_sq, v_var, v_rstd = sb("v_sq", [P, GH]), sb("v_var", [P, GH]), sb("v_rstd", [P, GH])
    sgu_gain, sgu_w, sgu_b = sb("sgu_gain", [P, GW]), sb("sgu_w", [P, GH, P]), sb("sgu_b", [P, GH])
    mixed, y_out = sb("mixed", [P, GW]), sb("y_out", [P, GW])
    qkm, qkm2 = sb("qkm", [P, NQ * HD]), sb("qkm2", [P, NQ * HD])
    q_sq, q_var, q_rstd = sb("q_sq", [P, NQ]), sb("q_var", [P, NQ]), sb("q_rstd", [P, NQ])
    qk_gain = sb("qk_gain", [P, NQ * HD])
    qkT_out = sb("qkT_out", [P, NQ // 2, P])
    v_out, c_out = sb("v_out", [P, GW]), sb("c_out", [P, 2 * GW])
    p_xT = ps("xT", [P, KB, P])
    p_proj = [ps(f"proj{n}", [P, BANK]) for n in range(4)]
    p_mix, p_qkT = ps("mix", [P, BANK]), ps("qkT", [P, BANK // P, P])

    const_in, x_in = sem("const_in"), sem("x_in")
    gains_ready, w_masked = sem("gains_ready"), sem("w_masked")
    x_sq_ready, x_rstd_ready, xs_ready, xt_free = sem("x_sq_ready"), sem("x_rstd_ready"), sem("xs_ready"), sem("xt_free")
    xT_ready, h_ready, h_free, hT_copied = sem("xT_ready"), sem("h_ready"), sem("h_free"), sem("hT_copied")
    proj_ready = [sem(f"proj{n}_ready") for n in range(4)]
    proj_free = [sem(f"proj{n}_free") for n in range(4)]
    uv_ready, uv_free, v_sq_ready, v_rstd_ready, vn_ready = (sem("uv_ready"), sem("uv_free"), sem("v_sq_ready"),
                                                             sem("v_rstd_ready"), sem("vn_ready"))
    mix_ready, mix_free, y_ready, y_stored = sem("mix_ready"), sem("mix_free"), sem("y_ready"), sem("y_stored")
    qk_ready, mq_ready, q_sq_ready, q_rstd_ready, qkn_ready, qkm_free = (
        sem("qk_ready"), sem("mq_ready"), sem("q_sq_ready"), sem("q_rstd_ready"), sem("qkn_ready"), sem("qkm_free"))
    qkT_ready, qkT_free, qkT_out_ready, qkT_stored = (sem("qkT_ready"), sem("qkT_free"), sem("qkT_out_ready"),
                                                      sem("qkT_stored"))
    v_ready, v_stored, c_ready, c_stored = sem("v_ready"), sem("v_stored"), sem("c_ready"), sem("c_stored")
    N_CONST = 6

    with nc.Block() as block:
        @block.sync
        def _(sp):
            for s in (y_stored, qkT_stored, v_stored, c_stored):
                sp.sem_inc(s, 16)

            def load_x(i):
                sp.wait_ge(xt_free, i + 1)
                sp.dma_start(xt[:], tile_of(d["x"], i)).then_inc(x_in, 16)

            def store(i):
                sp.wait_ge(v_ready, i + 1)
                sp.dma_start(tile_of(d["fox_v"], i), v_out[:]).then_inc(v_stored, 16)
                sp.wait_ge(c_ready, i + 1)
                sp.dma_start(tile_of(d["mlstm_vo"], i), c_out[:]).then_inc(c_stored, 16)
                sp.wait_ge(y_ready, i + 1)
                sp.wait_ge(qkT_out_ready, i + 1)
                sp.dma_start(tile_of(d["y1"], i)[:, 0:GW], y_out[:]).then_inc(y_stored, 16)
                sp.dma_start(cols_of(d["qkmT"], i), qkT_out[:]).then_inc(qkT_stored, 16)

            load_x(0)
            sp.dma_start(norm_gain[:], d["norm_g"].partition_broadcast(P)).then_inc(const_in, 16)
            sp.dma_start(sgu_gain[:], d["sgu_norm_g"].partition_broadcast(P)).then_inc(const_in, 16)
            sp.dma_start(qk_gain[:], d["qkm_g"].partition_broadcast(P)).then_inc(const_in, 16)
            sp.dma_start(sgu_w[:], d["sgu_wT"]).then_inc(const_in, 16)
            sp.dma_start(sgu_b[:], d["sgu_b"]).then_inc(const_in, 16)
            sp.dma_start(w[:], d["w_tok1"].rearrange("(k p) c -> p k c", p=P)).then_inc(const_in, 16)
            with sp.Fori(0, NT - 1) as i:
                load_x(i + 1)
                store(i)
            store(NT - 1)
            for s in (y_stored, qkT_stored, v_stored, c_stored):
                sp.wait_ge(s, 16 * (NT + 1))

        @block.gpsimd
        def _(pool):
            def rstd(out, var, total, eps):
                nc.gpsimd.tensor_tensor(var[:], total[:], eps.to_broadcast([P, out.shape[1]]), ALU.add)
                pool.drain()
                return nc.gpsimd.tensor_tensor(out[:], var[:], g.neg_half[:].to_broadcast([P, out.shape[1]]), ALU.pow)

            def x_norm(i):
                pool.wait_ge(x_sq_ready, i + 1)
                rstd(x_rstd, x_var, x_sq, g.eps[:]).then_inc(x_rstd_ready, 1)

            def tile(i):
                pool.wait_ge(h_ready, i + 1)
                nc.gpsimd.tensor_copy(hT[:, :, bass.ds(i * P, P)], h_slot[:]).then_inc(hT_copied, 1)

            def head_norms(i):
                pool.wait_ge(v_sq_ready, i + 1)
                rstd(v_rstd, v_var, v_sq, g.head_eps[:]).then_inc(v_rstd_ready, 1)
                pool.wait_ge(q_sq_ready, i + 1)
                rstd(q_rstd, q_var, q_sq, g.head_eps[:]).then_inc(q_rstd_ready, 1)

            pool.sem_inc(hT_copied, 1)
            pool.wait_ge(const_in, 16 * N_CONST)
            nc.gpsimd.affine_select(out=sgu_w[:], in_=sgu_w[:], compare_op=ALU.is_ge, fill=0.0, base=0,
                                    pattern=[[0, GH], [1, P]], channel_multiplier=-1).then_inc(w_masked, 1)
            x_norm(0)
            with pool.Fori(0, NT - 1) as i:
                tile(i)
                x_norm(i + 1)
                head_norms(i)
            tile(NT - 1)
            head_norms(NT - 1)

        @block.scalar
        def _(act):
            def square_x(i):
                act.wait_ge(x_in, 16 * (i + 1))
                nc.scalar.activation(junk[:], xt[:], ACT.Square, scale=DM ** -0.5, accum_out=x_sq[:]).then_inc(x_sq_ready, 1)

            def fill_slot(i):
                act.wait_ge(xT_ready, i + 1)
                act.wait_ge(h_free, i + 1)
                act.wait_ge(hT_copied, i + 1)
                nc.scalar.activation(h_slot[:], p_xT[:], ACT.Copy).then_inc(h_ready, 1)

            def evacuate(i):
                act.wait_ge(proj_ready[0], i + 1)
                act.wait_ge(uv_free, i + 1)
                nc.scalar.activation(uv[:], p_proj[0][:], ACT.Gelu_apprx_tanh).then_inc(uv_ready, 1)
                act.drain().then_inc(proj_free[0], 1)
                act.wait_ge(proj_ready[1], i + 1)
                act.wait_ge(qkm_free, i + 1)
                nc.scalar.activation(qkm[:, 0:512], p_proj[1][:], ACT.Copy).then_inc(qk_ready, 1)
                act.drain().then_inc(proj_free[1], 1)
                act.wait_ge(proj_ready[2], i + 1)
                act.wait_ge(v_stored, 16 * (i + 1))
                nc.scalar.activation(qkm[:, 512:768], p_proj[2][:, 0:GW], ACT.Copy).then_inc(mq_ready, 1)
                nc.scalar.activation(v_out[:], p_proj[2][:, GW:2 * GW], ACT.Copy).then_inc(v_ready, 1)
                act.drain().then_inc(proj_free[2], 1)
                act.wait_ge(proj_ready[3], i + 1)
                act.wait_ge(c_stored, 16 * (i + 1))
                nc.scalar.activation(c_out[:], p_proj[3][:], ACT.Copy).then_inc(c_ready, 1)
                act.drain().then_inc(proj_free[3], 1)

            for s in proj_free:
                act.sem_inc(s, 1)
            square_x(0)
            with act.Fori(0, NT - 1) as i:
                fill_slot(i)
                square_x(i + 1)
                evacuate(i)
            fill_slot(NT - 1)
            evacuate(NT - 1)

        @block.vector
        def _(dve):
            def scale_x(i):
                dve.wait_ge(x_in, 16 * (i + 1))
                dve.wait_ge(x_rstd_ready, i + 1)
                nc.vector.scalar_tensor_tensor(xs[:], xt[:], x_rstd[:], norm_gain[:], ALU.mult, ALU.mult)\
                    .then_inc(xs_ready, 1)
                dve.drain().then_inc(xt_free, 1)

            def norms(i):
                dve.wait_ge(uv_ready, i + 1)
                v = uv[:, GW:2 * GW]
                nc.vector.tensor_tensor(v2[:], v, v, ALU.mult)
                dve.drain()
                nc.vector.tensor_reduce(v_sq[:], heads(v2[:]), AX.X, ALU.add).then_inc(v_sq_ready, 1)
                dve.wait_ge(qk_ready, i + 1)
                dve.wait_ge(mq_ready, i + 1)
                nc.vector.tensor_tensor(qkm2[:], qkm[:], qkm[:], ALU.mult)
                dve.drain()
                nc.vector.tensor_reduce(q_sq[:], heads(qkm2[:]), AX.X, ALU.add).then_inc(q_sq_ready, 1)
                dve.wait_ge(v_rstd_ready, i + 1)
                nc.vector.tensor_tensor(heads(v2[:]), heads(v), along(v_rstd[:], HD), ALU.mult)
                dve.drain()
                nc.vector.tensor_tensor(vn[:], v2[:], sgu_gain[:], ALU.mult).then_inc(vn_ready, 1)
                dve.wait_ge(q_rstd_ready, i + 1)
                nc.vector.tensor_tensor(heads(qkm2[:]), heads(qkm[:]), along(q_rstd[:], HD), ALU.mult)
                dve.drain()
                nc.vector.tensor_tensor(qkm[:], qkm2[:], qk_gain[:], ALU.mult).then_inc(qkn_ready, 1)

            def outputs(i):
                dve.wait_ge(mix_ready, i + 1)
                nc.vector.tensor_tensor(heads(mixed[:]), heads(p_mix[:, 0:GW]), along(sgu_b[:], HD), ALU.add)\
                    .then_inc(mix_free, 1)
                dve.drain()
                dve.wait_ge(y_stored, 16 * (i + 1))
                nc.vector.tensor_tensor(y_out[:], uv[:, 0:GW], mixed[:], ALU.mult).then_inc(y_ready, 1)
                dve.drain().then_inc(uv_free, 1)
                dve.wait_ge(qkT_stored, 16 * (i + 1))
                dve.wait_ge(qkT_ready, 2 * i + 1)
                nc.vector.tensor_copy(qkT_out[:, 0:4, :], p_qkT[:]).then_inc(qkT_free, 1)
                dve.wait_ge(qkT_ready, 2 * i + 2)
                nc.vector.tensor_copy(qkT_out[:, 4:6, :], p_qkT[:, 0:2, :]).then_inc(qkT_free, 1)
                dve.drain().then_inc(qkT_out_ready, 1)

            for s in (xt_free, uv_free, mix_free, qkT_free):
                dve.sem_inc(s, 1)
            dve.wait_ge(const_in, 16 * N_CONST)
            nc.vector.tensor_scalar(sgu_gain[:], sgu_gain[:], float(HD) ** 0.5, None, ALU.mult)
            nc.vector.tensor_scalar(qk_gain[:, GW:2 * GW], qk_gain[:, GW:2 * GW], float(HD) ** 0.5, None, ALU.mult)
            dve.drain()
            scale_x(0)
            with dve.Fori(0, NT - 1) as i:
                dve.wait_ge(xT_ready, i + 1)
                scale_x(i + 1)
                norms(i)
                outputs(i)
            norms(NT - 1)
            outputs(NT - 1)

        @block.tensor
        def _(pe):
            def turn_x(i):
                pe.wait_ge(xs_ready, i + 1)
                for k in range(KB):
                    last = nc.tensor.transpose(p_xT[:, k, :], xs[:, k * P:(k + 1) * P], g.ident[:])
                last.then_inc(xT_ready, 1)

            def project(i):
                pe.wait_ge(h_ready, i + 1)
                for n in range(4):
                    pe.wait_ge(proj_free[n], i + 1)
                    for k in range(KB):
                        last = nc.tensor.matmul(p_proj[n][:], h_slot[:, k, :], w[:, k, n * BANK:(n + 1) * BANK],
                                                start=(k == 0), stop=(k == KB - 1))
                    last.then_inc(proj_ready[n], 1)
                pe.drain().then_inc(h_free, 1)

            def branch(i):
                pe.wait_ge(vn_ready, i + 1)
                pe.wait_ge(mix_free, i + 1)
                for h in range(GH):
                    last = nc.tensor.matmul(p_mix[:, h * HD:(h + 1) * HD], sgu_w[:, h, :], vn[:, h * HD:(h + 1) * HD],
                                            start=True, stop=True)
                last.then_inc(mix_ready, 1)
                pe.wait_ge(qkn_ready, i + 1)
                for first, n in ((0, 4), (4, 2)):
                    pe.wait_ge(qkT_free, 2 * i + 1 + (first > 0))
                    for j in range(n):
                        c = (first + j) * P
                        last = nc.tensor.transpose(p_qkT[:, j, :], qkm[:, c:c + P], g.ident[:])
                    last.then_inc(qkT_ready, 1)
                pe.drain().then_inc(qkm_free, 1)

            pe.sem_inc(h_free, 1)
            pe.sem_inc(qkm_free, 1)
            pe.wait_ge(const_in, 16 * N_CONST)
            pe.wait_ge(w_masked, 1)
            turn_x(0)
            project(0)
            with pe.Fori(1, NT) as i:
                pe.wait_ge(h_ready, i)
                turn_x(i)
                branch(i - 1)
                project(i)
            branch(NT - 1)
    ph.close()


GATE_PAIRS, CONV_PAIRS, SHIFT_PAIRS = 4, 2, 3
FIRST_SHIFT = GATE_PAIRS + CONV_PAIRS
LAST_PAIR = FIRST_SHIFT + SHIFT_PAIRS
CONV_K = 4
PAD = CONV_K - 1


def feature_pass_1(nc, d, g, hT):
    ph = Phase(nc, "f1")
    sb, ps, sem = ph.sb, ph.ps, ph.sem
    w = [sb(f"w{b}", [P, KB, P]) for b in range(2)]
    padded = [sb(f"padded{b}", [P, PAD + T]) for b in range(2)]
    work = sb("work", [P, T])
    out = [sb(f"out{b}", [P, T]) for b in range(2)]
    conv_w, conv_b = sb("conv_w", [P, 2 * CONV_PAIRS, CONV_K]), sb("conv_b", [P, 2 * CONV_PAIRS])
    mu = sb("mu", [P, 2 * SHIFT_PAIRS + 2])
    p_out = [ps(f"out{b}", [P, T]) for b in range(2)]
    const_in = sem("const_in")
    w_in = [sem(f"w{b}_in") for b in range(2)]
    p_ready = [sem(f"p{b}_ready") for b in range(2)]
    p_free = [sem(f"p{b}_free") for b in range(2)]
    padded_ready = [sem(f"padded{b}_ready") for b in range(2)]
    padded_free = [sem(f"padded{b}_free") for b in range(2)]
    work_ready = sem("work_ready")
    out_ready = [sem(f"out{b}_ready") for b in range(2)]
    stored = [sem(f"stored{b}") for b in range(2)]
    pads_ready = sem("pads_ready")

    def rows_of(dram, block):
        return dram[bass.ds(block * P, P), :]

    with nc.Block() as block:
        @block.sync
        def _(sp):
            def load(j, b):
                sp.dma_start(w[b][:].rearrange("p k c -> p (k c)"),
                             d["w_fm1"][bass.ds(2 * j + b, 1)].rearrange("a p c -> (a p) c")).then_inc(w_in[b], 16)

            def store(j, b, dst):
                sp.wait_ge(out_ready[b], j + 1)
                sp.dma_start(dst, out[b][:]).then_inc(stored[b], 16)

            def turn(j, dst, load_next=2):
                for b in range(2):
                    if b < load_next:
                        sp.wait_ge(p_ready[b], j + 1)
                        load(j + 1, b)
                    store(j, b, rows_of(*dst(j, b)))

            for b in range(2):
                sp.sem_inc(stored[b], 16)
            load(0, 0)
            load(0, 1)
            sp.dma_start(conv_w[:], d["conv_w"]).then_inc(const_in, 16)
            sp.dma_start(conv_b[:], d["conv_b"]).then_inc(const_in, 16)
            sp.dma_start(mu[:], d["rwkv_mu"]).then_inc(const_in, 16)
            with sp.Fori(0, GATE_PAIRS) as j:
                turn(j, lambda j, b: (d["z1T"], 2 * j + b))
            with sp.Fori(GATE_PAIRS, FIRST_SHIFT) as j:
                turn(j, lambda j, b: (d["mlstm_qkT"], 2 * (j - GATE_PAIRS) + b))
            with sp.Fori(FIRST_SHIFT, LAST_PAIR) as j:
                turn(j, lambda j, b: (d["rwkv_T"], 2 * (j - FIRST_SHIFT) + b))
            turn(LAST_PAIR, lambda j, b: (d["z1T"], 2 * GATE_PAIRS + b), load_next=1)
            store(LAST_PAIR + 1, 0, d["lowT"])
            for b in range(2):
                sp.wait_ge(stored[b], 16 * (LAST_PAIR + 2 + (b == 0)))

        @block.tensor
        def _(pe):
            def project(j, b):
                pe.wait_ge(w_in[b], 16 * (j + 1))
                pe.wait_ge(p_free[b], j + 1)
                for n in range(T // BANK):
                    for k in range(KB):
                        last = nc.tensor.matmul(p_out[b][:, n * BANK:(n + 1) * BANK], w[b][:, k, :],
                                                hT[:, k, n * BANK:(n + 1) * BANK], start=(k == 0), stop=(k == KB - 1))
                last.then_inc(p_ready[b], 1)

            with pe.Fori(0, LAST_PAIR + 1) as j:
                project(j, 0)
                project(j, 1)
            project(LAST_PAIR + 1, 0)

        @block.gpsimd
        def _(pool):
            for b in range(2):
                last = nc.gpsimd.memset(padded[b][:, 0:PAD], 0.0)
            last.then_inc(pads_ready, 1)

        @block.scalar
        def _(act):
            def straight(j, b, func):
                act.wait_ge(p_ready[b], j + 1)
                act.wait_ge(stored[b], 16 * (j + 1))
                nc.scalar.activation(out[b][:], p_out[b][:], func).then_inc(out_ready[b], 1)
                act.drain().then_inc(p_free[b], 1)

            def to_padded(j, b):
                act.wait_ge(p_ready[b], j + 1)
                act.wait_ge(padded_free[b], j - GATE_PAIRS + 1)
                nc.scalar.activation(padded[b][:, PAD:], p_out[b][:], ACT.Copy).then_inc(padded_ready[b], 1)
                act.drain().then_inc(p_free[b], 1)

            def silu_of_work(j, b, n):
                act.wait_ge(work_ready, n)
                act.wait_ge(stored[b], 16 * (j + 1))
                nc.scalar.activation(out[b][:], work[:], ACT.Silu).then_inc(out_ready[b], 1)

            for b in range(2):
                act.sem_inc(p_free[b], 1)
            with act.Fori(0, GATE_PAIRS) as j:
                for b in range(2):
                    straight(j, b, ACT.Silu)
            with act.Fori(GATE_PAIRS, FIRST_SHIFT) as j:
                for b in range(2):
                    to_padded(j, b)
                    silu_of_work(j, b, 2 * (j - GATE_PAIRS) + b + 1)
            with act.Fori(FIRST_SHIFT, LAST_PAIR) as j:
                for b in range(2):
                    to_padded(j, b)
            for b in range(2):
                to_padded(LAST_PAIR, b)
                silu_of_work(LAST_PAIR, b, 2 * CONV_PAIRS + b + 1)
            straight(LAST_PAIR + 1, 0, ACT.Copy)

        @block.vector
        def _(dve):
            def convolve(j, b, c):
                dve.wait_ge(padded_ready[b], j - GATE_PAIRS + 1)
                dve.wait_ge(out_ready[1 - b], j + b)
                nc.vector.tensor_scalar(work[:], padded[b][:, PAD:], conv_w[:, bass.ds(c, 1), PAD],
                                        conv_b[:, bass.ds(c, 1)], ALU.mult, ALU.add)
                for tap in range(PAD):
                    dve.drain()
                    last = nc.vector.scalar_tensor_tensor(work[:], padded[b][:, tap:tap + T],
                                                          conv_w[:, bass.ds(c, 1), tap], work[:], ALU.mult, ALU.add)
                last.then_inc(work_ready, 1)
                dve.drain().then_inc(padded_free[b], 1)

            def shift(j, b, c, dst, signal):
                dve.wait_ge(padded_ready[b], j - GATE_PAIRS + 1)
                x, previous = padded[b][:, PAD:], padded[b][:, PAD - 1:PAD - 1 + T]
                nc.vector.tensor_tensor(work[:], previous, x, ALU.subtract)
                dve.drain()
                nc.vector.scalar_tensor_tensor(dst[:], work[:], mu[:, bass.ds(c, 1)], x, ALU.mult, ALU.add)\
                    .then_inc(signal, 1)
                dve.drain().then_inc(padded_free[b], 1)

            for b in range(2):
                dve.sem_inc(padded_free[b], 1)
            dve.wait_ge(const_in, 16 * 3)
            dve.wait_ge(pads_ready, 1)
            with dve.Fori(GATE_PAIRS, FIRST_SHIFT) as j:
                for b in range(2):
                    convolve(j, b, 2 * (j - GATE_PAIRS) + b)
            dve.wait_ge(out_ready[1], FIRST_SHIFT)
            with dve.Fori(FIRST_SHIFT, LAST_PAIR) as j:
                for b in range(2):
                    dve.wait_ge(stored[b], 16 * (j + 1))
                    shift(j, b, 2 * (j - FIRST_SHIFT) + b, out[b], out_ready[b])
            for b in range(2):
                if b:
                    dve.wait_ge(out_ready[0], LAST_PAIR + 1)
                shift(LAST_PAIR, b, 2 * SHIFT_PAIRS + b, work, work_ready)
    ph.close()


def gates_phase(nc, d, g):
    ph = Phase(nc, "gates")
    sb, sem = ph.sb, ph.sem
    R = 2 * GH
    logit, i_gate, e, f_sum, a = (sb(n, [R, T]) for n in ("logit", "i_gate", "e", "f_sum", "a"))
    run_max, w_inter, w_new, e_neg_m, ones = (sb(n, [R, T]) for n in ("run_max", "w_inter", "w_new", "e_neg_m", "ones"))
    bias, i_bias = sb("bias", [R, 1]), sb("i_bias", [R, 1])
    prev, carry = sb("prev", [R, NT]), sb("carry", [R, NT])
    loaded, zeroed, abs_ready, exp_ready, ln_ready, args_ready, done, stored = (
        sem(n) for n in ("loaded", "zeroed", "abs_ready", "exp_ready", "ln_ready", "args_ready", "done", "stored"))

    def chunks(ap):
        return ap.rearrange("p (c t) -> p c t", t=P)

    with nc.Block() as block:
        @block.sync
        def _(sp):
            sp.wait_ge(zeroed, 1)
            sp.dma_start(logit[0:GH, :], d["lowT"][64:68, :]).then_inc(loaded, 16)
            sp.dma_start(logit[GH:R, :], d["lowT"][72:76, :]).then_inc(loaded, 16)
            sp.dma_start(i_gate[GH:R, :], d["lowT"][68:72, :]).then_inc(loaded, 16)
            sp.dma_start(bias[:], d["f_bias"]).then_inc(loaded, 16)
            sp.dma_start(i_bias[GH:R, :], d["i_bias"]).then_inc(loaded, 16)
            sp.wait_ge(done, 1)
            sp.dma_start(d["fox_rows"][0:GH, 0, :], f_sum[0:GH, :]).then_inc(stored, 16)
            sp.dma_start(d["fox_rows"][0:GH, 1, :], ones[0:GH, :]).then_inc(stored, 16)
            sp.dma_start(d["fox_rows"][GH:R, 0, :], ones[0:GH, :]).then_inc(stored, 16)
            sp.dma_start(d["fox_rows"][GH:R, 1, :], a[0:GH, :]).then_inc(stored, 16)
            for n, rows in enumerate((a, w_inter, w_new, e_neg_m)):
                sp.dma_start(d["mlstm_rows"][n * GH:(n + 1) * GH, :], rows[GH:R, :]).then_inc(stored, 16)
            sp.dma_start(d["mlstm_max"], run_max[GH:R, :]).then_inc(stored, 16)
            sp.dma_start(d["mlstm_carry"], carry[GH:R, :]).then_inc(stored, 16)
            sp.wait_ge(stored, 16 * 10)

        @block.scalar
        def _(act):
            act.wait_ge(abs_ready, 1)
            nc.scalar.activation(e[:], e[:], ACT.Exp).then_inc(exp_ready, 1)
            act.drain()
            nc.scalar.activation(e[:], e[:], ACT.Ln, bias=1.0).then_inc(ln_ready, 1)
            act.wait_ge(args_ready, 1)
            nc.scalar.activation(w_inter[:], w_inter[:], ACT.Exp)
            nc.scalar.activation(w_new[:], w_new[:], ACT.Exp)
            nc.scalar.activation(e_neg_m[:], e_neg_m[:], ACT.Exp, scale=-1.0)
            nc.scalar.activation(carry[:], carry[:], ACT.Exp)
            act.drain().then_inc(done, 1)

        @block.vector
        def _(dve):
            nc.vector.memset(i_gate[:], 0.0)
            nc.vector.memset(ones[:], 1.0)
            nc.vector.memset(i_bias[:], 0.0)
            dve.drain().then_inc(zeroed, 1)
            dve.wait_ge(loaded, 16 * 5)
            nc.vector.tensor_scalar(logit[:], logit[:], bias[:], None, ALU.add)
            dve.drain()
            nc.vector.scalar_tensor_tensor(e[:], logit[:], -1.0, logit[:], ALU.mult, ALU.min).then_inc(abs_ready, 1)
            dve.drain()
            nc.vector.tensor_scalar(logit[:], logit[:], 0.0, None, ALU.min)
            dve.drain()
            dve.wait_ge(ln_ready, 1)
            nc.vector.tensor_tensor(logit[:], logit[:], e[:], ALU.subtract)
            dve.drain()
            nc.vector.tensor_tensor_scan(f_sum[:], ones[:], logit[:], 0.0, ALU.mult, ALU.add)
            dve.drain()
            nc.vector.scalar_tensor_tensor(a[:], i_gate[:], i_bias[:], f_sum[:], ALU.add, ALU.subtract)
            dve.drain()
            nc.vector.tensor_tensor_scan(run_max[:], a[:], a[:], 0.0, ALU.max, ALU.max)
            dve.drain()
            nc.vector.memset(prev[:, 0:1], 0.0)
            nc.vector.tensor_copy(prev[:, 1:NT], chunks(run_max[:])[:, 0:NT - 1, P - 1])
            dve.drain()
            ends = chunks(run_max[:])[:, :, P - 1]
            nc.vector.tensor_tensor(carry[:], prev[:], ends, ALU.subtract)
            nc.vector.tensor_tensor(chunks(w_inter[:]), along(prev[:], P), chunks(run_max[:]), ALU.subtract)
            nc.vector.tensor_tensor(chunks(w_new[:]), chunks(a[:]), along(ends, P), ALU.subtract)
            nc.vector.tensor_tensor(e_neg_m[:], f_sum[:], run_max[:], ALU.add)
            dve.drain().then_inc(args_ready, 1)
    ph.close()


def keys_values(nc, d, g, name, src, w_src, nh, gain_src, scale, shift, kT_dst, v_dst):
    ph = Phase(nc, name)
    sb, ps, sem = ph.sb, ph.ps, ph.sem
    W = nh * HD
    w = sb("w", [P, KB, 2 * W])
    xt, junk, xs, x_slot = sb("xt", [P, DM]), sb("junk", [P, DM]), sb("xs", [P, DM]), sb("x_slot", [P, KB, P])
    x_sq, x_rstd = sb("x_sq", [P, 1]), sb("x_rstd", [P, 1])
    kn, k2, v_out, kT_out = sb("kn", [P, W]), sb("k2", [P, W]), sb("v_out", [P, W]), sb("kT_out", [P, W // P, P])
    k_sq, k_rstd, gain = sb("k_sq", [P, nh]), sb("k_rstd", [P, nh]), sb("gain", [P, W])
    p_xT, p_k, p_v, p_kT = ps("xT", [P, KB, P]), ps("k", [P, BANK]), ps("v", [P, BANK]), ps("kT", [P, W // P, P])
    names = ("const_in", "x_in", "x_sq_ready", "x_rstd_ready", "xs_ready", "xT_ready", "slot_ready", "k_ready", "v_ready",
             "v_out_ready", "k_sq_ready", "k_rstd_ready", "kn_ready", "kT_ready", "kT_out_ready", "v_stored", "kT_stored")
    (const_in, x_in, x_sq_ready, x_rstd_ready, xs_ready, xT_ready, slot_ready, k_ready, v_ready, v_out_ready, k_sq_ready,
     k_rstd_ready, kn_ready, kT_ready, kT_out_ready, v_stored, kT_stored) = (sem(n) for n in names)
    with nc.Block() as block:
        @block.sync
        def _(sp):
            sp.dma_start(gain[:], gain_src.partition_broadcast(P)).then_inc(const_in, 16)
            sp.dma_start(w[:], w_src.rearrange("(k p) c -> p k c", p=P)).then_inc(const_in, 16)
            for s in (v_stored, kT_stored):
                sp.sem_inc(s, 16)
            with sp.Fori(0, NMEM // P) as i:
                sp.dma_start(xt[:], tile_of(src, i)).then_inc(x_in, 16)
                sp.wait_ge(v_out_ready, i + 1)
                sp.wait_ge(kT_out_ready, i + 1)
                sp.dma_start(tile_of(v_dst, i), v_out[:]).then_inc(v_stored, 16)
                sp.dma_start(cols_of(kT_dst, i), kT_out[:]).then_inc(kT_stored, 16)
            for s in (v_stored, kT_stored):
                sp.wait_ge(s, 16 * (NMEM // P + 1))

        @block.scalar
        def _(act):
            with act.Fori(0, NMEM // P) as i:
                act.wait_ge(x_in, 16 * (i + 1))
                nc.scalar.activation(junk[:], xt[:], ACT.Square, scale=DM ** -0.5, accum_out=x_sq[:]).then_inc(x_sq_ready, 1)
                act.wait_ge(xT_ready, i + 1)
                for k in range(KB):
                    last = nc.scalar.activation(x_slot[:, k, :], p_xT[:, k, :], ACT.Identity, scale=scale[:, k:k + 1],
                                                bias=shift[:, k:k + 1] if shift is not None else 0.0)
                act.drain().then_inc(slot_ready, 1)
                act.wait_ge(v_ready, i + 1)
                act.wait_ge(v_stored, 16 * (i + 1))
                nc.scalar.activation(v_out[:], p_v[:, 0:W], ACT.Copy).then_inc(v_out_ready, 1)

        @block.gpsimd
        def _(pool):
            with pool.Fori(0, NMEM // P) as i:
                pool.wait_ge(x_sq_ready, i + 1)
                nc.gpsimd.tensor_tensor(x_sq[:], x_sq[:], g.eps[:], ALU.add)
                pool.drain()
                nc.gpsimd.tensor_tensor(x_rstd[:], x_sq[:], g.neg_half[:], ALU.pow).then_inc(x_rstd_ready, 1)
                pool.wait_ge(k_sq_ready, i + 1)
                nc.gpsimd.tensor_tensor(k_sq[:], k_sq[:], g.head_eps[:].to_broadcast([P, nh]), ALU.add)
                pool.drain()
                nc.gpsimd.tensor_tensor(k_rstd[:], k_sq[:], g.neg_half[:].to_broadcast([P, nh]), ALU.pow)\
                    .then_inc(k_rstd_ready, 1)

        @block.vector
        def _(dve):
            dve.wait_ge(const_in, 32)
            nc.vector.tensor_scalar(gain[:], gain[:], HD ** 0.5, None, ALU.mult)
            dve.drain()
            with dve.Fori(0, NMEM // P) as i:
                dve.wait_ge(x_rstd_ready, i + 1)
                nc.vector.tensor_scalar(xs[:], xt[:], x_rstd[:], None, ALU.mult).then_inc(xs_ready, 1)
                dve.wait_ge(k_ready, i + 1)
                nc.vector.tensor_copy(kn[:], p_k[:, 0:W])
                dve.drain()
                nc.vector.tensor_tensor(k2[:], kn[:], kn[:], ALU.mult)
                dve.drain()
                nc.vector.tensor_reduce(k_sq[:], heads(k2[:]), AX.X, ALU.add).then_inc(k_sq_ready, 1)
                dve.wait_ge(k_rstd_ready, i + 1)
                nc.vector.tensor_tensor(heads(k2[:]), heads(kn[:]), along(k_rstd[:], HD), ALU.mult)
                dve.drain()
                nc.vector.tensor_tensor(kn[:], k2[:], gain[:], ALU.mult).then_inc(kn_ready, 1)
                dve.wait_ge(kT_ready, i + 1)
                dve.wait_ge(kT_stored, 16 * (i + 1))
                nc.vector.tensor_copy(kT_out[:], p_kT[:]).then_inc(kT_out_ready, 1)

        @block.tensor
        def _(pe):
            pe.wait_ge(const_in, 32)
            with pe.Fori(0, NMEM // P) as i:
                pe.wait_ge(xs_ready, i + 1)
                for k in range(KB):
                    last = nc.tensor.transpose(p_xT[:, k, :], xs[:, k * P:(k + 1) * P], g.ident[:])
                last.then_inc(xT_ready, 1)
                pe.wait_ge(slot_ready, i + 1)
                for out, first, ready in ((p_k, 0, k_ready), (p_v, W, v_ready)):
                    for k in range(KB):
                        last = nc.tensor.matmul(out[:, 0:W], x_slot[:, k, :], w[:, k, first:first + W],
                                                start=(k == 0), stop=(k == KB - 1))
                    last.then_inc(ready, 1)
                pe.wait_ge(kn_ready, i + 1)
                for j in range(W // P):
                    last = nc.tensor.transpose(p_kT[:, j, :], kn[:, j * P:(j + 1) * P], g.ident[:])
                last.then_inc(kT_ready, 1)
    ph.close()


HALF = NT // 2
GROUP = BANK // P


def attention(nc, d, g, ph, nh, rows, kT, v, load, load_q, n_loads, key_cols, n_consts, y_dst, s_bufs, s_cols,
              bias=None, bias_consts=None):
    sb, ps, sem = ph.sb, ph.ps, ph.sem
    q = [sb(f"q{s}", [rows, HALF * P]) for s in range(2)]
    prob = [sb(f"prob{b}", [P, s_cols]) for b in range(2)]
    probT = [sb(f"probT{b}", [P, GROUP, P]) for b in range(2)]
    top, neg_top = [sb(f"top{b}", [P, 1]) for b in range(2)], [sb(f"neg_top{b}", [P, 1]) for b in range(2)]
    total, inv = [sb(f"total{b}", [P, 1]) for b in range(2)], sb("inv", [P, 1])
    y = [sb(f"y{s}", [P, HALF, HD]) for s in range(2)]
    p_s = [ps(f"s{b}", [P, s_cols]) for b in range(s_bufs)]
    p_t = [ps(f"t{b}", [P, GROUP, P]) for b in range(2)]
    p_o = [ps(f"o{b}", [P, BANK]) for b in range(2)]
    const_in = sem("const_in")
    q_in, q_free = [sem(f"q{s}_in") for s in range(2)], [sem(f"q{s}_free") for s in range(2)]
    s_ready, s_free, top_ready, prob_ready, prob_free = (sem(n) for n in ("s_ready", "s_free", "top_ready", "prob_ready",
                                                                          "prob_free"))
    t_ready, probT_ready = [sem(f"t{b}_ready") for b in range(2)], [sem(f"probT{b}_ready") for b in range(2)]
    o_ready, o_free, taken = sem("o_ready"), sem("o_free"), sem("taken")
    y_ready, y_stored = [sem(f"y{s}_ready") for s in range(2)], [sem(f"y{s}_stored") for s in range(2)]

    blocks = [key_cols(u) for u in range(NT)]
    groups, n = [], 0
    for u in range(NT):
        cut = [blocks[u][i:i + GROUP] for i in range(0, len(blocks[u]), GROUP)]
        groups.append([(n + i, c) for i, c in enumerate(cut)])
        n += len(cut)
    per_head = n
    assert per_head % 2 == 0

    def count(h, n):
        return h * (per_head // 2) + n // 2 + 1

    def runs(u):
        out = []
        for i, (c, _) in enumerate(blocks[u]):
            if out and (i * P) % BANK and out[-1][1] + out[-1][2] == c:
                out[-1][2] += P
            else:
                out.append([i * P, c, P])
        return out

    with nc.Block() as block:
        @block.sync
        def _(sp):
            for s in range(2):
                sp.sem_inc(y_stored[s], 16)
            load(sp, const_in)
            with sp.Fori(0, nh) as h:
                for s in range(2):
                    sp.wait_ge(q_free[s], h + 1)
                    load_q(sp, h, s, q[s], q_in[s])
                for s in range(2):
                    sp.wait_ge(y_ready[s], HALF * (h + 1))
                    sp.dma_start(y_dst(h, s), y[s][:]).then_inc(y_stored[s], 16)
            for s in range(2):
                sp.wait_ge(y_stored[s], 16 * (nh + 1))

        if bias_consts is not None:
            @block.gpsimd
            def _(pool):
                bias_consts(pool, const_in)

        @block.tensor
        def _(pe):
            def scores(h, u):
                if u % HALF == 0:
                    pe.wait_ge(q_in[u // HALF], 16 * n_loads * (h + 1))
                wait_apart(pe, s_free, NT * h + u + 1, taken)
                lhs = q[u // HALF][:, (u % HALF) * P:(u % HALF + 1) * P]
                for at, c, n in runs(u):
                    last = nc.tensor.matmul(p_s[u % s_bufs][:, at:at + n], lhs,
                                            kT[:, bass.ds(h, 1), c:c + n].rearrange("p a c -> p (a c)"),
                                            start=True, stop=True)
                last.then_inc(s_ready, 1)
                if u % HALF == HALF - 1:
                    pe.drain().then_inc(q_free[u // HALF], 1)

            def turn(h, u, n, part, first):
                for j in range(len(part)):
                    at = (first + j) * P
                    last = nc.tensor.transpose(p_t[n % 2][:, j, :], prob[u % 2][:, at:at + P], g.ident[:])
                last.then_inc(t_ready[n % 2], 1)

            def values(h, u):
                pe.wait_ge(prob_ready, NT * h + u + 1)
                pe.wait_ge(o_free, NT * h + u + 1)
                todo = groups[u]
                turn(h, u, *todo[0], 0)
                for i, (n, part) in enumerate(todo):
                    if i + 1 < len(todo):
                        turn(h, u, *todo[i + 1], (i + 1) * GROUP)
                    pe.wait_ge(probT_ready[n % 2], count(h, n))
                    for j, (_, vb) in enumerate(part):
                        last = nc.tensor.matmul(p_o[u % 2][:, 0:HD], probT[n % 2][:, j, :],
                                                v[:, vb, bass.ds(h * HD, HD)],
                                                start=(i == 0 and j == 0), stop=(i * GROUP + j == len(blocks[u]) - 1))
                last.then_inc(o_ready, 1)
                pe.drain().then_inc(prob_free, 1)

            for s in range(2):
                pe.sem_inc(q_free[s], 1)
            pe.sem_inc(prob_free, 2)
            pe.wait_ge(const_in, n_consts)
            with pe.Fori(0, nh) as h:
                scores(h, 0)
                for u in range(NT):
                    if u + 1 < NT:
                        scores(h, u + 1)
                    values(h, u)

        def copy_groups(eng, copy, h, u, parity):
            for n, part in groups[u]:
                if n % 2 == parity:
                    eng.wait_ge(t_ready[parity], count(h, n))
                    copy(probT[parity][:, 0:len(part), :], p_t[parity][:, 0:len(part), :]).then_inc(probT_ready[parity], 1)

        @block.scalar
        def _(act):
            def exps(h, u):
                act.wait_ge(top_ready, NT * h + u + 1)
                act.wait_ge(prob_free, NT * h + u + 1)
                n = len(blocks[u]) * P
                nc.scalar.activation(prob[u % 2][:, 0:n], p_s[u % s_bufs][:, 0:n], ACT.Exp, bias=neg_top[u % 2][:],
                                     accum_out=total[u % 2][:]).then_inc(prob_ready, 1)
                act.drain().then_inc(s_free, 1)

            act.sem_inc(s_free, s_bufs)
            with act.Fori(0, nh) as h:
                exps(h, 0)
                for u in range(NT):
                    if u + 1 < NT:
                        exps(h, u + 1)
                    copy_groups(act, lambda o, i: nc.scalar.activation(o, i, ACT.Copy), h, u, 1)

        @block.vector
        def _(dve):
            def maxima(h, u):
                dve.wait_ge(s_ready, NT * h + u + 1)
                s = p_s[u % s_bufs]
                if bias is not None:
                    bias(dve, h, u, s)
                    dve.drain()
                nc.vector.tensor_reduce(top[u % 2][:], s[:, 0:len(blocks[u]) * P], AX.X, ALU.max)
                dve.drain()
                nc.vector.tensor_scalar(neg_top[u % 2][:], top[u % 2][:], -1.0, None, ALU.mult).then_inc(top_ready, 1)

            def normalise(h, u):
                dve.wait_ge(prob_ready, NT * h + u + 1)
                nc.vector.reciprocal(inv[:], total[u % 2][:])
                dve.drain()
                dve.wait_ge(o_ready, NT * h + u + 1)
                s = u // HALF
                if u % HALF == 0:
                    dve.wait_ge(y_stored[s], 16 * (h + 1))
                nc.vector.tensor_scalar(y[s][:, u % HALF, :], p_o[u % 2][:, 0:HD], inv[:], None, ALU.mult)\
                    .then_inc(y_ready[s], 1)
                dve.drain().then_inc(o_free, 1)

            dve.sem_inc(o_free, 2)
            dve.wait_ge(const_in, n_consts)
            with dve.Fori(0, nh) as h:
                maxima(h, 0)
                for u in range(NT):
                    if u + 1 < NT:
                        maxima(h, u + 1)
                    copy_groups(dve, nc.vector.tensor_copy, h, u, 0)
                    normalise(h, u)
    ph.close()


def head_tiles(dram, first):
    def at(h, s):
        return dram.rearrange("(s u p) c -> p s u c", s=2, p=P)[:, s, :, bass.ds(h * HD + first, HD)]
    return at


def fox_attention(nc, d, g):
    ph = Phase(nc, "fox")
    rows = HD + 2
    kT, v, tri = ph.sb("kT", [rows, GH, T]), ph.sb("v", [P, NT, GW]), ph.sb("tri", [P, P])

    def load(sp, const_in):
        sp.dma_start(kT[0:HD], d["qkmT"][GW:2 * GW].rearrange("(h e) t -> e h t", e=HD)).then_inc(const_in, 16)
        sp.dma_start(kT[HD:rows], d["fox_rows"][GH:2 * GH].rearrange("h e t -> e h t")).then_inc(const_in, 16)
        sp.dma_start(v[:], d["fox_v"].rearrange("(n p) c -> p n c", p=P)).then_inc(const_in, 16)

    def load_q(sp, h, s, q, q_in):
        cols = slice(s * HALF * P, (s + 1) * HALF * P)
        sp.dma_start(q[0:HD], d["qkmT"][bass.ds(h * HD, HD), cols]).then_inc(q_in, 16)
        sp.dma_start(q[HD:rows], d["fox_rows"][bass.ds(h, 1), :, cols].rearrange("h e t -> (h e) t")).then_inc(q_in, 16)

    def bias_consts(pool, const_in):
        nc.gpsimd.memset(tri[:], 0.0)
        pool.drain()
        nc.gpsimd.affine_select(out=tri[:], in_=tri[:], compare_op=ALU.is_ge, fill=MASKED, base=0, pattern=[[-1, P]],
                                channel_multiplier=1).then_inc(const_in, 1)

    def bias(dve, h, u, s):
        nc.vector.tensor_tensor(s[:, u * P:(u + 1) * P], s[:, u * P:(u + 1) * P], tri[:], ALU.add)

    attention(nc, d, g, ph, GH, rows, kT, v, load, load_q, 2, lambda u: [(b * P, b) for b in range(u + 1)], 16 * 3 + 1,
              head_tiles(d["y1"], GW), 1, T, bias, bias_consts)


def mem_attention(nc, d, g):
    ph = Phase(nc, "mem")
    kT, v = ph.sb("kT", [HD, GH, NMEM]), ph.sb("v", [P, NMEM // P, GW])

    def load(sp, const_in):
        sp.dma_start(kT[:], d["mem_kT"].rearrange("(h e) t -> e h t", e=HD)).then_inc(const_in, 16)
        sp.dma_start(v[:], d["mem_v"].rearrange("(n p) c -> p n c", p=P)).then_inc(const_in, 16)

    def load_q(sp, h, s, q, q_in):
        sp.dma_start(q[:], d["qkmT"][bass.ds(2 * GW + h * HD, HD), s * HALF * P:(s + 1) * HALF * P]).then_inc(q_in, 16)

    attention(nc, d, g, ph, GH, HD, kT, v, load, load_q, 1, lambda u: [(b * P, b) for b in range(NMEM // P)], 16 * 2,
              head_tiles(d["y1"], 3 * GW), 2, NMEM)


def mlstm(nc, d, g):
    ph = Phase(nc, "mlstm")
    sb, ps, sem = ph.sb, ph.ps, ph.sem
    VW = HD + 1
    NB = GW // P
    qk = [sb(f"qk{b}", [P, 2 * NB, P]) for b in range(2)]
    va = [sb(f"va{b}", [P, GH, VW]) for b in range(2)]
    o_in = [sb(f"o{b}", [P, GW]) for b in range(2)]
    rows = [sb(f"rows{b}", [4 * GH, P]) for b in range(2)]
    k_pad = sb("k_pad", [P, GH, P])
    sel = sb("sel", [GH, GH, P])
    past = sb("past", [P, P])
    run_max, carry_row = sb("run_max", [GH, T]), sb("carry_row", [GH, NT])
    carry = sb("carry", [P, GH, NT])
    cols = sb("cols", [P, 4 * GH])
    kw = sb("kw", [P, GW])
    arg, e, sm = sb("arg", [P, GH, P]), sb("e", [P, GH, P]), sb("sm", [P, GH, P])
    state = sb("state", [P, NB, 2 * VW])
    nd, nd2 = sb("nd", [P, GH, VW]), sb("nd2", [P, GH, VW])
    den, den2, inv = sb("den", [P, GH]), sb("den2", [P, GH]), sb("inv", [P, GH])
    gate, gate2, h1, h2, y_out = sb("gate", [P, GW]), sb("gate2", [P, GW]), sb("h1", [P, GW]), sb("h2", [P, GW]), sb("y", [P, GW])
    o_gate, h_tmp = sb("o_gate", [P, GW]), sb("h_tmp", [P, GW])
    h_sq, h_var, h_rstd, gain = sb("h_sq", [P, GH]), sb("h_var", [P, GH]), sb("h_rstd", [P, GH]), sb("gain", [P, GW])
    p_t, p_st, p_max = ps("t", [P, BANK]), ps("st", [P, GH, P]), ps("max", [P, GH, P])
    p_num, p_inter, p_state = ps("num", [P, BANK]), ps("inter", [P, BANK]), ps("state", [P, BANK])
    const_in, zeroed, sel_ready, carry_ready = (sem(n) for n in ("const_in", "zeroed", "sel_ready", "carry_ready"))
    slot_in = [sem(f"slot{b}_in") for b in range(2)]
    names = ("pe_done", "o_used", "pad_ready", "t_ready", "cols_ready", "st_ready", "max_ready", "arg_ready", "e_ready",
             "mask_ready", "sm_ready", "kw_ready", "num_ready", "inter_ready", "state_out", "state_ready", "nd_done",
             "gate_in", "gate_ready", "gate_free", "h_sq_ready", "h_rstd_ready", "h_in", "y_ready", "y_stored")
    (pe_done, o_used, pad_ready, t_ready, cols_ready, st_ready, max_ready, arg_ready, e_ready, mask_ready, sm_ready,
     kw_ready, num_ready, inter_ready, state_out, state_ready, nd_done, gate_in, gate_ready, gate_free, h_sq_ready, h_rstd_ready,
     h_in, y_ready, y_stored) = (sem(n) for n in names)
    LOADS = 4

    def pairs(eng, chunk):
        with eng.Fori(0, NT // 2) as j:
            for b in range(2):
                chunk(2 * j + b, b, j)

    with nc.Block() as block:
        @block.sync
        def _(sp):
            def load(c, b):
                sp.dma_start(qk[b][:], cols_of(d["mlstm_qkT"], c)).then_inc(slot_in[b], 16)
                sp.dma_start(va[b][:, :, 0:HD], heads(tile_of(d["mlstm_vo"], c)[:, 0:GW])).then_inc(slot_in[b], 16)
                sp.dma_start(o_in[b][:], tile_of(d["mlstm_vo"], c)[:, GW:2 * GW]).then_inc(slot_in[b], 16)
                sp.dma_start(rows[b][:], d["mlstm_rows"][:, bass.ds(c * P, P)]).then_inc(slot_in[b], 16)

            def store(c):
                sp.wait_ge(y_ready, c + 1)
                sp.dma_start(tile_of(d["y1"], c)[:, 2 * GW:3 * GW], y_out[:]).then_inc(y_stored, 16)

            sp.sem_inc(y_stored, 16)
            sp.dma_start(run_max[:], d["mlstm_max"]).then_inc(const_in, 16)
            sp.dma_start(carry_row[:], d["mlstm_carry"]).then_inc(const_in, 16)
            sp.dma_start(gain[:], d["mlstm_out_g"].partition_broadcast(P)).then_inc(const_in, 16)
            sp.wait_ge(zeroed, 1)
            load(0, 0)
            load(1, 1)
            with sp.Fori(0, NT // 2 - 1) as j:
                for b in range(2):
                    c = 2 * j + b
                    sp.wait_ge(pe_done, c + 1)
                    sp.wait_ge(o_used, c + 1)
                    load(c + 2, b)
                    store(c)
            store(NT - 2)
            store(NT - 1)
            sp.wait_ge(y_stored, 16 * (NT + 1))

        @block.gpsimd
        def _(pool):
            nc.gpsimd.memset(sel[:], 0.0)
            nc.gpsimd.memset(k_pad[:], 0.0)
            nc.gpsimd.memset(state[:], 0.0)
            for b in range(2):
                nc.gpsimd.memset(va[b][:], 1.0)
            nc.gpsimd.memset(past[:], 1.0)
            pool.drain().then_inc(zeroed, 1)
            nc.gpsimd.affine_select(out=past[:], in_=past[:], compare_op=ALU.is_ge, fill=0.0, base=0, pattern=[[1, P]],
                                    channel_multiplier=-1)
            pool.drain()
            nc.gpsimd.affine_select(out=sel[:], in_=sel[:], compare_op=ALU.not_equal, fill=-1.0, base=0,
                                    pattern=[[-1, GH], [0, P]], channel_multiplier=1).then_inc(sel_ready, 1)

            def chunk(c, b, j):
                pool.wait_ge(e_ready, c + 1)
                nc.gpsimd.tensor_tensor(e[:], e[:], past[:].unsqueeze(1).to_broadcast([P, GH, P]), ALU.mult)\
                    .then_inc(mask_ready, 1)
                pool.wait_ge(gate_in, c + 1)
                nc.gpsimd.tensor_tensor(gate2[:], gate[:], g.one[:].to_broadcast([P, GW]), ALU.add).then_inc(gate_ready, 1)
                pool.drain().then_inc(gate_free, 1)
                pool.wait_ge(h_in, c + 1)
                nc.gpsimd.tensor_tensor(h2[:], h1[:], h1[:], ALU.mult).then_inc(h_sq_ready, 1)
                pool.wait_ge(nd_done, c + 1)
                nc.gpsimd.tensor_tensor(h_var[:], h_sq[:], g.head_eps[:].to_broadcast([P, GH]), ALU.add)
                pool.drain()
                nc.gpsimd.tensor_tensor(h_rstd[:], h_var[:], g.neg_half[:].to_broadcast([P, GH]), ALU.pow)\
                    .then_inc(h_rstd_ready, 1)

            pool.sem_inc(gate_free, 1)
            pairs(pool, chunk)

        @block.scalar
        def _(act):
            act.sem_inc(st_ready, 1)
            act.wait_ge(zeroed, 1)
            act.wait_ge(carry_ready, 1)
            nc.scalar.activation(carry[:], p_max[:, :, 0:NT], ACT.Copy, scale=-1.0).then_inc(carry_ready, 1)

            def chunk(c, b, j):
                act.wait_ge(slot_in[b], 16 * LOADS * (j + 1))
                act.wait_ge(st_ready, c + 1)
                for half in range(2):
                    at = slice(half * HD, (half + 1) * HD)
                    nc.scalar.activation(k_pad[at, half::2, :], qk[b][at, NB:2 * NB, :], ACT.Copy)
                act.drain().then_inc(pad_ready, 1)
                act.wait_ge(gate_free, c + 1)
                nc.scalar.activation(gate[:], o_in[b][:], ACT.Exp, scale=-1.0).then_inc(gate_in, 1)
                act.drain().then_inc(o_used, 1)
                act.wait_ge(arg_ready, c + 1)
                nc.scalar.activation(e[:], arg[:], ACT.Exp).then_inc(e_ready, 1)

            pairs(act, chunk)

        @block.tensor
        def _(pe):
            pe.wait_ge(const_in, 48)
            pe.wait_ge(sel_ready, 1)
            for h in range(GH):
                last = nc.tensor.matmul(p_max[:, h, 0:NT], sel[:, h, :], carry_row[:], start=True, stop=True)
            last.then_inc(carry_ready, 1)
            pe.wait_ge(carry_ready, 2)

            def chunk(c, b, j):
                pe.wait_ge(slot_in[b], 16 * LOADS * (j + 1))
                pe.wait_ge(kw_ready, c + 1)
                for n in range(NB):
                    nc.tensor.transpose(p_t[:, n * P:(n + 1) * P], qk[b][:, NB + n, :], g.ident[:])
                nc.tensor.transpose(p_t[:, GW:GW + 4 * GH], rows[b][:], g.ident[0:4 * GH, 0:4 * GH]).then_inc(t_ready, 1)
                for h in range(GH):
                    last = nc.tensor.matmul(p_max[:, h, :], sel[:, h, :], run_max[:, bass.ds(c * P, P)],
                                            start=True, stop=True)
                last.then_inc(max_ready, 1)
                pe.wait_ge(pad_ready, c + 1)
                for h in range(GH):
                    last = nc.tensor.matmul(p_st[:, h, :], k_pad[:, h, :], qk[b][:, h // 2, :], start=True, stop=True)
                last.then_inc(st_ready, 1)
                pe.wait_ge(state_ready, c + 1)
                for n in range(NB):
                    last = nc.tensor.matmul(p_inter[:, n * 2 * VW:(n + 1) * 2 * VW], qk[b][:, n, :], state[:, n, :],
                                            start=True, stop=True)
                last.then_inc(inter_ready, 1)
                pe.wait_ge(kw_ready, c + 2)
                for n in range(NB):
                    last = nc.tensor.matmul(p_state[:, n * 2 * VW:(n + 1) * 2 * VW], kw[:, n * P:(n + 1) * P],
                                            va[b][:, 2 * n:2 * n + 2, :].rearrange("p h d -> p (h d)"),
                                            start=True, stop=True)
                last.then_inc(state_out, 1)
                pe.wait_ge(sm_ready, c + 1)
                for h in range(GH):
                    last = nc.tensor.matmul(p_num[:, h * VW:(h + 1) * VW], sm[:, h, :], va[b][:, h, :],
                                            start=True, stop=True)
                last.then_inc(num_ready, 1)
                pe.drain().then_inc(pe_done, 1)

            pairs(pe, chunk)

        @block.vector
        def _(dve):
            def chunk(c, b, j):
                dve.wait_ge(t_ready, c + 1)
                nc.vector.tensor_copy(cols[:], p_t[:, GW:GW + 4 * GH])
                dve.drain()
                a, w_inter, w_new, e_neg_m = (cols[:, n * GH:(n + 1) * GH] for n in range(4))
                nc.vector.scalar_tensor_tensor(heads(kw[:]), heads(p_t[:, 0:GW]), HD ** -0.5, along(w_new, HD),
                                               ALU.mult, ALU.mult).then_inc(kw_ready, 1)
                dve.wait_ge(max_ready, c + 1)
                for h in range(GH):
                    nc.vector.tensor_scalar(arg[:, h, :], p_max[:, h, :], a[:, h:h + 1], 0.0, ALU.add, ALU.min)
                dve.drain().then_inc(arg_ready, 1)
                dve.wait_ge(inter_ready, c + 1)
                nc.vector.tensor_tensor(nd[:], p_inter[:, 0:GH * VW].rearrange("p (h d) -> p h d", d=VW), along(w_inter, VW),
                                        ALU.mult)
                dve.wait_ge(state_out, c + 1)
                for n in range(NB):
                    for half in range(2):
                        at, h = slice(half * HD, (half + 1) * HD), 2 * n + half
                        cs = slice(half * VW, (half + 1) * VW)
                        nc.vector.scalar_tensor_tensor(state[at, n, cs], state[at, n, cs], carry[at, h, bass.ds(c, 1)],
                                                       p_state[at, n * 2 * VW + half * VW:n * 2 * VW + (half + 1) * VW],
                                                       ALU.mult, ALU.add)
                dve.drain().then_inc(state_ready, 1)
                dve.wait_ge(st_ready, c + 2)
                dve.wait_ge(mask_ready, c + 1)
                nc.vector.scalar_tensor_tensor(sm[:], p_st[:], HD ** -0.5, e[:], ALU.mult, ALU.mult).then_inc(sm_ready, 1)
                dve.wait_ge(num_ready, c + 1)
                nc.vector.tensor_tensor(nd2[:], nd[:], p_num[:, 0:GH * VW].rearrange("p (h d) -> p h d", d=VW), ALU.add)
                dve.drain()
                nc.vector.scalar_tensor_tensor(den[:], nd2[:, :, HD], -1.0, nd2[:, :, HD], ALU.mult, ALU.max)
                dve.drain()
                nc.vector.tensor_tensor(den2[:], den[:], e_neg_m, ALU.max)
                dve.drain()
                nc.vector.reciprocal(inv[:], den2[:])
                dve.wait_ge(gate_ready, c + 1)
                nc.vector.reciprocal(o_gate[:], gate2[:])
                dve.drain()
                nc.vector.tensor_tensor(heads(h_tmp[:]), nd2[:, :, 0:HD], along(inv[:], HD), ALU.mult)
                dve.drain()
                nc.vector.tensor_tensor(h1[:], h_tmp[:], o_gate[:], ALU.mult).then_inc(h_in, 1)
                dve.wait_ge(h_sq_ready, c + 1)
                nc.vector.tensor_reduce(h_sq[:], heads(h2[:]), AX.X, ALU.add).then_inc(nd_done, 1)
                dve.wait_ge(h_rstd_ready, c + 1)
                nc.vector.tensor_tensor(heads(h_tmp[:]), heads(h1[:]), along(h_rstd[:], HD), ALU.mult)
                dve.drain()
                dve.wait_ge(y_stored, 16 * (c + 1))
                nc.vector.tensor_tensor(y_out[:], h_tmp[:], gain[:], ALU.mult).then_inc(y_ready, 1)

            dve.wait_ge(const_in, 48)
            nc.vector.tensor_scalar(gain[:], gain[:], HD ** 0.5, None, ALU.mult)
            dve.wait_ge(zeroed, 1)
            dve.wait_ge(carry_ready, 2)
            dve.sem_inc(kw_ready, 1)
            dve.sem_inc(state_ready, 1)
            pairs(dve, chunk)
    ph.close()


F_B, F_K, F_KK, F_R, F_V, F_RK = range(6)
NF = 6
NB = GW // P
RANK = 16
DECAY = float(np.exp(-0.5))


def rwkv_factors(nc, d, g, big, to_next):
    ph = Phase(nc, "rfac")
    sb, ps, sem = ph.sb, ph.ps, ph.sem
    low = [sb(f"low{n}", [RANK, 1 + T]) for n in range(2)]
    low_s = [sb(f"low_s{n}", [RANK, T]) for n in range(2)]
    low_mu = sb("low_mu", [RANK, 2])
    up = sb("up", [RANK, 2, GW])
    cols = sb("cols", [P, NB, 5])
    head_ones = sb("head_ones", [P, P])
    not_first = sb("not_first", [P, T])
    r, k, sg, a, kk, cum, tmp = (sb(n, [P, T]) for n in ("r", "k", "sg", "a", "kk", "cum", "tmp"))
    mid = sb("mid", [P, NB, NT])
    p_w, p_a = ps("w", [P, T]), ps("a", [P, T])
    const_in, rk_in, v_in, consts_ready, shifted, tanh_ready, w_ready, a_ready, sg_ready, a_done = (
        sem(n) for n in ("const_in", "rk_in", "v_in", "consts_ready", "shifted", "tanh_ready", "w_ready", "a_ready",
                         "sg_ready", "a_done"))
    sq_ready, sum_ready, clamped, norm_ready, arg_ready, exp_ready, block_done, pad_ready = (
        sem(n) for n in ("sq_ready", "sum_ready", "clamped", "norm_ready", "arg_ready", "exp_ready", "block_done",
                         "pad_ready"))

    def chunks(ap):
        return ap.rearrange("p (c t) -> p c t", t=P)

    with nc.Block() as block:
        @block.sync
        def _(sp):
            sp.wait_ge(pad_ready, 1)
            sp.dma_start(low[0][:, 1:], d["lowT"][0:RANK, :]).then_inc(const_in, 16)
            sp.dma_start(low[1][:, 1:], d["lowT"][32:32 + RANK, :]).then_inc(const_in, 16)
            sp.dma_start(low_mu[:], d["rwkv_low_mu"]).then_inc(const_in, 16)
            sp.dma_start(up[:], d["rwkv_up"]).then_inc(const_in, 16)
            sp.dma_start(cols[:], d["rwkv_cols"]).then_inc(const_in, 16)
            for n in range(NB):
                if n:
                    sp.wait_ge(block_done, n)
                sp.dma_start(r[:], d["rwkv_T"][n * P:(n + 1) * P, :]).then_inc(rk_in, 16)
                sp.dma_start(k[:], d["rwkv_T"][GW + n * P:GW + (n + 1) * P, :]).then_inc(rk_in, 16)
                sp.dma_start(big[:, n, F_V, :], d["rwkv_T"][2 * GW + n * P:2 * GW + (n + 1) * P, :]).then_inc(v_in, 16)
            sp.wait_ge(v_in, 16 * NB)

        @block.gpsimd
        def _(pool):
            for n in range(2):
                nc.gpsimd.memset(low[n][:, 0:1], 0.0)
            pool.drain().then_inc(pad_ready, 1)
            nc.gpsimd.memset(not_first[:], 1.0)
            nc.gpsimd.memset(head_ones[:], 1.0)
            nc.gpsimd.memset(to_next[:], 1.0)
            pool.drain()
            nc.gpsimd.memset(chunks(not_first[:])[:, :, 0:1], 0.0)
            nc.gpsimd.affine_select(out=head_ones[:, 0:HD], in_=head_ones[:, 0:HD], compare_op=ALU.is_ge, fill=0.0,
                                    base=HD - 1, pattern=[[0, HD]], channel_multiplier=-1)
            nc.gpsimd.affine_select(out=head_ones[:, HD:P], in_=head_ones[:, HD:P], compare_op=ALU.is_ge, fill=0.0,
                                    base=-HD, pattern=[[0, HD]], channel_multiplier=1)
            pool.drain().then_inc(consts_ready, 1)

        @block.tensor
        def _(pe):
            pe.wait_ge(consts_ready, 1)
            pe.wait_ge(shifted, 1)
            pe.wait_ge(tanh_ready, 1)
            for n in range(NB):
                if n:
                    pe.wait_ge(clamped, n)
                    pe.wait_ge(a_done, n)
                for out, i, ready in ((p_w, 0, w_ready), (p_a, 1, a_ready)):
                    for c in range(0, T, BANK):
                        last = nc.tensor.matmul(out[:, c:c + BANK], up[:, i, n * P:(n + 1) * P], low_s[i][:, c:c + BANK],
                                                start=True, stop=True)
                    last.then_inc(ready, 1)
                pe.wait_ge(sg_ready, n + 1)
                pe.wait_ge(sq_ready, n + 1)
                for c in range(0, T, BANK):
                    last = nc.tensor.matmul(p_w[:, c:c + BANK], head_ones[:], tmp[:, c:c + BANK], start=True, stop=True)
                last.then_inc(sum_ready, 1)

        @block.scalar
        def _(act):
            act.wait_ge(shifted, 1)
            nc.scalar.activation(low_s[0][:], low_s[0][:], ACT.Tanh).then_inc(tanh_ready, 1)
            for n in range(NB):
                act.wait_ge(w_ready, n + 1)
                if n:
                    act.wait_ge(block_done, n)
                nc.scalar.activation(sg[:], p_w[:], ACT.Sigmoid, bias=cols[:, n, 0:1]).then_inc(sg_ready, 1)
                act.wait_ge(a_ready, n + 1)
                nc.scalar.activation(a[:], p_a[:], ACT.Sigmoid, bias=cols[:, n, 1:2]).then_inc(a_done, 1)
                act.wait_ge(clamped, n + 1)
                nc.scalar.activation(tmp[:], tmp[:], ACT.Sqrt).then_inc(norm_ready, 1)
                for i, (src, scale) in enumerate(((cum, -DECAY), (tmp, -DECAY), (cum, DECAY))):
                    act.wait_ge(arg_ready, 4 * n + i + 1)
                    nc.scalar.activation(tmp[:], src[:], ACT.Exp, scale=scale).then_inc(exp_ready, 1)
                act.wait_ge(arg_ready, 4 * n + 4)
                nc.scalar.activation(mid[:, n, :], mid[:, n, :], ACT.Exp, scale=-DECAY).then_inc(exp_ready, 1)

        @block.vector
        def _(dve):
            dve.wait_ge(const_in, 16 * 5)
            dve.wait_ge(pad_ready, 1)
            for i in range(2):
                x, previous = low[i][:, 1:], low[i][:, 0:T]
                nc.vector.tensor_tensor(low_s[i][:], previous, x, ALU.subtract)
                dve.drain()
                nc.vector.scalar_tensor_tensor(low_s[i][:], low_s[i][:], low_mu[:, i:i + 1], x, ALU.mult, ALU.add)
            dve.drain().then_inc(shifted, 1)
            dve.wait_ge(consts_ready, 1)
            for n in range(NB):
                f = [big[:, n, i, :] for i in range(NF)]
                k_k, k_a, r_k = (cols[:, n, i:i + 1] for i in (2, 3, 4))
                dve.wait_ge(rk_in, 32 * (n + 1))
                nc.vector.tensor_scalar(kk[:], k[:], k_k, None, ALU.mult)
                dve.drain()
                nc.vector.tensor_tensor(tmp[:], kk[:], kk[:], ALU.mult).then_inc(sq_ready, 1)
                dve.wait_ge(sum_ready, n + 1)
                nc.vector.tensor_scalar(tmp[:], p_w[:], 1e-24, None, ALU.max).then_inc(clamped, 1)
                dve.wait_ge(a_done, n + 1)
                nc.vector.tensor_scalar(f[F_RK], a[:], 1.0, k_a, ALU.subtract, ALU.mult)
                dve.drain()
                nc.vector.scalar_tensor_tensor(f[F_K], f[F_RK], 1.0, k[:], ALU.add, ALU.mult)
                dve.drain()
                nc.vector.scalar_tensor_tensor(f[F_RK], r[:], r_k, f[F_K], ALU.mult, ALU.mult)
                dve.wait_ge(norm_ready, n + 1)
                nc.vector.reciprocal(tmp[:], tmp[:])
                dve.drain()
                nc.vector.tensor_tensor(kk[:], kk[:], tmp[:], ALU.mult)
                dve.drain()
                nc.vector.tensor_tensor(f[F_B], kk[:], a[:], ALU.mult)
                dve.wait_ge(sg_ready, n + 1)
                nc.vector.tensor_tensor_scan(cum[:], not_first[:], sg[:], 0.0, ALU.mult, ALU.add)
                dve.drain()
                nc.vector.tensor_copy(mid[:, n, :], chunks(cum[:])[:, :, P // 2 - 1])
                dve.drain()
                nc.vector.tensor_tensor(chunks(cum[:]), chunks(cum[:]), along(mid[:, n, :], P), ALU.subtract)\
                    .then_inc(arg_ready, 1)
                dve.wait_ge(exp_ready, 4 * n + 1)
                nc.vector.tensor_tensor(f[F_R], r[:], tmp[:], ALU.mult)
                nc.vector.tensor_copy(to_next[:, n, :], chunks(tmp[:])[:, :, P - 1])
                dve.drain()
                nc.vector.tensor_tensor(tmp[:], cum[:], sg[:], ALU.subtract).then_inc(arg_ready, 1)
                dve.wait_ge(exp_ready, 4 * n + 2)
                nc.vector.tensor_tensor(f[F_KK], kk[:], tmp[:], ALU.mult)
                dve.drain().then_inc(arg_ready, 1)
                dve.wait_ge(exp_ready, 4 * n + 3)
                nc.vector.tensor_tensor(f[F_B], f[F_B], tmp[:], ALU.mult)
                nc.vector.tensor_tensor(f[F_K], f[F_K], tmp[:], ALU.mult)
                dve.drain().then_inc(arg_ready, 1)
                dve.wait_ge(exp_ready, 4 * n + 4)
                nc.vector.tensor_tensor(to_next[:, n, 0:NT - 1], to_next[:, n, 0:NT - 1], mid[:, n, 1:NT], ALU.mult)
                dve.drain().then_inc(block_done, 1)
    ph.close()


def rwkv_chunks(nc, d, g, big, to_next):
    ph = Phase(nc, "rwkv")
    sb, ps, sem = ph.sb, ph.ps, ph.sem
    LEVELS = 7
    slot = sb("slot", [P, NB, NF, P])
    pad = sb("pad", [P, GH, F_KK + 1, P])
    keep = sb("keep", [P, 4, P], U32)
    keep_low = sb("keep_low", [P, GH, P], U32)
    level = sb("level", [P, LEVELS, P])
    level0 = sb("level0", [P, P])
    tri = sb("tri", [P, GH, P])
    prod = sb("prod", [P, GH, 4, P])
    a_low = sb("a_low", [P, GH, P])
    lt = sb("lt", [P, LEVELS, GH, P])
    x = sb("x", [P, 2, 2, 2, P])
    xl = [sb(f"xl{p}", [P, 2, P]) for p in range(2)]
    tok = sb("tok", [P, 2, GW])
    v = sb("v", [P, GW])
    head_sel = sb("head_sel", [P, 2])
    bonus = sb("bonus", [P, GH])
    state = sb("state", [P, NB, P])
    u, removed, y, y2, y3, y4, y_out = (sb(n, [P, GW]) for n in ("u", "removed", "y", "y2", "y3", "y4", "y_out"))
    y_sq, y_var, y_rstd, gain = sb("y_sq", [P, GH]), sb("y_var", [P, GH]), sb("y_rstd", [P, GH]), sb("gain", [P, GW])
    p_b = [ps(f"b{n}", [P, BANK]) for n in range(8)]
    P_A, P_TOK, P_V, P_U = 4, 5, 6, 7
    names = ("const_in", "zeroed", "masks_ready", "slot_ready", "slot_free", "prod_out", "a_out", "tok_out", "v_out",
             "prod_ready", "a_ready", "tok_ready", "v_ready", "lt_ready", "x_first", "taken", "u_out", "u_ready", "removed_out",
             "removed_ready", "y_out_ready", "state_out", "state_ready", "y_ready", "y_sq_ready", "y_sum_ready", "y_rstd_ready",
             "bonus_ready", "bonus_free", "out_ready", "stored")
    (const_in, zeroed, masks_ready, slot_ready, slot_free, prod_out, a_out, tok_out, v_out, prod_ready, a_ready, tok_ready,
     v_ready, lt_ready, x_first, taken, u_out, u_ready, removed_out, removed_ready, y_done, state_out, state_ready, y_ready,
     y_sq_ready, y_sum_ready, y_rstd_ready, bonus_ready, bonus_free, out_ready, stored) = (sem(n) for n in names)
    xl_out, xl_ready, x_out, x_ready = ([sem(f"{n}{p}") for p in range(2)] for n in ("xl_out", "xl_ready", "x_out", "x_ready"))
    UP = LEVELS - 1

    def chunk_of(c):
        return big[:, :, :, bass.ds(c * P, P)]

    with nc.Block() as block:
        @block.sync
        def _(sp):
            sp.sem_inc(stored, 16)
            sp.dma_start(gain[:], d["rwkv_ln_g"].partition_broadcast(P)).then_inc(const_in, 16)
            with sp.Fori(0, NT) as c:
                sp.wait_ge(out_ready, c + 1)
                sp.dma_start(tile_of(d["y1"], c)[:, 4 * GW:5 * GW], y_out[:]).then_inc(stored, 16)
            sp.wait_ge(stored, 16 * (NT + 1))

        @block.gpsimd
        def _(pool):
            nc.gpsimd.memset(pad[:], 0.0)
            nc.gpsimd.memset(state[:], 0.0)
            nc.gpsimd.memset(prod[:], 0.0)
            nc.gpsimd.memset(a_low[:], 0.0)
            pool.drain().then_inc(zeroed, 1)
            nc.gpsimd.memset(tri[:], 1.0)
            nc.gpsimd.memset(level[:], 1.0)
            nc.gpsimd.memset(level0[:], 1.0)
            nc.gpsimd.memset(head_sel[:], 1.0)
            pool.drain()

            def where(ap, base, pattern, mult):
                nc.gpsimd.affine_select(out=ap, in_=ap, compare_op=ALU.is_ge, fill=0.0, base=base, pattern=pattern,
                                        channel_multiplier=mult)
                pool.drain()

            where(tri[:, 0::2, :], -1, [[0, 2], [1, P]], -1)
            where(tri[:, 1::2, :], 0, [[0, 2], [1, P]], -1)
            nc.gpsimd.tensor_copy(keep[:], tri[:])
            pool.drain()
            nc.gpsimd.memset(tri[:], 1.0)
            pool.drain()
            where(tri[:], -1, [[0, GH], [-1, P]], 1)
            nc.gpsimd.tensor_copy(keep_low[:], tri[:])
            where(head_sel[:, 0:1], HD - 1, [[0, 1]], -1)
            where(head_sel[:, 1:2], -HD, [[0, 1]], 1)
            for i in range(LEVELS):
                n = 1 << i
                ap = level[:, i, :].rearrange("p (b t) -> p b t", t=2 * n)
                nc.gpsimd.memset(ap[:, :, 0:n], 0.0)
                pool.drain()
                where(ap, 0, [[-2 * n, P // (2 * n)], [0, 2 * n]], 1)
                where(ap, n - 1, [[2 * n, P // (2 * n)], [0, 2 * n]], -1)
            ap = level0[:].rearrange("p (b s) -> p b s", s=2)
            nc.gpsimd.memset(ap[:, :, 1:2], 0.0)
            pool.drain()
            where(ap, -1, [[-2, P // 2], [-1, 2]], 1)
            where(ap, 1, [[2, P // 2], [1, 2]], -1)
            pool.drain().then_inc(masks_ready, 1)

            def chunk(c):
                pool.wait_ge(prod_ready, c + 1)
                pool.wait_ge(slot_free, c + 1)
                for i in range(LEVELS):
                    nc.gpsimd.tensor_tensor(lt[:, i], prod[:, :, 0, :], level[:, i:i + 1, :].to_broadcast([P, GH, P]),
                                            ALU.mult).then_inc(lt_ready, 1)
                pool.wait_ge(v_ready, c + 1)
                nc.gpsimd.tensor_tensor(heads(y4[:]), heads(v[:]), along(bonus[:], HD), ALU.mult).then_inc(bonus_ready, 1)
                pool.wait_ge(y_ready, c + 1)
                nc.gpsimd.tensor_tensor(y2[:], y[:], y[:], ALU.mult).then_inc(y_sq_ready, 1)
                pool.wait_ge(y_sum_ready, c + 1)
                nc.gpsimd.tensor_tensor(y_var[:], y_sq[:], g.head_eps[:].to_broadcast([P, GH]), ALU.add)
                pool.drain()
                nc.gpsimd.tensor_tensor(y_rstd[:], y_var[:], g.neg_half[:].to_broadcast([P, GH]), ALU.pow)\
                    .then_inc(y_rstd_ready, 1)

            with pool.Fori(0, NT) as c:
                chunk(c)

        @block.scalar
        def _(act):
            act.wait_ge(zeroed, 1)

            def chunk(c):
                act.wait_ge(slot_free, c + 1)
                nc.scalar.activation(slot[:], chunk_of(c), ACT.Copy)
                for half in range(2):
                    at = slice(half * HD, (half + 1) * HD)
                    nc.scalar.activation(pad[at, half::2], chunk_of(c)[at, :, 0:F_KK + 1], ACT.Copy)
                act.drain().then_inc(slot_ready, 1)
                act.wait_ge(tok_out, c + 1)
                nc.scalar.activation(tok[:].rearrange("p a c -> p (a c)"), p_b[P_TOK][:], ACT.Copy).then_inc(tok_ready, 1)
                act.wait_ge(v_out, c + 1)
                act.wait_ge(bonus_free, c + 1)
                nc.scalar.activation(v[:], p_b[P_V][:, 0:GW], ACT.Copy)
                nc.scalar.activation(bonus[:], p_b[P_V][:, GW:GW + GH], ACT.Copy)
                act.drain().then_inc(v_ready, 1)
                for i in range(UP):
                    for p in range(2):
                        act.wait_ge(xl_out[p], UP * c + i + 1)
                        nc.scalar.activation(xl[p][:].rearrange("p h c -> p (h c)"), p_b[p][:, 0:2 * P], ACT.Copy)\
                            .then_inc(xl_ready[p], 1)
                act.wait_ge(u_out, c + 1)
                nc.scalar.activation(u[:], p_b[P_U][:, 0:GW], ACT.Copy).then_inc(u_ready, 1)
                act.wait_ge(removed_out, c + 1)
                nc.scalar.activation(removed[:], p_b[P_A][:, 0:GW], ACT.Copy, scale=-1.0).then_inc(removed_ready, 1)
                act.wait_ge(y_done, c + 1)
                nc.scalar.activation(y[:], p_b[P_TOK][:, 0:GW], ACT.Copy).then_inc(y_ready, 1)

            with act.Fori(0, NT) as c:
                chunk(c)

        @block.tensor
        def _(pe):
            pe.wait_ge(zeroed, 1)
            pe.wait_ge(masks_ready, 1)
            pe.sem_inc(slot_free, 1)

            def products(c):
                pe.wait_ge(slot_ready, c + 1)
                pe.wait_ge(state_ready, c + 1)
                for h in range(GH):
                    rhs = slot[:, h // 2, F_KK:F_R + 1, :].rearrange("p f t -> p (f t)")
                    for i, f in enumerate((F_B, F_K)):
                        last = nc.tensor.matmul(p_b[h][:, i * 2 * P:(i + 1) * 2 * P], pad[:, h, f, :], rhs,
                                                start=True, stop=True)
                    last.then_inc(prod_out, 1)
                for h in range(GH):
                    last = nc.tensor.matmul(p_b[P_A][:, h * P:(h + 1) * P], pad[:, h, F_KK, :], slot[:, h // 2, F_B, :],
                                            start=True, stop=True)
                last.then_inc(a_out, 1)
                for i, f in enumerate((F_B, F_K)):
                    for n in range(NB):
                        at = i * GW + n * P
                        last = nc.tensor.transpose(p_b[P_TOK][:, at:at + P], slot[:, n, f, :], g.ident[:])
                last.then_inc(tok_out, 1)
                for n in range(NB):
                    nc.tensor.transpose(p_b[P_V][:, n * P:(n + 1) * P], slot[:, n, F_V, :], g.ident[:])
                for n in range(NB):
                    last = nc.tensor.matmul(p_b[P_V][:, GW + 2 * n:GW + 2 * n + 2], slot[:, n, F_RK, :], head_sel[:],
                                            start=True, stop=True)
                last.then_inc(v_out, 1)

            def inverse(c):
                pe.wait_ge(x_first, c + 1)
                for i in range(UP):
                    pe.wait_ge(lt_ready, LEVELS * c + i + 2)
                    for p in range(2):
                        if i:
                            pe.wait_ge(x_ready[p], UP * c + i)
                        for j in range(2):
                            last = nc.tensor.matmul(p_b[p][:, j * P:(j + 1) * P], lt[:, i + 1, 2 * p + j, :], x[:, p, 0, j, :],
                                                    start=True, stop=True)
                        last.then_inc(xl_out[p], 1)
                    for p in range(2):
                        pe.wait_ge(xl_ready[p], UP * c + i + 1)
                        for j in range(2):
                            nc.tensor.matmul(p_b[2 + p][:, j * P:(j + 1) * P], x[:, p, 1, j, :], xl[p][:, j, :],
                                             start=True, stop=True)
                            last = nc.tensor.matmul(p_b[2 + p][:, (2 + j) * P:(3 + j) * P], xl[p][:, j, :], x[:, p, 1, j, :],
                                                    start=True, stop=True)
                        last.then_inc(x_out[p], 1)

            def through_state(c):
                pe.wait_ge(v_ready, c + 1)
                for n in range(NB):
                    nc.tensor.matmul(p_b[P_U][:, n * P:(n + 1) * P], slot[:, n, F_KK, :], state[:, n, :], start=True, stop=False)
                    for h in (2 * n, 2 * n + 1):
                        last = nc.tensor.matmul(p_b[P_U][:, h * HD:(h + 1) * HD], prod[:, h, 2, :], v[:, h * HD:(h + 1) * HD],
                                                start=False, stop=(h % 2 == 1))
                last.then_inc(u_out, 1)
                pe.wait_ge(u_ready, c + 1)
                for p in range(2):
                    pe.wait_ge(x_ready[p], UP * (c + 1))
                for h in range(GH):
                    last = nc.tensor.matmul(p_b[P_A][:, h * HD:(h + 1) * HD], x[:, h // 2, 1, h % 2, :],
                                            u[:, h * HD:(h + 1) * HD], start=True, stop=True)
                last.then_inc(removed_out, 1)
                pe.wait_ge(tok_ready, c + 1)
                pe.wait_ge(removed_ready, c + 1)
                for n in range(NB):
                    cs = slice(n * P, (n + 1) * P)
                    nc.tensor.matmul(p_b[P_V][:, cs], g.ident[:], state[:, n, :], start=True, stop=False)
                    nc.tensor.matmul(p_b[P_V][:, cs], tok[:, 1, cs], v[:, cs], start=False, stop=False)
                    last = nc.tensor.matmul(p_b[P_V][:, cs], tok[:, 0, cs], removed[:, cs], start=False, stop=True)
                last.then_inc(state_out, 1)
                for n in range(NB):
                    nc.tensor.matmul(p_b[P_TOK][:, n * P:(n + 1) * P], slot[:, n, F_R, :], state[:, n, :], start=True, stop=False)
                    for h in (2 * n, 2 * n + 1):
                        hs = slice(h * HD, (h + 1) * HD)
                        nc.tensor.matmul(p_b[P_TOK][:, hs], prod[:, h, 3, :], v[:, hs], start=False, stop=False)
                        last = nc.tensor.matmul(p_b[P_TOK][:, hs], prod[:, h, 1, :], removed[:, hs], start=False,
                                                stop=(h % 2 == 1))
                last.then_inc(y_done, 1)
                pe.drain().then_inc(slot_free, 1)

            with pe.Fori(0, NT) as c:
                products(c)
                inverse(c)
                through_state(c)

        @block.vector
        def _(dve):
            dve.wait_ge(const_in, 16)
            nc.vector.tensor_scalar(gain[:], gain[:], HD ** 0.5, None, ALU.mult)
            dve.wait_ge(zeroed, 1)
            dve.wait_ge(masks_ready, 1)
            dve.sem_inc(bonus_free, 1)
            dve.sem_inc(state_ready, 1)

            def chunk(c):
                dve.wait_ge(slot_free, c + 1)
                for h in range(GH):
                    wait_apart(dve, prod_out, GH * c + h + 1, taken)
                    nc.vector.copy_predicated(prod[:, h].rearrange("p f t -> p (f t)"), keep[:].rearrange("p f t -> p (f t)"),
                                              p_b[h][:])
                dve.drain().then_inc(prod_ready, 1)
                wait_apart(dve, a_out, c + 1, taken)
                nc.vector.copy_predicated(a_low[:].rearrange("p h s -> p (h s)"), keep_low[:].rearrange("p h s -> p (h s)"),
                                          p_b[P_A][:])
                dve.drain()
                dve.wait_ge(lt_ready, LEVELS * c + 1)
                ident = g.ident[:].unsqueeze(1).to_broadcast([P, 2, P])
                for p in range(2):
                    nc.vector.tensor_tensor(x[:, p, 0], a_low[:, 2 * p:2 * p + 2, :],
                                            level0[:].unsqueeze(1).to_broadcast([P, 2, P]), ALU.mult)
                dve.drain()
                for p in range(2):
                    nc.vector.tensor_tensor(x[:, p, 0], ident, x[:, p, 0], ALU.subtract)
                    nc.vector.tensor_tensor(x[:, p, 1], ident, lt[:, 0, 2 * p:2 * p + 2, :], ALU.subtract)
                dve.drain().then_inc(x_first, 1)
                for i in range(UP):
                    for p in range(2):
                        dve.wait_ge(x_out[p], UP * c + i + 1)
                        xp = x[:, p].rearrange("p a h c -> p (a h c)")
                        nc.vector.tensor_tensor(xp, xp, p_b[2 + p][:], ALU.subtract).then_inc(x_ready[p], 1)
                dve.drain()
                dve.wait_ge(state_out, c + 1)
                dve.wait_ge(y_done, c + 1)
                for n in range(NB):
                    for half in range(2):
                        at = slice(half * HD, (half + 1) * HD)
                        nc.vector.tensor_scalar(state[at, n, at], p_b[P_V][at, n * P + half * HD:n * P + (half + 1) * HD],
                                                to_next[at, n, bass.ds(c, 1)], None, ALU.mult)
                dve.drain().then_inc(state_ready, 1)
                dve.wait_ge(y_sq_ready, c + 1)
                nc.vector.tensor_reduce(y_sq[:], heads(y2[:]), AX.X, ALU.add).then_inc(y_sum_ready, 1)
                dve.wait_ge(y_rstd_ready, c + 1)
                nc.vector.tensor_tensor(heads(y3[:]), heads(y[:]), along(y_rstd[:], HD), ALU.mult)
                dve.drain()
                nc.vector.tensor_tensor(y3[:], y3[:], gain[:], ALU.mult)
                dve.drain()
                dve.wait_ge(bonus_ready, c + 1)
                dve.wait_ge(stored, 16 * (c + 1))
                nc.vector.tensor_tensor(y_out[:], y3[:], y4[:], ALU.add).then_inc(out_ready, 1)
                dve.drain().then_inc(bonus_free, 1)

            with dve.Fori(0, NT) as c:
                chunk(c)
    ph.close()


def rwkv(nc, d, g):
    with nc.sbuf_tensor("rwkv_big", [P, NB, NF, T], F32) as big, nc.sbuf_tensor("rwkv_to_next", [P, NB, NT], F32) as to_next:
        rwkv_factors(nc, d, g, big, to_next)
        rwkv_chunks(nc, d, g, big, to_next)


D2 = 512
H2 = D2 // HD
GRID_W = 64
WIN_R, WIN_C = 8, 16
REL_C = 2 * WIN_C - 1
REL_R = 2 * WIN_R - 1
TK2 = T + NMEM


def ada_phase(nc, d, g):
    ph = Phase(nc, "ada")
    sb, ps, sem = ph.sb, ph.ps, ph.sem
    w = [sb(f"w{b}", [P, KB, BANK]) for b in range(2)]
    cond, cond_x = sb("cond", [P, KB, 2]), sb("cond_x", [P, KB, P])
    b_cols, g_cols, mod, b_gate = sb("b_cols", [P, 2 * KB]), sb("g_cols", [P, KB]), sb("mod", [P, 2 * KB, 2]), sb("b_gate", [P, DM])
    p_mod, p_gate = ps("mod", [P, 2 * KB, 2]), ps("gate", [P, DM])
    const_in, cond_ready, wide_ready, mod_ready, gate_ready = (
        sem(n) for n in ("const_in", "cond_ready", "wide_ready", "mod_ready", "gate_ready"))
    w_in, w_used = [sem(f"w{b}_in") for b in range(2)], [sem(f"w{b}_used") for b in range(2)]
    CHUNKS = 3 * DM // BANK
    PAIRS = CHUNKS // 2

    with nc.Block() as block:
        @block.sync
        def _(sp):
            def load(j, b):
                sp.dma_start(w[b][:], d["w_ada"].rearrange("(k p) c -> p k c", p=P)[:, :, bass.ds((2 * j + b) * BANK, BANK)])\
                    .then_inc(w_in[b], 16)

            for dst, src in ((cond, d["cond"]), (b_cols, d["b_ada_cols"]), (g_cols, d["norm_g2"])):
                sp.dma_start(dst[:], src).then_inc(const_in, 16)
            sp.dma_start(b_gate[:], d["b_ada_gate"].partition_broadcast(P)).then_inc(const_in, 16)
            for b in range(2):
                load(0, b)
            with sp.Fori(1, PAIRS) as j:
                for b in range(2):
                    sp.wait_ge(w_used[b], j)
                    load(j, b)

        @block.scalar
        def _(act):
            act.wait_ge(const_in, 64)
            nc.scalar.activation(cond[:], cond[:], ACT.Silu).then_inc(cond_ready, 1)

        @block.tensor
        def _(pe):
            pe.wait_ge(cond_ready, 1)
            with pe.Fori(0, PAIRS - 1) as j:
                for b in range(2):
                    pe.wait_ge(w_in[b], 16 * (j + 1))
                    for n in range(BANK // P):
                        for k in range(KB):
                            last = nc.tensor.matmul(
                                p_mod[:, bass.ds((2 * j + b) * (BANK // P) + n, 1), :].rearrange("p a c -> p (a c)"),
                                w[b][:, k, n * P:(n + 1) * P], cond[:, k, :], start=(k == 0), stop=(k == KB - 1))
                    last.then_inc(w_used[b], 1)
            pe.drain().then_inc(mod_ready, 1)
            pe.wait_ge(wide_ready, 1)
            for b in range(2):
                pe.wait_ge(w_in[b], 16 * PAIRS)
                for k in range(KB):
                    last = nc.tensor.matmul(p_gate[:, b * BANK:(b + 1) * BANK], cond_x[:, k, :], w[b][:, k, :],
                                            start=(k == 0), stop=(k == KB - 1))
            last.then_inc(gate_ready, 1)

        @block.vector
        def _(dve):
            dve.wait_ge(const_in, 64)
            dve.wait_ge(cond_ready, 1)
            nc.vector.tensor_copy(cond_x[:], cond[:, :, 0:1].to_broadcast([P, KB, P])).then_inc(wide_ready, 1)
            dve.wait_ge(mod_ready, 1)
            nc.vector.tensor_tensor(mod[:], p_mod[:], along(b_cols[:], 2), ALU.add)
            dve.drain()
            for i, (scale, shift) in enumerate(((g.scale_x, g.shift_x), (g.scale_c, g.shift_c))):
                nc.vector.tensor_copy(shift[:], mod[:, 0:KB, i])
                nc.vector.scalar_tensor_tensor(scale[:], mod[:, KB:2 * KB, i], 1.0, g_cols[:], ALU.add, ALU.mult)
            dve.wait_ge(gate_ready, 1)
            nc.vector.tensor_tensor(g.gate_x[:], p_gate[:], b_gate[:], ALU.add)
            dve.drain()
    ph.close()


def rel_phase(nc, d, g):
    ph = Phase(nc, "rel")
    sb, ps, sem = ph.sb, ph.ps, ph.sem
    R = 33
    HR = H2 * REL_R
    rel, hot, out = sb("rel", [R, HR]), sb("hot", [R, GRID_W, GRID_W]), sb("out", [HR, GRID_W * GRID_W])
    p_out = ps("out", [P, 8, BANK])
    zeroed, rel_in, hot_ready, out_ready, copied, stored = (
        sem(n) for n in ("zeroed", "rel_in", "hot_ready", "out_ready", "copied", "stored"))
    low, high = WIN_C // 2, GRID_W - WIN_C // 2

    with nc.Block() as block:
        @block.sync
        def _(sp):
            sp.wait_ge(zeroed, 1)
            sp.dma_start(rel[0:REL_C, :], d["rel_bias"]).then_inc(rel_in, 16)
            sp.wait_ge(copied, 1)
            sp.dma_start(d["rel_table"], out[:]).then_inc(stored, 16)
            sp.wait_ge(stored, 16)

        @block.gpsimd
        def _(pool):
            nc.gpsimd.memset(rel[0:32, :], 0.0)
            pool.drain()
            nc.gpsimd.memset(rel[32:33, :], MASKED)
            pool.drain()
            nc.gpsimd.memset(hot[:], 0.0)
            pool.drain().then_inc(zeroed, 1)
            nc.gpsimd.affine_select(out=hot[0:32], in_=hot[0:32], compare_op=ALU.not_equal, fill=1.0, base=WIN_C - 1,
                                    pattern=[[-1, GRID_W], [1, GRID_W]], channel_multiplier=-1)
            pool.drain()
            far = hot[32:33]
            nc.gpsimd.memset(far[:, 0:low, WIN_C:], 1.0)
            pool.drain()
            nc.gpsimd.memset(far[:, high:, 0:GRID_W - WIN_C], 1.0)
            pool.drain()
            mid = far[:, low:high, :]
            for sign in (1, -1):
                nc.gpsimd.affine_select(out=mid, in_=mid, compare_op=ALU.is_ge, fill=1.0,
                                        base=0 if sign > 0 else WIN_C - 1,
                                        pattern=[[-sign, high - low], [sign, GRID_W]], channel_multiplier=0)
                pool.drain()
            pool.drain().then_inc(hot_ready, 1)

        @block.tensor
        def _(pe):
            pe.wait_ge(rel_in, 16)
            pe.wait_ge(hot_ready, 1)
            flat = hot[:].rearrange("p q k -> p (q k)")
            for n in range(8):
                last = nc.tensor.matmul(p_out[0:HR, n, :], rel[:], flat[:, n * BANK:(n + 1) * BANK], start=True, stop=True)
            last.then_inc(out_ready, 1)

        @block.scalar
        def _(act):
            act.wait_ge(out_ready, 1)
            nc.scalar.activation(out[:], p_out[0:HR].rearrange("p n c -> p (n c)"), ACT.Copy).then_inc(copied, 1)
    ph.close()


def tile_pass_2(nc, d, g, x2T):
    ph = Phase(nc, "p2")
    sb, ps, sem = ph.sb, ph.ps, ph.sem
    MB = 5 * GW // P
    NQ = 2 * H2
    w_out, w_tok = sb("w_out", [P, MB, DM]), sb("w_tok", [P, KB, 3 * D2])
    y, z, x = sb("y", [P, MB * P]), sb("z", [P, MB, P]), sb("x", [P, DM])
    mix, x1, xs, slot = sb("mix", [P, MB, P]), sb("x1", [P, DM]), sb("xs", [P, DM]), sb("slot", [P, KB, P])
    x_sq, x_var, x_rstd = sb("x_sq", [P, 1]), sb("x_var", [P, 1]), sb("x_rstd", [P, 1])
    qk, qk2 = sb("qk", [P, 2 * D2]), sb("qk2", [P, 2 * D2])
    q_sq, q_var, q_rstd, gain = sb("q_sq", [P, NQ]), sb("q_var", [P, NQ]), sb("q_rstd", [P, NQ]), sb("gain", [P, 2, HD])
    v_out, qkT_out = sb("v_out", [P, D2]), sb("qkT_out", [P, KB, P])
    p_t, p_o = ps("t", [P, 12, P]), ps("o", [P, DM])
    p_proj = ps("proj", [P, 3, BANK])
    names = ("const_in", "y_in", "z_in", "x_in", "yT_ready", "mix_ready", "o_ready", "x1_ready", "x_sq_ready", "x_rstd_ready",
             "xs_ready", "xT_ready", "slot_ready", "x2T_copied", "proj_ready", "qk_ready", "v_ready", "q2_ready", "q_sq_ready",
             "q_rstd_ready", "qkn_ready", "qkT_ready", "qkT_out_ready", "x1_stored", "v_stored", "qkT_stored", "qkT_free")
    (const_in, y_in, z_in, x_in, yT_ready, mix_ready, o_ready, x1_ready, x_sq_ready, x_rstd_ready, xs_ready, xT_ready,
     slot_ready, x2T_copied, proj_ready, qk_ready, v_ready, q2_ready, q_sq_ready, q_rstd_ready, qkn_ready, qkT_ready,
     qkT_out_ready, x1_stored, v_stored, qkT_stored, qkT_free) = (sem(n) for n in names)
    N_CONST = 4

    with nc.Block() as block:
        @block.sync
        def _(sp):
            def load(i, first=False):
                if not first:
                    sp.wait_ge(mix_ready, i)
                sp.dma_start(y[:], tile_of(d["y1"], i)).then_inc(y_in, 16)
                sp.dma_start(z[:], cols_of(d["z1T"], i)).then_inc(z_in, 16)
                if not first:
                    sp.wait_ge(x1_ready, i)
                sp.dma_start(x[:], tile_of(d["x"], i)).then_inc(x_in, 16)

            def store_x1(i):
                sp.wait_ge(x1_ready, i + 1)
                sp.dma_start(tile_of(d["x1"], i), x1[:]).then_inc(x1_stored, 16)

            def store_qkv(i):
                sp.wait_ge(v_ready, i + 1)
                sp.wait_ge(qkT_out_ready, i + 1)
                sp.dma_start(tile_of(d["v2"], i), v_out[:]).then_inc(v_stored, 16)
                sp.dma_start(cols_of(d["qk2T"], i), qkT_out[:]).then_inc(qkT_stored, 16)

            for s in (x1_stored, v_stored, qkT_stored):
                sp.sem_inc(s, 16)
            load(0, first=True)
            sp.dma_start(w_out[:], d["w_out1"].rearrange("(k p) c -> p k c", p=P)).then_inc(const_in, 16)
            sp.dma_start(w_tok[:], d["w_tok2"].rearrange("(k p) c -> p k c", p=P)).then_inc(const_in, 16)
            for n, src in enumerate((d["q_norm_g2"], d["k_norm_g2"])):
                sp.dma_start(gain[:, n, :], src.partition_broadcast(P)).then_inc(const_in, 16)
            load(1)
            store_x1(0)
            with sp.Fori(2, NT) as i:
                load(i)
                store_x1(i - 1)
                store_qkv(i - 2)
            store_x1(NT - 1)
            store_qkv(NT - 2)
            store_qkv(NT - 1)
            for s in (x1_stored, v_stored, qkT_stored):
                sp.wait_ge(s, 16 * (NT + 1))

        @block.tensor
        def _(pe):
            def turn_y(i, first=False):
                pe.wait_ge(y_in, 16 * (i + 1))
                if not first:
                    pe.wait_ge(slot_ready, i)
                for k in range(MB):
                    last = nc.tensor.transpose(p_t[:, k, :], y[:, k * P:(k + 1) * P], g.ident[:])
                last.then_inc(yT_ready, 1)

            def out_project(i, first=False):
                pe.wait_ge(mix_ready, i + 1)
                if not first:
                    pe.wait_ge(x1_ready, i)
                for n in range(DM // BANK):
                    for k in range(MB):
                        last = nc.tensor.matmul(p_o[:, n * BANK:(n + 1) * BANK], mix[:, k, :],
                                                w_out[:, k, n * BANK:(n + 1) * BANK], start=(k == 0), stop=(k == MB - 1))
                last.then_inc(o_ready, 1)

            def turn_x(i):
                pe.wait_ge(xs_ready, i + 1)
                for k in range(KB):
                    last = nc.tensor.transpose(p_t[:, k, :], xs[:, k * P:(k + 1) * P], g.ident[:])
                last.then_inc(xT_ready, 1)

            def project(i):
                pe.wait_ge(slot_ready, i + 1)
                pe.wait_ge(qkT_free, i + 1)
                for n in range(3):
                    for k in range(KB):
                        last = nc.tensor.matmul(p_proj[:, n, :], slot[:, k, :], w_tok[:, k, n * D2:(n + 1) * D2],
                                                start=(k == 0), stop=(k == KB - 1))
                    last.then_inc(proj_ready, 1)

            def turn_qk(i):
                pe.wait_ge(qkn_ready, i + 1)
                for k in range(KB):
                    last = nc.tensor.transpose(p_proj[:, k // 4, (k % 4) * P:(k % 4 + 1) * P], qk[:, k * P:(k + 1) * P], g.ident[:])
                last.then_inc(qkT_ready, 1)

            pe.wait_ge(const_in, 16 * N_CONST)
            turn_y(0, first=True)
            out_project(0, first=True)
            turn_x(0)
            with pe.Fori(1, NT) as i:
                turn_y(i)
                project(i - 1)
                out_project(i)
                turn_qk(i - 1)
                turn_x(i)
            project(NT - 1)
            turn_qk(NT - 1)

        @block.scalar
        def _(act):
            def square(i):
                act.wait_ge(x1_ready, i + 1)
                nc.scalar.activation(xs[:], x1[:], ACT.Square, scale=DM ** -0.5, accum_out=x_sq[:]).then_inc(x_sq_ready, 1)

            def fill_slot(i):
                act.wait_ge(xT_ready, i + 1)
                act.wait_ge(x2T_copied, i + 1)
                for k in range(KB):
                    nc.scalar.activation(slot[:, k, :], p_t[:, k, :], ACT.Identity, scale=g.scale_x[:, k:k + 1],
                                         bias=g.shift_x[:, k:k + 1])
                act.drain().then_inc(slot_ready, 1)

            def evacuate(i):
                act.wait_ge(proj_ready, 3 * i + 2)
                act.wait_ge(qkT_free, i + 1)
                nc.scalar.activation(qk[:], p_proj[:, 0:2, :].rearrange("p n c -> p (n c)"), ACT.Copy).then_inc(qk_ready, 1)
                act.wait_ge(proj_ready, 3 * i + 3)
                act.wait_ge(v_stored, 16 * (i + 1))
                nc.scalar.activation(v_out[:], p_proj[:, 2, :], ACT.Copy).then_inc(v_ready, 1)

            square(0)
            fill_slot(0)
            with act.Fori(1, NT) as i:
                evacuate(i - 1)
                square(i)
                fill_slot(i)
            evacuate(NT - 1)

        @block.gpsimd
        def _(pool):
            def x_norm(i):
                pool.wait_ge(x_sq_ready, i + 1)
                nc.gpsimd.tensor_tensor(x_var[:], x_sq[:], g.eps[:], ALU.add)
                pool.drain()
                nc.gpsimd.tensor_tensor(x_rstd[:], x_var[:], g.neg_half[:], ALU.pow).then_inc(x_rstd_ready, 1)

            def tile(i):
                pool.wait_ge(slot_ready, i + 1)
                nc.gpsimd.tensor_copy(x2T[:, :, bass.ds(i * P, P)], slot[:]).then_inc(x2T_copied, 1)

            def head_norms(i):
                pool.wait_ge(qk_ready, i + 1)
                nc.gpsimd.tensor_tensor(qk2[:], qk[:], qk[:], ALU.mult).then_inc(q2_ready, 1)
                pool.wait_ge(q_sq_ready, i + 1)
                nc.gpsimd.tensor_tensor(q_var[:], q_sq[:], g.head_eps[:].to_broadcast([P, NQ]), ALU.add)
                pool.drain()
                nc.gpsimd.tensor_tensor(q_rstd[:], q_var[:], g.neg_half[:].to_broadcast([P, NQ]), ALU.pow)\
                    .then_inc(q_rstd_ready, 1)

            pool.sem_inc(x2T_copied, 1)
            x_norm(0)
            tile(0)
            with pool.Fori(1, NT) as i:
                head_norms(i - 1)
                x_norm(i)
                tile(i)
            head_norms(NT - 1)

        @block.vector
        def _(dve):
            def gate(i):
                dve.wait_ge(yT_ready, i + 1)
                dve.wait_ge(z_in, 16 * (i + 1))
                nc.vector.tensor_tensor(mix[:], p_t[:, 0:MB, :], z[:], ALU.mult).then_inc(mix_ready, 1)

            def residual(i):
                dve.wait_ge(o_ready, i + 1)
                dve.wait_ge(x_in, 16 * (i + 1))
                dve.wait_ge(x1_stored, 16 * (i + 1))
                nc.vector.tensor_tensor(x1[:], p_o[:], x[:], ALU.add).then_inc(x1_ready, 1)
                dve.wait_ge(x_rstd_ready, i + 1)
                nc.vector.tensor_scalar(xs[:], x1[:], x_rstd[:], None, ALU.mult).then_inc(xs_ready, 1)

            def norms(i):
                dve.wait_ge(q2_ready, i + 1)
                nc.vector.tensor_reduce(q_sq[:], heads(qk2[:]), AX.X, ALU.add).then_inc(q_sq_ready, 1)
                dve.wait_ge(q_rstd_ready, i + 1)
                nc.vector.tensor_tensor(heads(qk2[:]), heads(qk[:]), along(q_rstd[:], HD), ALU.mult)
                dve.drain()
                for n in range(2):
                    cs = slice(n * D2, (n + 1) * D2)
                    nc.vector.tensor_tensor(heads(qk[:, cs]), heads(qk2[:, cs]), gain[:, n:n + 1, :].to_broadcast([P, H2, HD]),
                                            ALU.mult)
                dve.drain().then_inc(qkn_ready, 1)

            def copy_heads(i):
                dve.wait_ge(qkT_ready, i + 1)
                dve.wait_ge(qkT_stored, 16 * (i + 1))
                nc.vector.tensor_copy(qkT_out[:], p_proj[:, 0:2, :].rearrange("p n (j t) -> p (n j) t", t=P))\
                    .then_inc(qkT_free, 1)
                dve.drain().then_inc(qkT_out_ready, 1)

            dve.wait_ge(const_in, 16 * N_CONST)
            nc.vector.tensor_scalar(gain[:, 1, :], gain[:, 1, :], HD ** 0.5, None, ALU.mult)
            dve.drain().then_inc(qkT_free, 1)
            gate(0)
            residual(0)
            with dve.Fori(1, NT) as i:
                gate(i)
                norms(i - 1)
                residual(i)
                copy_heads(i - 1)
            norms(NT - 1)
            copy_heads(NT - 1)
    ph.close()


def feature_pass_2(nc, d, g, x2T):
    ph = Phase(nc, "f2")
    sb, ps, sem = ph.sb, ph.ps, ph.sem
    w = [sb(f"w{b}", [P, KB, P]) for b in range(2)]
    out = [sb(f"out{b}", [P, T]) for b in range(2)]
    p_out = [ps(f"out{b}", [P, T]) for b in range(2)]
    w_in, p_ready, p_free, out_ready, stored = ([sem(f"{n}{b}") for b in range(2)]
                                                for n in ("w_in", "p_ready", "p_free", "out_ready", "stored"))
    IN_PAIRS, PAIRS = D2 // P // 2, 3 * D2 // P // 2

    with nc.Block() as block:
        @block.sync
        def _(sp):
            def load(j, b):
                sp.dma_start(w[b][:].rearrange("p k c -> p (k c)"),
                             d["w_fm2"][bass.ds(2 * j + b, 1)].rearrange("a p c -> (a p) c")).then_inc(w_in[b], 16)

            def turn(j, dst, first, more=True):
                for b in range(2):
                    if more:
                        sp.wait_ge(p_ready[b], j + 1)
                        load(j + 1, b)
                    sp.wait_ge(out_ready[b], j + 1)
                    sp.dma_start(dst[bass.ds((2 * (j - first) + b) * P, P), :], out[b][:]).then_inc(stored[b], 16)

            for b in range(2):
                sp.sem_inc(stored[b], 16)
                load(0, b)
            with sp.Fori(0, IN_PAIRS) as j:
                turn(j, d["f_inT"], 0)
            with sp.Fori(IN_PAIRS, PAIRS - 1) as j:
                turn(j, d["z2T"], IN_PAIRS)
            turn(PAIRS - 1, d["z2T"], IN_PAIRS, more=False)
            for b in range(2):
                sp.wait_ge(stored[b], 16 * (PAIRS + 1))

        @block.tensor
        def _(pe):
            with pe.Fori(0, PAIRS) as j:
                for b in range(2):
                    pe.wait_ge(w_in[b], 16 * (j + 1))
                    pe.wait_ge(p_free[b], j + 1)
                    for n in range(T // BANK):
                        for k in range(KB):
                            last = nc.tensor.matmul(p_out[b][:, n * BANK:(n + 1) * BANK], w[b][:, k, :],
                                                    x2T[:, k, n * BANK:(n + 1) * BANK], start=(k == 0), stop=(k == KB - 1))
                    last.then_inc(p_ready[b], 1)

        @block.scalar
        def _(act):
            for b in range(2):
                act.sem_inc(p_free[b], 1)
            for first, end, func in ((0, IN_PAIRS, ACT.Copy), (IN_PAIRS, PAIRS, ACT.Silu)):
                with act.Fori(first, end) as j:
                    for b in range(2):
                        act.wait_ge(p_ready[b], j + 1)
                        act.wait_ge(stored[b], 16 * (j + 1))
                        nc.scalar.activation(out[b][:], p_out[b][:], func).then_inc(out_ready[b], 1)
                        act.drain().then_inc(p_free[b], 1)
    ph.close()


RADIX = 4
TF = T // RADIX
NF_T = TF // P
FG = 4
FK = D2 // P


def fourier(nc, d, g):
    ph = Phase(nc, "four")
    sb, ps, sem = ph.sb, ph.ps, ph.sem
    u = sb("u", [P, FK, T])
    ch = sb("ch", [P, 2, P])
    w4, wcs = sb("w4", [P, FK, D2]), sb("wcs", [P, 2, FK, D2])
    e0, e1 = sb("e0", [P, FK, P]), sb("e1", [P, FK, P])
    fold = sb("fold", [P, 4, FK, P])
    d1w = sb("d1w", [P, 2, D2])
    zz = sb("zz", [P, NF_T, RADIX, 2, D2])
    cs = [sb(f"cs{b}", [P, NF_T, 2, P]) for b in range(2)]
    out = [sb(f"out{b}", [P, D2]) for b in range(2)]
    p_b = [ps(f"b{n}", [P, BANK]) for n in range(8)]
    names = ("const_in", "u_in", "w_ready", "w_copied", "fold_ready", "f_ready", "s_copied", "d1_copied", "d_done", "y_ready",
             "y_out")
    const_in, u_in, w_ready, w_copied, fold_ready, f_ready, s_copied, d1_copied, d_done, y_ready, y_out = (sem(n) for n in names)
    cs_in, out_ready, stored = ([sem(f"{n}{b}") for b in range(2)] for n in ("cs_in", "out_ready", "stored"))

    with nc.Block() as block:
        @block.sync
        def _(sp):
            sp.dma_start(ch[:], d["dft_channels"]).then_inc(const_in, 16)
            sp.dma_start(w4[:], d["w_four"].rearrange("(k p) c -> p k c", p=P)).then_inc(const_in, 16)
            sp.dma_start(u[:], d["f_inT"].rearrange("(k p) t -> p k t", p=P)).then_inc(u_in, 16)
            for b in range(2):
                sp.sem_inc(stored[b], 16)

            def load(j, m):
                sp.dma_start(cs[m % 2][:].rearrange("p n s m -> p (n s m)"),
                             d["dft_tokens"][bass.ds(j * NF_T + m, 1)].rearrange("a p c -> (a p) c")).then_inc(cs_in[m % 2], 16)

            load(0, 0)
            load(0, 1)

            def turn(j, m, more):
                if more:
                    sp.wait_ge(y_ready, NF_T * j + m + 1)
                    load(j + (m + 2) // NF_T, (m + 2) % NF_T)
                sp.wait_ge(out_ready[m % 2], NF_T // 2 * j + m // 2 + 1)
                sp.dma_start(d["y2"].rearrange("(m j) c -> j m c", j=RADIX)[bass.ds(j, 1), m * P:(m + 1) * P, 0:D2]
                             .rearrange("a m c -> (a m) c"), out[m % 2][:]).then_inc(stored[m % 2], 16)

            with sp.Fori(0, RADIX - 1) as j:
                for m in range(NF_T):
                    turn(j, m, True)
            for m in range(NF_T):
                turn(RADIX - 1, m, m + 2 < NF_T)
            for b in range(2):
                sp.wait_ge(stored[b], 16 * (RADIX * NF_T // 2 + 1))

        @block.tensor
        def _(pe):
            pe.wait_ge(const_in, 32)
            for i in range(2):
                for k in range(FK):
                    last = nc.tensor.matmul(p_b[i * FK + k][:], ch[:, i, :], w4[:, k, :], start=True, stop=True)
            last.then_inc(w_ready, 1)
            pe.wait_ge(w_copied, 1)

            def fold_products(n):
                pe.wait_ge(fold_ready, n + 1)
                pe.wait_ge(d_done, n + 1)
                for f in range(4):
                    for i in range(2):
                        for k in range(FK):
                            last = nc.tensor.matmul(p_b[2 * f + i][:], fold[:, f, k, :], wcs[:, i, k, :],
                                                    start=(k == 0), stop=(k == FK - 1))
                        last.then_inc(f_ready, 1)

            with pe.Fori(0, NF_T) as n:
                fold_products(n)
            pe.wait_ge(s_copied, NF_T)
            pe.wait_ge(d_done, NF_T + 1)
            with pe.Fori(0, RADIX) as j:
                for m in range(NF_T):
                    pe.wait_ge(cs_in[m % 2], 16 * (NF_T // 2 * j + m // 2 + 1))
                    pe.wait_ge(y_out, NF_T * j + m + 1)
                    for n in range(NF_T):
                        for i in range(2):
                            last = nc.tensor.matmul(p_b[m % 2][:], cs[m % 2][:, n, i, :],
                                                    zz[:, n, bass.ds(j, 1), i, :].rearrange("p a c -> p (a c)"),
                                                    start=(n == 0 and i == 0), stop=(n == NF_T - 1 and i == 1))
                    last.then_inc(y_ready, 1)

        @block.scalar
        def _(act):
            act.wait_ge(w_ready, 1)
            for i in range(2):
                for k in range(FK):
                    nc.scalar.activation(wcs[:, i, k, :], p_b[i * FK + k][:], ACT.Copy)
            act.drain().then_inc(w_copied, 1)
            with act.Fori(0, NF_T) as n:
                for f in range(2):
                    for i in range(2):
                        act.wait_ge(f_ready, 8 * n + 2 * f + i + 1)
                        nc.scalar.activation(zz[:, bass.ds(n, 1), 2 * f, i, :].rearrange("p a c -> p (a c)"), p_b[2 * f + i][:], ACT.Copy)
                act.drain().then_inc(s_copied, 1)
                act.wait_ge(f_ready, 8 * (n + 1))
                act.wait_ge(d_done, n + 1)
                for i in range(2):
                    nc.scalar.activation(d1w[:, i, :], p_b[6 + i][:], ACT.Copy)
                act.drain().then_inc(d1_copied, 1)
            act.sem_inc(y_out, 2)
            with act.Fori(0, RADIX) as j:
                for m in range(NF_T):
                    act.wait_ge(y_ready, NF_T * j + m + 1)
                    act.wait_ge(stored[m % 2], 16 * (NF_T // 2 * j + m // 2 + 1))
                    nc.scalar.activation(out[m % 2][:], p_b[m % 2][:], ACT.Copy).then_inc(out_ready[m % 2], 1)
                    act.drain().then_inc(y_out, 1)

        @block.vector
        def _(dve):
            dve.wait_ge(u_in, 16)
            dve.sem_inc(d_done, 1)
            with dve.Fori(0, NF_T) as n:
                q = [u[:, :, bass.ds(i * TF + n * P, P)] for i in range(RADIX)]
                nc.vector.tensor_tensor(e0[:], q[0], q[2], ALU.add)
                nc.vector.tensor_tensor(e1[:], q[1], q[3], ALU.add)
                nc.vector.tensor_tensor(fold[:, 2], q[0], q[2], ALU.subtract)
                nc.vector.tensor_tensor(fold[:, 3], q[1], q[3], ALU.subtract)
                dve.drain()
                nc.vector.tensor_tensor(fold[:, 0], e0[:], e1[:], ALU.add)
                nc.vector.tensor_tensor(fold[:, 1], e0[:], e1[:], ALU.subtract)
                dve.drain().then_inc(fold_ready, 1)
                dve.wait_ge(d1_copied, n + 1)
                for residue, at_c, at_s in ((1, ALU.subtract, ALU.add), (3, ALU.add, ALU.subtract)):
                    for i, op in enumerate((at_c, at_s)):
                        nc.vector.tensor_tensor(zz[:, bass.ds(n, 1), residue, i, :].rearrange("p a c -> p (a c)"), p_b[4 + i][:],
                                                d1w[:, 1 - i, :], op)
                dve.drain().then_inc(d_done, 1)
    ph.close()


def neighbourhood(nc, d, g):
    ph = Phase(nc, "nbr")
    SPAN = 10
    EDGE = REL_R - 1
    kT, v = ph.sb("kT", [HD, H2, TK2]), ph.sb("v", [P, TK2 // P, D2])
    inner, edge = ph.sb("inner", [P, H2, SPAN, GRID_W]), ph.sb("edge", [P, H2, EDGE, GRID_W])
    blank = ph.sem("blank")
    first_inner, last_inner = 2, NT - 3
    win = WIN_R * GRID_W // P

    def key_cols(u):
        if u < first_inner:
            local = range(win)
        elif u > last_inner:
            local = range(NT - win, NT)
        else:
            local = range(u - 2, u - 2 + SPAN * GRID_W // P)
        return [(b * P, b) for b in [*local, *range(NT, TK2 // P)]]

    def load(sp, const_in):
        sp.dma_start(kT[:, :, 0:T], d["qk2T"][D2:2 * D2].rearrange("(h e) t -> e h t", e=HD)).then_inc(const_in, 16)
        sp.dma_start(kT[:, :, T:TK2], d["ctx_kT"].rearrange("(h e) t -> e h t", e=HD)).then_inc(const_in, 16)
        sp.dma_start(v[:, 0:NT, :], d["v2"].rearrange("(n p) c -> p n c", p=P)).then_inc(const_in, 16)
        sp.dma_start(v[:, NT:, :], d["ctx_v"].rearrange("(n p) c -> p n c", p=P)).then_inc(const_in, 16)
        table = d["rel_table"].rearrange("(h r) (q k) -> q h r k", r=REL_R, k=GRID_W)
        sp.wait_ge(blank, 1)
        for e in range(2):
            at = slice(e * GRID_W, (e + 1) * GRID_W)
            for h in range(H2):
                sp.dma_start(inner[at, h, e:e + WIN_R, :], table[:, h, 3:3 + WIN_R, :]).then_inc(const_in, 16)
                sp.dma_start(edge[at, h, :, :], table[:, h, 1 - e:1 - e + EDGE, :]).then_inc(const_in, 16)

    def blanks(pool, const_in):
        nc.gpsimd.memset(inner[:], MASKED).then_inc(blank, 1)

    def load_q(sp, h, s, q, q_in):
        sp.dma_start(q[:], d["qk2T"][bass.ds(h * HD, HD), s * HALF * P:(s + 1) * HALF * P]).then_inc(q_in, 16)

    def bias(dve, h, u, s):
        if first_inner <= u <= last_inner:
            n, table = SPAN * GRID_W, inner[:, bass.ds(h, 1)]
        else:
            top = 0 if u < first_inner else 2 * NT - WIN_R
            j = top - 2 * u + WIN_R - 1 - 1
            n, table = WIN_R * GRID_W, edge[:, bass.ds(h, 1), j:j + WIN_R, :]
        nc.vector.tensor_tensor(s[:, 0:n], s[:, 0:n], table.rearrange("p a r k -> p (a r k)"), ALU.add)

    attention(nc, d, g, ph, H2, HD, kT, v, load, load_q, 1, key_cols, 16 * (4 + 4 * H2), head_tiles(d["y2"], D2), 2, 2 * BANK,
              bias, blanks)


def final_pass(nc, d, g):
    ph = Phase(nc, "fin")
    sb, ps, sem = ph.sb, ph.ps, ph.sem
    w = sb("w", [P, KB, DM])
    y, z, x1, mix, out = ([sb(f"{n}{b}", shape) for b in range(2)] for n, shape in
                          (("y", [P, DM]), ("z", [P, KB, P]), ("x1", [P, DM]), ("mix", [P, KB, P]), ("out", [P, DM])))
    scaled = [sb(f"scaled{b}", [P, DM]) for b in range(2)]
    p_t = [ps(f"t{b}", [P, KB, P]) for b in range(2)]
    p_o = [ps(f"o{b}", [P, DM]) for b in range(2)]
    const_in = sem("const_in")
    in_, t_ready, mix_ready, o_ready, out_ready, stored = ([sem(f"{n}{b}") for b in range(2)] for n in (
        "in", "t_ready", "mix_ready", "o_ready", "out_ready", "stored"))
    PAIRS = NT // 2

    with nc.Block() as block:
        @block.sync
        def _(sp):
            def load(j, b):
                i = 2 * j + b
                sp.dma_start(y[b][:], tile_of(d["y2"], i)).then_inc(in_[b], 16)
                sp.dma_start(z[b][:], cols_of(d["z2T"], i)).then_inc(in_[b], 16)
                sp.dma_start(x1[b][:], tile_of(d["x1"], i)).then_inc(in_[b], 16)

            def store(j, b):
                sp.wait_ge(out_ready[b], j + 1)
                sp.dma_start(tile_of(d["out"], 2 * j + b), out[b][:]).then_inc(stored[b], 16)

            sp.dma_start(w[:], d["w_out2"].rearrange("(k p) c -> p k c", p=P)).then_inc(const_in, 16)
            for b in range(2):
                sp.sem_inc(stored[b], 16)
                load(0, b)
            with sp.Fori(0, PAIRS - 1) as j:
                for b in range(2):
                    store(j, b)
                    load(j + 1, b)
            for b in range(2):
                store(PAIRS - 1, b)
            for b in range(2):
                sp.wait_ge(stored[b], 16 * (PAIRS + 1))

        @block.tensor
        def _(pe):
            pe.wait_ge(const_in, 16)

            def turn(j, b):
                pe.wait_ge(in_[b], 48 * (j + 1))
                for k in range(KB):
                    last = nc.tensor.transpose(p_t[b][:, k, :], y[b][:, k * P:(k + 1) * P], g.ident[:])
                last.then_inc(t_ready[b], 1)

            def project(j, b):
                pe.wait_ge(mix_ready[b], j + 1)
                for n in range(DM // BANK):
                    for k in range(KB):
                        last = nc.tensor.matmul(p_o[b][:, n * BANK:(n + 1) * BANK], mix[b][:, k, :],
                                                w[:, k, n * BANK:(n + 1) * BANK], start=(k == 0), stop=(k == KB - 1))
                last.then_inc(o_ready[b], 1)

            turn(0, 0)
            with pe.Fori(0, PAIRS - 1) as j:
                turn(j, 1)
                project(j, 0)
                turn(j + 1, 0)
                project(j, 1)
            turn(PAIRS - 1, 1)
            project(PAIRS - 1, 0)
            project(PAIRS - 1, 1)

        @block.vector
        def _(dve):
            def gate(j, b):
                dve.wait_ge(t_ready[b], j + 1)
                nc.vector.tensor_tensor(mix[b][:], p_t[b][:], z[b][:], ALU.mult).then_inc(mix_ready[b], 1)

            def residual(j, b):
                dve.wait_ge(o_ready[b], j + 1)
                nc.vector.tensor_tensor(scaled[b][:], p_o[b][:], g.gate_x[:], ALU.mult)
                dve.drain()
                dve.wait_ge(stored[b], 16 * (j + 1))
                nc.vector.tensor_tensor(out[b][:], scaled[b][:], x1[b][:], ALU.add).then_inc(out_ready[b], 1)

            gate(0, 0)
            with dve.Fori(0, PAIRS - 1) as j:
                gate(j, 1)
                residual(j, 0)
                gate(j + 1, 0)
                residual(j, 1)
            gate(PAIRS - 1, 1)
            residual(PAIRS - 1, 0)
            residual(PAIRS - 1, 1)
    ph.close()


SCRATCH = {
    "y1": (T, 5 * GW),
    "z1T": (5 * GW, T),
    "qkmT": (3 * GW, T),
    "fox_v": (T, GW),
    "mlstm_vo": (T, 2 * GW),
    "mlstm_qkT": (2 * GW, T),
    "rwkv_T": (3 * GW, T),
    "fox_rows": (2 * GH, 2, T),
    "mlstm_rows": (4 * GH, T),
    "mlstm_max": (GH, T),
    "mlstm_carry": (GH, NT),
    "mem_kT": (GW, NMEM),
    "mem_v": (NMEM, GW),
    "lowT": (P, T),
    "x1": (T, DM),
    "rel_table": (H2 * REL_R, GRID_W * GRID_W),
    "qk2T": (2 * D2, T),
    "v2": (T, D2),
    "f_inT": (D2, T),
    "z2T": (2 * D2, T),
    "y2": (T, DM),
    "ctx_kT": (D2, NMEM),
    "ctx_v": (NMEM, D2),
}


class OnChip:
    pass


def build(nc, arrays, phases):
    scratch = {n: nc.dram_tensor(f"scratch_{n}", shape, F32, kind="Internal").ap() for n, shape in SCRATCH.items()}
    d, g = {**arrays, **scratch}, OnChip()
    with ExitStack() as ctx:
        def sb(name, shape):
            return ctx.enter_context(nc.sbuf_tensor(name, shape, F32))

        g.ident = sb("ident", [P, P])
        g.neg_half, g.eps, g.head_eps, g.one = (sb(n, [P, 1]) for n in ("neg_half", "eps", "head_eps", "one"))
        g.scale_x, g.shift_x, g.scale_c, g.shift_c = (sb(n, [P, KB]) for n in ("scale_x", "shift_x", "scale_c", "shift_c"))
        g.gate_x = sb("gate_x", [P, DM])
        phases(nc, d, g, sb)


def all_phases(nc, d, g, sb):
    consts_phase(nc, g)
    ada_phase(nc, d, g)
    rel_phase(nc, d, g)
    keys_values(nc, d, g, "ctxkv", d["ctx"], d["ctx_w_kv"], H2, d["ctx_k_g"], g.scale_c, g.shift_c, d["ctx_kT"], d["ctx_v"])
    with nc.sbuf_tensor("hT", [P, KB, T], F32) as hT:
        tile_pass_1(nc, d, g, hT)
        feature_pass_1(nc, d, g, hT)
    gates_phase(nc, d, g)
    with nc.sbuf_tensor("mem_scale", [P, KB], F32) as mem_scale, nc.semaphore("mem_scale_in") as mem_scale_in:
        nc.sync.dma_start(mem_scale[:], d["mem_norm_g"]).then_inc(mem_scale_in, 16)
        nc.scalar.wait_ge(mem_scale_in, 16)
        keys_values(nc, d, g, "memkv", d["mem"], d["mem_w_kv"], GH, d["mem_k_g"], mem_scale, None, d["mem_kT"], d["mem_v"])
        nc.sync.sem_clear(mem_scale_in)
    fox_attention(nc, d, g)
    mlstm(nc, d, g)
    rwkv(nc, d, g)
    mem_attention(nc, d, g)
    with nc.sbuf_tensor("x2T", [P, KB, T], F32) as x2T:
        tile_pass_2(nc, d, g, x2T)
        feature_pass_2(nc, d, g, x2T)
    fourier(nc, d, g)
    neighbourhood(nc, d, g)
    final_pass(nc, d, g)


PHASES = all_phases


def kernel(**inputs):
    import concourse.bacc as bacc
    from concourse.bass_utils import run_bass_kernel_spmd

    a = {n: np.asarray(v) for n, v in inputs.items()}
    at = {}
    col = 0
    for name, width in (("au", GW), ("av", GW), ("az", GW), ("bq", GW), ("bk", GW), ("bv", GW), ("bf", GH), ("bz", GW),
                        ("cq", GW), ("ck", GW), ("cv", GW), ("ci", GH), ("cf", GH), ("co", GW), ("cz", GW),
                        ("dr", GW), ("dw", 16), ("dk", GW), ("dv", GW), ("da", 16), ("dz", GW), ("mq", GW), ("mz", GW)):
        at[name] = slice(col, col + width)
        col += width
    w_in = a["w_in"][0]

    def columns(*names):
        return np.concatenate([w_in[:, at[n]] for n in names], axis=1)

    def blocks(w):
        k, c = w.shape[0] // P, w.shape[1] // P
        return w.reshape(k, P, c, P).transpose(2, 1, 0, 3).reshape(c, P, k * P)

    low = np.zeros((DM, P), np.float32)
    for first, name in ((0, "dw"), (32, "da"), (64, "bf"), (68, "ci"), (72, "cf")):
        n = at[name].stop - at[name].start
        low[:, first:first + n] = w_in[:, at[name]]

    def col_blocks(v):
        return v.reshape(-1, P).T

    def row(*vs):
        return np.concatenate(vs)

    w_out = a["w_out"][0]
    w_in_2 = a["w_in_2"][0]
    b_ada = a["b_ada_2"][0]
    channel = np.arange(P)
    angle_c = 2 * np.pi / P * np.outer(channel, channel)
    token, position = np.arange(TF), np.arange(T)
    angle_t = 2 * np.pi / T * (np.outer(token, position) % T)
    waves = np.stack([np.cos(angle_t), -np.sin(angle_t)]) * (T * P) ** -0.5
    waves = waves.reshape(2, NF_T, P, NF_T, P, RADIX).transpose(5, 3, 2, 1, 0, 4)

    arrays = {
        "x": a["x"][0],
        "norm_g": a["norm_g"][0],
        "w_tok1": columns("au", "av", "bq", "bk", "mq", "bv", "cv", "co"),
        "w_fm1": blocks(np.concatenate([columns("az", "bz", "cz", "mz", "cq", "ck", "dr", "dk", "dv", "dz"), low], 1)),
        "sgu_norm_g": a["sgu_norm_g"][0],
        "sgu_wT": a["sgu_w"][0].transpose(2, 0, 1),
        "sgu_b": a["sgu_b"][0].T,
        "conv_w": a["mlstm_conv_w"][0].reshape(4, 4, P).transpose(2, 1, 0),
        "conv_b": col_blocks(a["mlstm_conv_b"][0]),
        "rwkv_mu": col_blocks(row(*[a["rwkv_mu"][0][at[n].start - at["dr"].start:at[n].stop - at["dr"].start]
                                    for n in ("dr", "dk", "dv", "dz")])),
        "f_bias": row(a["fox_f_b"][0], a["mlstm_f_b"][0])[:, None],
        "i_bias": a["mlstm_i_b"][0][:, None],
        "mem": a["mem"][0],
        "mem_norm_g": col_blocks(a["mem_norm_g"][0]),
        "mem_w_kv": a["mem_w_kv"][0],
        "mem_k_g": row(*[a["mem_k_g"][0]] * GH),
        "mlstm_out_g": a["mlstm_out_g"][0],
        "rwkv_low_mu": np.stack([a["rwkv_mu"][0][at[n].start - at["dr"].start:at[n].stop - at["dr"].start]
                                 for n in ("dw", "da")], axis=1),
        "rwkv_up": np.stack([a["rwkv_w2"][0], a["rwkv_a2"][0]], axis=1),
        "rwkv_cols": np.stack([col_blocks(v) for v in (a["rwkv_w0"][0], a["rwkv_a0"][0], a["rwkv_k_k"][0],
                                                       a["rwkv_k_a"][0], a["rwkv_r_k"][0].reshape(-1))], axis=2),
        "rwkv_ln_g": a["rwkv_ln_g"][0],
        "qkm_g": row(*[a["fox_q_g"][0]] * GH, *[a["fox_k_g"][0]] * GH, *[a["mem_q_g"][0]] * GH),
        "w_out1": np.concatenate([w_out[n * GW:(n + 1) * GW] for n in (0, 1, 2, 4, 3)]),
        "cond": np.stack([col_blocks(a["c_2"][0]), col_blocks(a["c_ctx_2"])], axis=2),
        "w_ada": a["w_ada_2"][0],
        "b_ada_cols": col_blocks(b_ada[:2 * DM]),
        "b_ada_gate": b_ada[2 * DM:],
        "norm_g2": col_blocks(a["norm_g_2"][0]),
        "rel_bias": a["rel_bias_2"][0].reshape(-1, REL_C).T,
        "ctx": a["ctx_2"][0],
        "ctx_w_kv": w_in_2[:, 3 * D2:5 * D2],
        "ctx_k_g": row(*[a["k_norm_g_2"][0]] * H2),
        "w_tok2": w_in_2[:, 2 * D2:5 * D2],
        "q_norm_g2": a["q_norm_g_2"][0],
        "k_norm_g2": a["k_norm_g_2"][0],
        "w_fm2": blocks(np.concatenate([w_in_2[:, 0:2 * D2], w_in_2[:, 5 * D2:6 * D2]], 1)),
        "w_four": a["w_four_2"][0],
        "w_out2": a["w_out_2"][0],
        "dft_channels": np.stack([np.cos(angle_c), np.sin(angle_c)], axis=1).astype(np.float32),
        "dft_tokens": waves.reshape(RADIX * NF_T, P, NF_T * 2 * P).astype(np.float32),
    }
    arrays = {n: np.ascontiguousarray(v) for n, v in arrays.items()}
    nc = bacc.Bacc("TRN2", target_bir_lowering=False, num_devices=1)
    dram = {n: nc.dram_tensor(f"in_{n}", v.shape, F32, kind="ExternalInput").ap() for n, v in arrays.items()}
    dram["out"] = nc.dram_tensor("out", (T, DM), F32, kind="ExternalOutput").ap()
    build(nc, dram, PHASES)
    r = run_bass_kernel_spmd(nc, [{f"in_{n}": v for n, v in arrays.items()}], core_ids=[0])
    return r.results[0]["out"].reshape(1, T, DM)
```

```python
from contextlib import ExitStack

import numpy as np

import concourse.bass as bass
from concourse import mybir

F32 = mybir.dt.float32
F32R = mybir.dt.float32r
U32 = mybir.dt.uint32
ALU = mybir.AluOpType
ACT = mybir.ActivationFunctionType
AX = mybir.AxisListType

P = 128
T = 2048
NT = T // P
DM = 1024
KB = DM // P
HD = 64
GH = 4
GW = GH * HD
NMEM = 256
EPS = 1e-6
MASKED = -1e30
BANK = 512


PASSES = ((0, 0), (0, 1), (1, 0))


class Phase:

    def __init__(self, nc, name):
        self.nc, self.name, self.ctx, self.sems = nc, name, ExitStack(), []

    def sb(self, name, shape, dt=F32):
        return self.ctx.enter_context(self.nc.sbuf_tensor(f"{self.name}_{name}", shape, dt))

    def ps(self, name, shape, dt=F32):
        return self.ctx.enter_context(self.nc.psum_tensor(f"{self.name}_psum_{name}", shape, dt))

    def sem(self, name):
        s = self.ctx.enter_context(self.nc.semaphore(f"{self.name}_{name}"))
        self.sems.append(s)
        return s

    def close(self):
        for s in self.sems:
            self.nc.sync.sem_clear(s)
        self.nc.all_engine_barrier()
        self.ctx.close()


def along(column, n):
    return column.unsqueeze(2).to_broadcast([column.shape[0], column.shape[1], n])


def heads(ap, n=HD):
    return ap.rearrange("p (h d) -> p h d", d=n)


def raw(ap):
    return ap.bitcast(F32)


def split(nc, dve, high, low, src):
    nc.vector.tensor_copy(high, src)
    dve.drain()
    return nc.vector.tensor_tensor(low, src, high, ALU.subtract)


def same_head(nc, pool, ones):
    nc.gpsimd.memset(ones[:], 1.0)
    pool.drain()
    nc.gpsimd.affine_select(out=ones[:, 0:HD], in_=ones[:, 0:HD], compare_op=ALU.is_ge, fill=0.0, base=HD - 1,
                            pattern=[[0, HD]], channel_multiplier=-1)
    nc.gpsimd.affine_select(out=ones[:, HD:P], in_=ones[:, HD:P], compare_op=ALU.is_ge, fill=0.0, base=-HD,
                            pattern=[[0, HD]], channel_multiplier=1)


def wait_apart(eng, sem, value, taken):
    eng.wait_ge(sem, value)
    eng.sem_inc(taken, 1)


def tile_of(dram, i):
    return dram[bass.ds(i * P, P), :]


def cols_of(dram, i):
    return dram.rearrange("(b p) t -> p b t", p=P)[:, :, bass.ds(i * P, P)]


def consts_phase(nc, g):
    ph = Phase(nc, "const")
    ones_ready = ph.sem("ones_ready")
    with nc.Block() as block:
        @block.gpsimd
        def _(pool):
            nc.gpsimd.memset(g.ident[:], 0.0)
            pool.drain()
            nc.gpsimd.affine_select(out=g.ident[:], in_=g.ident[:], compare_op=ALU.not_equal, fill=1.0, base=0,
                                    pattern=[[-1, P]], channel_multiplier=1)
            nc.gpsimd.memset(g.neg_half[:], -0.5)
            nc.gpsimd.memset(g.eps[:], EPS)
            nc.gpsimd.memset(g.head_eps[:], HD * EPS)
            nc.gpsimd.memset(g.one[:], 1.0).then_inc(ones_ready, 1)
    ph.close()


def tile_pass_1(nc, d, g):
    ph = Phase(nc, "p1")
    sb, ps, sem = ph.sb, ph.ps, ph.sem
    NQ = 12
    w_parts = [sb(f"w_{part}", [P, KB, 4 * BANK], F32R) for part in ("high", "low")]
    staging = [sb(f"staging{b}", [P, 4 * BANK]) for b in range(2)]
    xt, junk, xs = sb("xt", [P, DM]), sb("junk", [P, DM]), sb("xs", [P, DM])
    norm_gain = sb("norm_gain", [P, DM])
    x_sq, x_var, x_rstd = sb("x_sq", [P, 1]), sb("x_var", [P, 1]), sb("x_rstd", [P, 1])
    h_slot = sb("h_slot", [P, KB, P])
    h_parts = [sb(f"h_{part}", [P, KB, P], F32R) for part in ("high", "low")]
    uv, vn, v2 = sb("uv", [P, 2 * GW]), sb("vn", [P, GW]), sb("v2", [P, GW])
    v_sq, v_var, v_rstd = sb("v_sq", [P, GH]), sb("v_var", [P, GH]), sb("v_rstd", [P, GH])
    sgu_gain, sgu_w, sgu_b = sb("sgu_gain", [P, GW]), sb("sgu_w", [P, GH, P]), sb("sgu_b", [P, GH])
    mixed, y_out = sb("mixed", [P, GW]), sb("y_out", [P, GW])
    qkm, qkm2 = sb("qkm", [P, NQ * HD]), sb("qkm2", [P, NQ * HD])
    q_sq, q_var, q_rstd = sb("q_sq", [P, NQ]), sb("q_var", [P, NQ]), sb("q_rstd", [P, NQ])
    qk_gain = sb("qk_gain", [P, NQ * HD])
    qkT_out = sb("qkT_out", [P, 2, NQ // 2, P], F32R)
    v_out, c_out = sb("v_out", [P, GW]), sb("c_out", [P, 2 * GW])
    p_xT = ps("xT", [P, KB, P])
    p_proj = [ps(f"proj{n}", [P, BANK]) for n in range(4)]
    p_mix, p_qkT = ps("mix", [P, BANK]), ps("qkT", [P, BANK // P, P])

    const_in, x_in = sem("const_in"), sem("x_in")
    gains_ready, w_masked = sem("gains_ready"), sem("w_masked")
    x_sq_ready, x_rstd_ready, xs_ready, xt_free = sem("x_sq_ready"), sem("x_rstd_ready"), sem("xs_ready"), sem("xt_free")
    xT_ready, h_high_ready, h_ready, h_free, hT_stored = (sem("xT_ready"), sem("h_high_ready"), sem("h_ready"), sem("h_free"),
                                                          sem("hT_stored"))
    w_in, w_high_ready, w_ready = [sem(f"w{b}_in") for b in range(2)], sem("w_high_ready"), sem("w_ready")
    proj_ready = [sem(f"proj{n}_ready") for n in range(4)]
    proj_free = [sem(f"proj{n}_free") for n in range(4)]
    uv_ready, uv_free, v_sq_ready, v_rstd_ready, vn_ready = (sem("uv_ready"), sem("uv_free"), sem("v_sq_ready"),
                                                             sem("v_rstd_ready"), sem("vn_ready"))
    mix_ready, mix_free, y_ready, y_stored = sem("mix_ready"), sem("mix_free"), sem("y_ready"), sem("y_stored")
    qk_ready, mq_ready, q_sq_ready, q_rstd_ready, qkn_ready, qkm_free = (
        sem("qk_ready"), sem("mq_ready"), sem("q_sq_ready"), sem("q_rstd_ready"), sem("qkn_ready"), sem("qkm_free"))
    qkT_ready, qkT_free, qkT_out_ready, qkT_stored = (sem("qkT_ready"), sem("qkT_free"), sem("qkT_out_ready"),
                                                      sem("qkT_stored"))
    v_ready, v_stored, c_ready, c_stored = sem("v_ready"), sem("v_stored"), sem("c_ready"), sem("c_stored")
    N_CONST = 5

    with nc.Block() as block:
        @block.sync
        def _(sp):
            for s in (y_stored, qkT_stored, qkT_stored, v_stored, c_stored):
                sp.sem_inc(s, 16)

            def load_x(i):
                sp.wait_ge(xt_free, i + 1)
                sp.dma_start(xt[:], tile_of(d["x"], i)).then_inc(x_in, 16)

            def keep(i):
                sp.wait_ge(h_high_ready, i + 1)
                sp.dma_start(cols_of(d["hT"], i), h_slot[:]).then_inc(hT_stored, 16)

            def store(i):
                sp.wait_ge(v_ready, i + 1)
                sp.dma_start(tile_of(d["fox_v"], i), v_out[:]).then_inc(v_stored, 16)
                sp.wait_ge(c_ready, i + 1)
                sp.dma_start(tile_of(d["mlstm_vo"], i), c_out[:]).then_inc(c_stored, 16)
                sp.wait_ge(y_ready, i + 1)
                sp.wait_ge(qkT_out_ready, i + 1)
                sp.dma_start(tile_of(d["y1"], i)[:, 0:GW], y_out[:]).then_inc(y_stored, 16)
                for part in range(2):
                    sp.dma_start(cols_of(d["qkmT"][part], i), raw(qkT_out[:, part])).then_inc(qkT_stored, 16)

            load_x(0)
            sp.sem_inc(hT_stored, 16)
            sp.dma_start(norm_gain[:], d["norm_g"].partition_broadcast(P)).then_inc(const_in, 16)
            sp.dma_start(sgu_gain[:], d["sgu_norm_g"].partition_broadcast(P)).then_inc(const_in, 16)
            sp.dma_start(qk_gain[:], d["qkm_g"].partition_broadcast(P)).then_inc(const_in, 16)
            sp.dma_start(sgu_w[:], d["sgu_wT"]).then_inc(const_in, 16)
            sp.dma_start(sgu_b[:], d["sgu_b"]).then_inc(const_in, 16)
            for k in range(KB):
                if k >= 2:
                    sp.wait_ge(w_ready, k - 1)
                sp.dma_start(staging[k % 2][:], d["w_tok1"][k * P:(k + 1) * P, :]).then_inc(w_in[k % 2], 16)
            with sp.Fori(0, NT - 1) as i:
                load_x(i + 1)
                keep(i)
                store(i)
            keep(NT - 1)
            store(NT - 1)
            sp.wait_ge(hT_stored, 16 * (NT + 1))
            for s in (y_stored, v_stored, c_stored):
                sp.wait_ge(s, 16 * (NT + 1))
            sp.wait_ge(qkT_stored, 32 * (NT + 1))

        @block.gpsimd
        def _(pool):
            def rstd(out, var, total, eps):
                nc.gpsimd.tensor_tensor(var[:], total[:], eps.to_broadcast([P, out.shape[1]]), ALU.add)
                pool.drain()
                return nc.gpsimd.tensor_tensor(out[:], var[:], g.neg_half[:].to_broadcast([P, out.shape[1]]), ALU.pow)

            def x_norm(i):
                pool.wait_ge(x_sq_ready, i + 1)
                rstd(x_rstd, x_var, x_sq, g.eps[:]).then_inc(x_rstd_ready, 1)

            def h_low(i):
                pool.wait_ge(h_high_ready, i + 1)
                nc.gpsimd.tensor_tensor(h_parts[1][:], h_slot[:], h_parts[0][:], ALU.subtract).then_inc(h_ready, 1)

            def head_norms(i):
                pool.wait_ge(v_sq_ready, i + 1)
                rstd(v_rstd, v_var, v_sq, g.head_eps[:]).then_inc(v_rstd_ready, 1)
                pool.wait_ge(q_sq_ready, i + 1)
                rstd(q_rstd, q_var, q_sq, g.head_eps[:]).then_inc(q_rstd_ready, 1)

            pool.wait_ge(const_in, 16 * N_CONST)
            nc.gpsimd.affine_select(out=sgu_w[:], in_=sgu_w[:], compare_op=ALU.is_ge, fill=0.0, base=0,
                                    pattern=[[0, GH], [1, P]], channel_multiplier=-1).then_inc(w_masked, 1)
            x_norm(0)
            for k in range(KB):
                pool.wait_ge(w_high_ready, k + 1)
                nc.gpsimd.tensor_tensor(w_parts[1][:, k], staging[k % 2][:], w_parts[0][:, k], ALU.subtract).then_inc(w_ready, 1)
            with pool.Fori(0, NT - 1) as i:
                h_low(i)
                x_norm(i + 1)
                head_norms(i)
            h_low(NT - 1)
            head_norms(NT - 1)

        @block.scalar
        def _(act):
            def square_x(i):
                act.wait_ge(x_in, 16 * (i + 1))
                nc.scalar.activation(junk[:], xt[:], ACT.Square, scale=DM ** -0.5, accum_out=x_sq[:]).then_inc(x_sq_ready, 1)

            def fill_slot(i):
                act.wait_ge(xT_ready, i + 1)
                act.wait_ge(h_free, i + 1)
                act.wait_ge(hT_stored, 16 * (i + 1))
                nc.scalar.activation(h_slot[:], p_xT[:], ACT.Copy)
                nc.scalar.activation(h_parts[0][:], p_xT[:], ACT.Copy)
                act.drain().then_inc(h_high_ready, 1)

            def evacuate(i):
                act.wait_ge(proj_ready[0], i + 1)
                act.wait_ge(uv_free, i + 1)
                nc.scalar.activation(uv[:], p_proj[0][:], ACT.Gelu_apprx_tanh).then_inc(uv_ready, 1)
                act.drain().then_inc(proj_free[0], 1)
                act.wait_ge(proj_ready[1], i + 1)
                act.wait_ge(qkm_free, i + 1)
                nc.scalar.activation(qkm[:, 0:512], p_proj[1][:], ACT.Copy).then_inc(qk_ready, 1)
                act.drain().then_inc(proj_free[1], 1)
                act.wait_ge(proj_ready[2], i + 1)
                act.wait_ge(v_stored, 16 * (i + 1))
                nc.scalar.activation(qkm[:, 512:768], p_proj[2][:, 0:GW], ACT.Copy).then_inc(mq_ready, 1)
                nc.scalar.activation(v_out[:], p_proj[2][:, GW:2 * GW], ACT.Copy).then_inc(v_ready, 1)
                act.drain().then_inc(proj_free[2], 1)
                act.wait_ge(proj_ready[3], i + 1)
                act.wait_ge(c_stored, 16 * (i + 1))
                nc.scalar.activation(c_out[:], p_proj[3][:], ACT.Copy).then_inc(c_ready, 1)
                act.drain().then_inc(proj_free[3], 1)

            for s in proj_free:
                act.sem_inc(s, 1)
            square_x(0)
            for k in range(KB):
                act.wait_ge(w_in[k % 2], 16 * (k // 2 + 1))
                nc.scalar.activation(w_parts[0][:, k], staging[k % 2][:], ACT.Copy).then_inc(w_high_ready, 1)
            with act.Fori(0, NT - 1) as i:
                fill_slot(i)
                square_x(i + 1)
                evacuate(i)
            fill_slot(NT - 1)
            evacuate(NT - 1)

        @block.vector
        def _(dve):
            def scale_x(i):
                dve.wait_ge(x_in, 16 * (i + 1))
                dve.wait_ge(x_rstd_ready, i + 1)
                nc.vector.scalar_tensor_tensor(xs[:], xt[:], x_rstd[:], norm_gain[:], ALU.mult, ALU.mult)\
                    .then_inc(xs_ready, 1)
                dve.drain().then_inc(xt_free, 1)

            def norms(i):
                dve.wait_ge(uv_ready, i + 1)
                v = uv[:, GW:2 * GW]
                nc.vector.tensor_tensor(v2[:], v, v, ALU.mult)
                dve.drain()
                nc.vector.tensor_reduce(v_sq[:], heads(v2[:]), AX.X, ALU.add).then_inc(v_sq_ready, 1)
                dve.wait_ge(qk_ready, i + 1)
                dve.wait_ge(mq_ready, i + 1)
                nc.vector.tensor_tensor(qkm2[:], qkm[:], qkm[:], ALU.mult)
                dve.drain()
                nc.vector.tensor_reduce(q_sq[:], heads(qkm2[:]), AX.X, ALU.add).then_inc(q_sq_ready, 1)
                dve.wait_ge(v_rstd_ready, i + 1)
                nc.vector.tensor_tensor(heads(v2[:]), heads(v), along(v_rstd[:], HD), ALU.mult)
                dve.drain()
                nc.vector.tensor_tensor(vn[:], v2[:], sgu_gain[:], ALU.mult).then_inc(vn_ready, 1)
                dve.wait_ge(q_rstd_ready, i + 1)
                nc.vector.tensor_tensor(heads(qkm2[:]), heads(qkm[:]), along(q_rstd[:], HD), ALU.mult)
                dve.drain()
                nc.vector.tensor_tensor(qkm[:], qkm2[:], qk_gain[:], ALU.mult).then_inc(qkn_ready, 1)

            def outputs(i):
                dve.wait_ge(mix_ready, i + 1)
                nc.vector.tensor_tensor(heads(mixed[:]), heads(p_mix[:, 0:GW]), along(sgu_b[:], HD), ALU.add)\
                    .then_inc(mix_free, 1)
                dve.drain()
                dve.wait_ge(y_stored, 16 * (i + 1))
                nc.vector.tensor_tensor(y_out[:], uv[:, 0:GW], mixed[:], ALU.mult).then_inc(y_ready, 1)
                dve.drain().then_inc(uv_free, 1)
                dve.wait_ge(qkT_stored, 32 * (i + 1))
                dve.wait_ge(qkT_ready, 2 * i + 1)
                split(nc, dve, qkT_out[:, 0, 0:4], qkT_out[:, 1, 0:4], p_qkT[:]).then_inc(qkT_free, 1)
                dve.wait_ge(qkT_ready, 2 * i + 2)
                split(nc, dve, qkT_out[:, 0, 4:6], qkT_out[:, 1, 4:6], p_qkT[:, 0:2, :]).then_inc(qkT_free, 1)
                dve.drain().then_inc(qkT_out_ready, 1)

            for s in (xt_free, uv_free, mix_free, qkT_free):
                dve.sem_inc(s, 1)
            dve.wait_ge(const_in, 16 * N_CONST)
            nc.vector.tensor_scalar(sgu_gain[:], sgu_gain[:], float(HD) ** 0.5, None, ALU.mult)
            nc.vector.tensor_scalar(qk_gain[:, GW:2 * GW], qk_gain[:, GW:2 * GW], float(HD) ** 0.5, None, ALU.mult)
            dve.drain()
            scale_x(0)
            with dve.Fori(0, NT - 1) as i:
                dve.wait_ge(xT_ready, i + 1)
                scale_x(i + 1)
                norms(i)
                outputs(i)
            norms(NT - 1)
            outputs(NT - 1)

        @block.tensor
        def _(pe):
            def turn_x(i):
                pe.wait_ge(xs_ready, i + 1)
                for k in range(KB):
                    last = nc.tensor.transpose(p_xT[:, k, :], xs[:, k * P:(k + 1) * P], g.ident[:])
                last.then_inc(xT_ready, 1)

            def project(i):
                pe.wait_ge(h_ready, i + 1)
                for n in range(4):
                    pe.wait_ge(proj_free[n], i + 1)
                    for k in range(KB):
                        for j, (w_part, h_part) in enumerate(PASSES):
                            last = nc.tensor.matmul(p_proj[n][:], h_parts[h_part][:, k, :],
                                                    w_parts[w_part][:, k, n * BANK:(n + 1) * BANK],
                                                    start=(k == 0 and j == 0), stop=(k == KB - 1 and j == len(PASSES) - 1))
                    last.then_inc(proj_ready[n], 1)
                pe.drain().then_inc(h_free, 1)

            def branch(i):
                pe.wait_ge(vn_ready, i + 1)
                pe.wait_ge(mix_free, i + 1)
                for h in range(GH):
                    last = nc.tensor.matmul(p_mix[:, h * HD:(h + 1) * HD], sgu_w[:, h, :], vn[:, h * HD:(h + 1) * HD],
                                            start=True, stop=True)
                last.then_inc(mix_ready, 1)
                pe.wait_ge(qkn_ready, i + 1)
                for first, n in ((0, 4), (4, 2)):
                    pe.wait_ge(qkT_free, 2 * i + 1 + (first > 0))
                    for j in range(n):
                        c = (first + j) * P
                        last = nc.tensor.transpose(p_qkT[:, j, :], qkm[:, c:c + P], g.ident[:])
                    last.then_inc(qkT_ready, 1)
                pe.drain().then_inc(qkm_free, 1)

            pe.sem_inc(h_free, 1)
            pe.sem_inc(qkm_free, 1)
            pe.wait_ge(const_in, 16 * N_CONST)
            pe.wait_ge(w_masked, 1)
            turn_x(0)
            pe.wait_ge(w_ready, KB)
            project(0)
            with pe.Fori(1, NT) as i:
                pe.wait_ge(h_high_ready, i)
                turn_x(i)
                branch(i - 1)
                project(i)
            branch(NT - 1)
    ph.close()


GATE_PAIRS, CONV_PAIRS, SHIFT_PAIRS = 4, 2, 3
FIRST_SHIFT = GATE_PAIRS + CONV_PAIRS
LAST_PAIR = FIRST_SHIFT + SHIFT_PAIRS
CONV_K = 4
PAD = CONV_K - 1


class FeaturePass:
    CHUNK = BANK // 2

    def __init__(self, ph, staging):
        self.w = [ph.sb(f"w{b}", [P, KB, P]) for b in range(2)]
        self.w_parts = [[ph.sb(f"w{b}_{part}", [P, KB, P], F32R) for part in ("high", "low")] for b in range(2)]
        self.p_out = [ph.ps(f"out{b}", [P, T]) for b in range(2)]
        self.x_parts = [ph.sb(f"x_{part}", [P, KB, T], F32R) for part in ("high", "low")]
        self.staging = [s[:].rearrange("p (k t) -> p k t", k=KB) for s in staging]
        self.staged = [ph.sem(f"staged{i}") for i in range(len(staging))]
        self.x_high_ready, self.x_ready, self.taken = ph.sem("x_high_ready"), ph.sem("x_ready"), ph.sem("taken")
        self.w_in, self.w_ready, self.p_ready, self.p_free = (
            [ph.sem(f"{n}{b}") for b in range(2)] for n in ("w_in", "w_ready", "p_ready", "p_free"))

    def load(self, sp, w_dram, j, b):
        sp.dma_start(self.w[b][:].rearrange("p k c -> p (k c)"),
                     w_dram[bass.ds(2 * j + b, 1)].rearrange("a p c -> (a p) c")).then_inc(self.w_in[b], 16)

    def load_input(self, sp, x_dram):
        n_staging = len(self.staging)
        for n in range(T // self.CHUNK):
            if n >= n_staging:
                sp.wait_ge(self.x_ready, n - n_staging + 1)
            sp.dma_start(self.staging[n % n_staging], x_dram.rearrange("(k p) t -> p k t", p=P)[
                :, :, n * self.CHUNK:(n + 1) * self.CHUNK]).then_inc(self.staged[n % n_staging], 16)

    def pieces(self):
        for n in range(T // self.CHUNK):
            yield n, slice(n * self.CHUNK, (n + 1) * self.CHUNK), self.staging[n % len(self.staging)]

    def round_input(self, nc, act):
        for n, at, piece in self.pieces():
            act.wait_ge(self.staged[n % len(self.staging)], 16 * (n // len(self.staging) + 1))
            nc.scalar.activation(self.x_parts[0][:, :, at], piece, ACT.Copy).then_inc(self.x_high_ready, 1)

    def rest_of_input(self, nc, dve):
        for n, at, piece in self.pieces():
            dve.wait_ge(self.x_high_ready, n + 1)
            nc.vector.tensor_tensor(self.x_parts[1][:, :, at], piece, self.x_parts[0][:, :, at], ALU.subtract)\
                .then_inc(self.x_ready, 1)

    def split_weights(self, nc, pool, j, b, first=False):
        if not first:
            pool.wait_ge(self.p_ready[b], j)
        wait_apart(pool, self.w_in[b], 16 * (j + 1), self.taken)
        nc.gpsimd.tensor_copy(self.w_parts[b][0][:], self.w[b][:])
        pool.drain()
        nc.gpsimd.tensor_tensor(self.w_parts[b][1][:], self.w[b][:], self.w_parts[b][0][:], ALU.subtract)\
            .then_inc(self.w_ready[b], 1)

    def project(self, nc, pe, j, b):
        pe.wait_ge(self.w_ready[b], j + 1)
        pe.wait_ge(self.p_free[b], j + 1)
        for n in range(T // BANK):
            at = slice(n * BANK, (n + 1) * BANK)
            pe.wait_ge(self.x_ready, (n + 1) * BANK // self.CHUNK)
            for k in range(KB):
                for i, (w_part, x_part) in enumerate(PASSES):
                    last = nc.tensor.matmul(self.p_out[b][:, at], self.w_parts[b][w_part][:, k, :],
                                            self.x_parts[x_part][:, k, at],
                                            start=(k == 0 and i == 0), stop=(k == KB - 1 and i == len(PASSES) - 1))
        last.then_inc(self.p_ready[b], 1)


def feature_pass_1(nc, d, g):
    ph = Phase(nc, "f1")
    sb, ps, sem = ph.sb, ph.ps, ph.sem
    work = sb("work", [P, T])
    out = [sb(f"out{b}", [P, T]) for b in range(2)]
    fp = FeaturePass(ph, [*out, work])
    p_out, p_ready, p_free, w_ready = fp.p_out, fp.p_ready, fp.p_free, fp.w_ready
    padded = [sb(f"padded{b}", [P, PAD + T]) for b in range(2)]
    conv_w, conv_b = sb("conv_w", [P, 2 * CONV_PAIRS, CONV_K]), sb("conv_b", [P, 2 * CONV_PAIRS])
    mu = sb("mu", [P, 2 * SHIFT_PAIRS + 2])
    const_in = sem("const_in")
    padded_ready = [sem(f"padded{b}_ready") for b in range(2)]
    padded_free = [sem(f"padded{b}_free") for b in range(2)]
    work_ready = sem("work_ready")
    out_ready = [sem(f"out{b}_ready") for b in range(2)]
    stored = [sem(f"stored{b}") for b in range(2)]
    pads_ready = sem("pads_ready")

    def rows_of(dram, block):
        return dram[bass.ds(block * P, P), :]

    with nc.Block() as block:
        @block.sync
        def _(sp):
            def store(j, b, dst):
                sp.wait_ge(out_ready[b], j + 1)
                sp.dma_start(dst, out[b][:]).then_inc(stored[b], 16)

            def turn(j, dst, load_next=2):
                for b in range(2):
                    if b < load_next:
                        sp.wait_ge(w_ready[b], j + 1)
                        fp.load(sp, d["w_fm1"], j + 1, b)
                    store(j, b, rows_of(*dst(j, b)))

            for b in range(2):
                sp.sem_inc(stored[b], 16)
            for b in range(2):
                fp.load(sp, d["w_fm1"], 0, b)
            fp.load_input(sp, d["hT"])
            sp.dma_start(conv_w[:], d["conv_w"]).then_inc(const_in, 16)
            sp.dma_start(conv_b[:], d["conv_b"]).then_inc(const_in, 16)
            sp.dma_start(mu[:], d["rwkv_mu"]).then_inc(const_in, 16)
            with sp.Fori(0, GATE_PAIRS) as j:
                turn(j, lambda j, b: (d["z1T"], 2 * j + b))
            with sp.Fori(GATE_PAIRS, FIRST_SHIFT) as j:
                turn(j, lambda j, b: (d["mlstm_qkT"], 2 * (j - GATE_PAIRS) + b))
            with sp.Fori(FIRST_SHIFT, LAST_PAIR) as j:
                turn(j, lambda j, b: (d["rwkv_T"], 2 * (j - FIRST_SHIFT) + b))
            turn(LAST_PAIR, lambda j, b: (d["z1T"], 2 * GATE_PAIRS + b), load_next=1)
            store(LAST_PAIR + 1, 0, d["lowT"])
            for b in range(2):
                sp.wait_ge(stored[b], 16 * (LAST_PAIR + 2 + (b == 0)))

        @block.tensor
        def _(pe):
            with pe.Fori(0, LAST_PAIR + 1) as j:
                fp.project(nc, pe, j, 0)
                fp.project(nc, pe, j, 1)
            fp.project(nc, pe, LAST_PAIR + 1, 0)

        @block.gpsimd
        def _(pool):
            for b in range(2):
                last = nc.gpsimd.memset(padded[b][:, 0:PAD], 0.0)
            last.then_inc(pads_ready, 1)
            for b in range(2):
                fp.split_weights(nc, pool, 0, b, first=True)
            with pool.Fori(1, LAST_PAIR + 1) as j:
                fp.split_weights(nc, pool, j, 0)
                fp.split_weights(nc, pool, j, 1)
            fp.split_weights(nc, pool, LAST_PAIR + 1, 0)

        @block.scalar
        def _(act):
            def straight(j, b, func):
                act.wait_ge(p_ready[b], j + 1)
                act.wait_ge(stored[b], 16 * (j + 1))
                nc.scalar.activation(out[b][:], p_out[b][:], func).then_inc(out_ready[b], 1)
                act.drain().then_inc(p_free[b], 1)

            def to_padded(j, b):
                act.wait_ge(p_ready[b], j + 1)
                act.wait_ge(padded_free[b], j - GATE_PAIRS + 1)
                nc.scalar.activation(padded[b][:, PAD:], p_out[b][:], ACT.Copy).then_inc(padded_ready[b], 1)
                act.drain().then_inc(p_free[b], 1)

            def silu_of_work(j, b, n):
                act.wait_ge(work_ready, n)
                act.wait_ge(stored[b], 16 * (j + 1))
                nc.scalar.activation(out[b][:], work[:], ACT.Silu).then_inc(out_ready[b], 1)

            for b in range(2):
                act.sem_inc(p_free[b], 1)
            fp.round_input(nc, act)
            with act.Fori(0, GATE_PAIRS) as j:
                for b in range(2):
                    straight(j, b, ACT.Silu)
            with act.Fori(GATE_PAIRS, FIRST_SHIFT) as j:
                for b in range(2):
                    to_padded(j, b)
                    silu_of_work(j, b, 2 * (j - GATE_PAIRS) + b + 1)
            with act.Fori(FIRST_SHIFT, LAST_PAIR) as j:
                for b in range(2):
                    to_padded(j, b)
            for b in range(2):
                to_padded(LAST_PAIR, b)
                silu_of_work(LAST_PAIR, b, 2 * CONV_PAIRS + b + 1)
            straight(LAST_PAIR + 1, 0, ACT.Copy)

        @block.vector
        def _(dve):
            def convolve(j, b, c):
                dve.wait_ge(padded_ready[b], j - GATE_PAIRS + 1)
                dve.wait_ge(out_ready[1 - b], j + b)
                nc.vector.tensor_scalar(work[:], padded[b][:, PAD:], conv_w[:, bass.ds(c, 1), PAD],
                                        conv_b[:, bass.ds(c, 1)], ALU.mult, ALU.add)
                for tap in range(PAD):
                    dve.drain()
                    last = nc.vector.scalar_tensor_tensor(work[:], padded[b][:, tap:tap + T],
                                                          conv_w[:, bass.ds(c, 1), tap], work[:], ALU.mult, ALU.add)
                last.then_inc(work_ready, 1)
                dve.drain().then_inc(padded_free[b], 1)

            def shift(j, b, c, dst, signal):
                dve.wait_ge(padded_ready[b], j - GATE_PAIRS + 1)
                x, previous = padded[b][:, PAD:], padded[b][:, PAD - 1:PAD - 1 + T]
                nc.vector.tensor_tensor(work[:], previous, x, ALU.subtract)
                dve.drain()
                nc.vector.scalar_tensor_tensor(dst[:], work[:], mu[:, bass.ds(c, 1)], x, ALU.mult, ALU.add)\
                    .then_inc(signal, 1)
                dve.drain().then_inc(padded_free[b], 1)

            fp.rest_of_input(nc, dve)
            for b in range(2):
                dve.sem_inc(padded_free[b], 1)
            dve.wait_ge(const_in, 16 * 3)
            dve.wait_ge(pads_ready, 1)
            with dve.Fori(GATE_PAIRS, FIRST_SHIFT) as j:
                for b in range(2):
                    convolve(j, b, 2 * (j - GATE_PAIRS) + b)
            dve.wait_ge(out_ready[1], FIRST_SHIFT)
            with dve.Fori(FIRST_SHIFT, LAST_PAIR) as j:
                for b in range(2):
                    dve.wait_ge(stored[b], 16 * (j + 1))
                    shift(j, b, 2 * (j - FIRST_SHIFT) + b, out[b], out_ready[b])
            for b in range(2):
                if b:
                    dve.wait_ge(out_ready[0], LAST_PAIR + 1)
                shift(LAST_PAIR, b, 2 * SHIFT_PAIRS + b, work, work_ready)
    ph.close()


def gates_phase(nc, d, g):
    ph = Phase(nc, "gates")
    sb, sem = ph.sb, ph.sem
    R = 2 * GH
    logit, i_gate, e, f_sum, a = (sb(n, [R, T]) for n in ("logit", "i_gate", "e", "f_sum", "a"))
    run_max, w_inter, w_new, e_neg_m, ones = (sb(n, [R, T]) for n in ("run_max", "w_inter", "w_new", "e_neg_m", "ones"))
    bias, i_bias = sb("bias", [R, 1]), sb("i_bias", [R, 1])
    fox, one = [sb(f"fox{n}", [R, T], F32R) for n in range(4)], sb("one", [R, T], F32R)
    prev, carry = sb("prev", [R, NT]), sb("carry", [R, NT])
    loaded, zeroed, abs_ready, exp_ready, ln_ready, args_ready, done, stored = (
        sem(n) for n in ("loaded", "zeroed", "abs_ready", "exp_ready", "ln_ready", "args_ready", "done", "stored"))

    def chunks(ap):
        return ap.rearrange("p (c t) -> p c t", t=P)

    with nc.Block() as block:
        @block.sync
        def _(sp):
            sp.wait_ge(zeroed, 1)
            sp.dma_start(logit[0:GH, :], d["lowT"][64:68, :]).then_inc(loaded, 16)
            sp.dma_start(logit[GH:R, :], d["lowT"][72:76, :]).then_inc(loaded, 16)
            sp.dma_start(i_gate[GH:R, :], d["lowT"][68:72, :]).then_inc(loaded, 16)
            sp.dma_start(bias[:], d["f_bias"]).then_inc(loaded, 16)
            sp.dma_start(i_bias[GH:R, :], d["i_bias"]).then_inc(loaded, 16)
            sp.wait_ge(done, 1)
            for n, (of_query, of_key) in enumerate(((fox[0], one), (fox[1], one), (one, fox[2]), (one, fox[3]))):
                sp.dma_start(d["fox_rows"][0:GH, n, :], raw(of_query[0:GH, :])).then_inc(stored, 16)
                sp.dma_start(d["fox_rows"][GH:R, n, :], raw(of_key[0:GH, :])).then_inc(stored, 16)
            for n, rows in enumerate((a, w_inter, w_new, e_neg_m)):
                sp.dma_start(d["mlstm_rows"][n * GH:(n + 1) * GH, :], rows[GH:R, :]).then_inc(stored, 16)
            sp.dma_start(d["mlstm_max"], run_max[GH:R, :]).then_inc(stored, 16)
            sp.dma_start(d["mlstm_carry"], carry[GH:R, :]).then_inc(stored, 16)
            sp.wait_ge(stored, 16 * 14)

        @block.scalar
        def _(act):
            act.wait_ge(abs_ready, 1)
            nc.scalar.activation(e[:], e[:], ACT.Exp).then_inc(exp_ready, 1)
            act.drain()
            nc.scalar.activation(e[:], e[:], ACT.Ln, bias=1.0).then_inc(ln_ready, 1)
            act.wait_ge(args_ready, 1)
            nc.scalar.activation(w_inter[:], w_inter[:], ACT.Exp)
            nc.scalar.activation(w_new[:], w_new[:], ACT.Exp)
            nc.scalar.activation(e_neg_m[:], e_neg_m[:], ACT.Exp, scale=-1.0)
            nc.scalar.activation(carry[:], carry[:], ACT.Exp)
            act.drain().then_inc(done, 1)

        @block.vector
        def _(dve):
            nc.vector.memset(i_gate[:], 0.0)
            nc.vector.memset(ones[:], 1.0)
            nc.vector.memset(i_bias[:], 0.0)
            dve.drain().then_inc(zeroed, 1)
            dve.wait_ge(loaded, 16 * 5)
            nc.vector.tensor_scalar(logit[:], logit[:], bias[:], None, ALU.add)
            dve.drain()
            nc.vector.scalar_tensor_tensor(e[:], logit[:], -1.0, logit[:], ALU.mult, ALU.min).then_inc(abs_ready, 1)
            dve.drain()
            nc.vector.tensor_scalar(logit[:], logit[:], 0.0, None, ALU.min)
            dve.drain()
            dve.wait_ge(ln_ready, 1)
            nc.vector.tensor_tensor(logit[:], logit[:], e[:], ALU.subtract)
            dve.drain()
            nc.vector.tensor_tensor_scan(f_sum[:], ones[:], logit[:], 0.0, ALU.mult, ALU.add)
            dve.drain()
            nc.vector.scalar_tensor_tensor(a[:], i_gate[:], i_bias[:], f_sum[:], ALU.add, ALU.subtract)
            dve.drain()
            nc.vector.tensor_copy(one[:], ones[:])
            split(nc, dve, fox[0][:], fox[1][:], f_sum[:])
            split(nc, dve, fox[2][:], fox[3][:], a[:])
            nc.vector.tensor_tensor_scan(run_max[:], a[:], a[:], 0.0, ALU.max, ALU.max)
            dve.drain()
            nc.vector.memset(prev[:, 0:1], 0.0)
            nc.vector.tensor_copy(prev[:, 1:NT], chunks(run_max[:])[:, 0:NT - 1, P - 1])
            dve.drain()
            ends = chunks(run_max[:])[:, :, P - 1]
            nc.vector.tensor_tensor(carry[:], prev[:], ends, ALU.subtract)
            nc.vector.tensor_tensor(chunks(w_inter[:]), along(prev[:], P), chunks(run_max[:]), ALU.subtract)
            nc.vector.tensor_tensor(chunks(w_new[:]), chunks(a[:]), along(ends, P), ALU.subtract)
            nc.vector.tensor_tensor(e_neg_m[:], f_sum[:], run_max[:], ALU.add)
            dve.drain().then_inc(args_ready, 1)
    ph.close()


def keys_values(nc, g, block, ph, banks, src, w_src, nh, gain_src, scale, shift, scale_ready, kT_dst, v_dst):
    sb, sem = ph.sb, ph.sem
    W = nh * HD
    w = sb("w", [P, KB, 2 * W])
    xt, xs, x_slot = sb("xt", [P, NMEM // P, DM]), sb("xs", [P, DM]), sb("x_slot", [P, KB, P])
    x_sq, x_rstd = sb("x_sq", [P, 1]), sb("x_rstd", [P, 1])
    kn, k2, v_out, kT_out = sb("kn", [P, W]), sb("k2", [P, W]), sb("v_out", [P, W]), sb("kT_out", [P, 2, W // P, P], F32R)
    k_sq, k_rstd, gain = sb("k_sq", [P, nh]), sb("k_rstd", [P, nh]), sb("gain", [P, W])
    p_xT, p_k, p_v, p_kT = banks
    names = ("const_in", "x_in", "x_sq_ready", "x_rstd_ready", "xs_ready", "xT_ready", "slot_ready", "k_ready", "v_ready",
             "v_out_ready", "k_sq_ready", "k_rstd_ready", "kn_ready", "kT_ready", "kT_out_ready", "v_stored", "kT_stored")
    (const_in, x_in, x_sq_ready, x_rstd_ready, xs_ready, xT_ready, slot_ready, k_ready, v_ready, v_out_ready, k_sq_ready,
     k_rstd_ready, kn_ready, kT_ready, kT_out_ready, v_stored, kT_stored) = (sem(n) for n in names)
    def tile(i):
        return xt[:, bass.ds(i, 1), :].rearrange("p a c -> p (a c)")

    def load(eng):
        eng.dma_start(xt[:], src.rearrange("(n p) c -> p n c", p=P)).then_inc(x_in, 16)
        eng.dma_start(gain[:], gain_src.partition_broadcast(P)).then_inc(const_in, 16)
        eng.dma_start(w[:], w_src.rearrange("(k p) c -> p k c", p=P)).then_inc(const_in, 16)

    def store(sp):
        for s in (v_stored, kT_stored, kT_stored):
            sp.sem_inc(s, 16)
        with sp.Fori(0, NMEM // P) as i:
            sp.wait_ge(v_out_ready, i + 1)
            sp.wait_ge(kT_out_ready, i + 1)
            sp.dma_start(tile_of(v_dst, i), v_out[:]).then_inc(v_stored, 16)
            for part in range(2):
                sp.dma_start(cols_of(kT_dst[part], i), raw(kT_out[:, part])).then_inc(kT_stored, 16)
        sp.wait_ge(v_stored, 16 * (NMEM // P + 1))
        sp.wait_ge(kT_stored, 32 * (NMEM // P + 1))

    @block.scalar
    def _(act):
        act.wait_ge(x_in, 16)
        with act.Fori(0, NMEM // P) as i:
            nc.scalar.activation(xs[:], tile(i), ACT.Square, scale=DM ** -0.5, accum_out=x_sq[:]).then_inc(x_sq_ready, 1)
            act.wait_ge(xT_ready, i + 1)
            scale_ready(act)
            for k in range(KB):
                last = nc.scalar.activation(x_slot[:, k, :], p_xT[:, k, :], ACT.Identity, scale=scale[:, k:k + 1],
                                            bias=shift[:, k:k + 1] if shift is not None else 0.0)
            act.drain().then_inc(slot_ready, 1)
            act.wait_ge(v_ready, i + 1)
            act.wait_ge(v_stored, 16 * (i + 1))
            nc.scalar.activation(v_out[:], p_v[:, 0:W], ACT.Copy).then_inc(v_out_ready, 1)

    @block.gpsimd
    def _(pool):
        with pool.Fori(0, NMEM // P) as i:
            pool.wait_ge(x_sq_ready, i + 1)
            nc.gpsimd.tensor_tensor(x_sq[:], x_sq[:], g.eps[:], ALU.add)
            pool.drain()
            nc.gpsimd.tensor_tensor(x_rstd[:], x_sq[:], g.neg_half[:], ALU.pow).then_inc(x_rstd_ready, 1)
            pool.wait_ge(k_sq_ready, i + 1)
            nc.gpsimd.tensor_tensor(k_sq[:], k_sq[:], g.head_eps[:].to_broadcast([P, nh]), ALU.add)
            pool.drain()
            nc.gpsimd.tensor_tensor(k_rstd[:], k_sq[:], g.neg_half[:].to_broadcast([P, nh]), ALU.pow)\
                .then_inc(k_rstd_ready, 1)

    @block.vector
    def _(dve):
        dve.wait_ge(const_in, 32)
        nc.vector.tensor_scalar(gain[:], gain[:], HD ** 0.5, None, ALU.mult)
        dve.drain()
        with dve.Fori(0, NMEM // P) as i:
            dve.wait_ge(x_rstd_ready, i + 1)
            nc.vector.tensor_scalar(xs[:], tile(i), x_rstd[:], None, ALU.mult).then_inc(xs_ready, 1)
            dve.wait_ge(k_ready, i + 1)
            nc.vector.tensor_copy(kn[:], p_k[:, 0:W])
            dve.drain()
            nc.vector.tensor_tensor(k2[:], kn[:], kn[:], ALU.mult)
            dve.drain()
            nc.vector.tensor_reduce(k_sq[:], heads(k2[:]), AX.X, ALU.add).then_inc(k_sq_ready, 1)
            dve.wait_ge(k_rstd_ready, i + 1)
            nc.vector.tensor_tensor(heads(k2[:]), heads(kn[:]), along(k_rstd[:], HD), ALU.mult)
            dve.drain()
            nc.vector.tensor_tensor(kn[:], k2[:], gain[:], ALU.mult).then_inc(kn_ready, 1)
            dve.wait_ge(kT_ready, i + 1)
            dve.wait_ge(kT_stored, 32 * (i + 1))
            split(nc, dve, kT_out[:, 0], kT_out[:, 1], p_kT[:, 0:W // P]).then_inc(kT_out_ready, 1)

    @block.tensor
    def _(pe):
        pe.wait_ge(const_in, 32)
        with pe.Fori(0, NMEM // P) as i:
            pe.wait_ge(xs_ready, i + 1)
            for k in range(KB):
                last = nc.tensor.transpose(p_xT[:, k, :], xs[:, k * P:(k + 1) * P], g.ident[:])
            last.then_inc(xT_ready, 1)
            pe.wait_ge(slot_ready, i + 1)
            for out, first, ready in ((p_k, 0, k_ready), (p_v, W, v_ready)):
                for k in range(KB):
                    last = nc.tensor.matmul(out[:, 0:W], x_slot[:, k, :], w[:, k, first:first + W],
                                            start=(k == 0), stop=(k == KB - 1))
                last.then_inc(ready, 1)
            pe.wait_ge(kn_ready, i + 1)
            for j in range(W // P):
                last = nc.tensor.transpose(p_kT[:, j, :], kn[:, j * P:(j + 1) * P], g.ident[:])
            last.then_inc(kT_ready, 1)
    return load, store


HALF = NT // 2
GROUP = BANK // P


def attention(nc, d, g, ph, nh, kT, k_x, v, load, load_q, n_loads, key_cols, n_consts, y_dst, s_bufs, s_at,
              bias=None, bias_consts=None, order=range(NT), turned_by_scalar=(1,), o_bufs=2):
    sb, ps, sem = ph.sb, ph.ps, ph.sem
    q = [[sb(f"q{s}_{part}", [P, HALF * P], F32R) for part in ("high", "low")] for s in range(2)]
    q_x = [sb(f"q{s}_x", [k_x.shape[0], HALF * P], F32R) if k_x is not None else None for s in range(2)]
    blocks = [key_cols(u) for u in order]
    s_cols = [len(b) * P for b in blocks]
    prob = [sb(f"prob{b}", [P, max(s_cols[b::s_bufs])]) for b in range(s_bufs)]
    probT = [sb(f"probT{b}", [P, GROUP, P]) for b in range(2)]
    top, neg_top = ([sb(f"{n}{b}", [P, 1]) for b in range(s_bufs)] for n in ("top", "neg_top"))
    total, inv = [sb(f"total{b}", [P, 1]) for b in range(s_bufs + 1)], sb("inv", [P, 1])
    y = [sb(f"y{s}", [P, HALF, HD]) for s in range(2)]
    p_s = ps("s", [P, max(s_at(i) + n for i, n in enumerate(s_cols))])
    p_t = [ps(f"t{b}", [P, GROUP, P]) for b in range(2)]
    p_o = [ps(f"o{b}", [P, BANK]) for b in range(o_bufs)]
    const_in = sem("const_in")
    q_in, q_free = [sem(f"q{s}_in") for s in range(2)], [sem(f"q{s}_free") for s in range(2)]
    s_ready, top_ready, prob_ready = sem("s_ready"), sem("top_ready"), sem("prob_ready")
    t_ready, probT_ready = [sem(f"t{b}_ready") for b in range(2)], [sem(f"probT{b}_ready") for b in range(2)]
    o_ready, o_free = sem("o_ready"), sem("o_free")
    y_ready, y_stored = [sem(f"y{s}_ready") for s in range(2)], [sem(f"y{s}_stored") for s in range(2)]

    halves = [u // HALF for u in order]
    first_of = [halves.index(s) for s in range(2)]
    last_of = [NT - 1 - halves[::-1].index(s) for s in range(2)]
    groups, n = [], 0
    for b in blocks:
        cut = [b[i:i + GROUP] for i in range(0, len(b), GROUP)]
        groups.append([(n + i, c) for i, c in enumerate(cut)])
        n += len(cut)
    per_head = n
    assert per_head % 2 == 0

    def count(h, n):
        return h * (per_head // 2) + n // 2 + 1

    def scores_of(i):
        return p_s[:, s_at(i):s_at(i) + s_cols[i]]

    def runs(u):
        out = []
        for i, (c, _) in enumerate(blocks[u]):
            if out and (i * P) % BANK and out[-1][1] + out[-1][2] == c:
                out[-1][2] += P
            else:
                out.append([i * P, c, P])
        return out

    with nc.Block() as block:
        @block.sync
        def _(sp):
            for s in range(2):
                sp.sem_inc(y_stored[s], 16)
            load(sp, const_in)
            with sp.Fori(0, nh) as h:
                for s in range(2):
                    sp.wait_ge(q_free[s], h + 1)
                    load_q(sp, h, s, q[s], q_x[s], q_in[s])
                for s in range(2):
                    sp.wait_ge(y_ready[s], HALF * (h + 1))
                    sp.dma_start(y_dst(h, s), y[s][:]).then_inc(y_stored[s], 16)
            for s in range(2):
                sp.wait_ge(y_stored[s], 16 * (nh + 1))

        if bias_consts is not None:
            @block.gpsimd
            def _(pool):
                bias_consts(pool, const_in)

        @block.tensor
        def _(pe):
            def scores(h, i):
                s, at_q = halves[i], order[i] % HALF * P
                if i == first_of[s]:
                    pe.wait_ge(q_in[s], 16 * n_loads * (h + 1))
                rows = [(x, kT) for x in q[s]] + ([(q_x[s], k_x)] if k_x is not None else [])
                for at, c, n in runs(i):
                    for j, (x, keys) in enumerate(rows):
                        last = nc.tensor.matmul(scores_of(i)[:, at:at + n], x[:, at_q:at_q + P],
                                                keys[:, bass.ds(h, 1), c:c + n].rearrange("p a c -> p (a c)"),
                                                start=(j == 0), stop=(j == len(rows) - 1))
                last.then_inc(s_ready, 1)
                if i == last_of[s]:
                    pe.drain().then_inc(q_free[s], 1)

            def turn(i, k):
                n, part = groups[i][k]
                for j in range(len(part)):
                    at = (k * GROUP + j) * P
                    last = nc.tensor.transpose(p_t[n % 2][:, j, :], prob[i % s_bufs][:, at:at + P], g.ident[:])
                last.then_inc(t_ready[n % 2], 1)

            def tile(h, i):
                pe.wait_ge(prob_ready, NT * h + i + 1)
                turn(i, 0)
                if i + s_bufs < NT:
                    scores(h, i + s_bufs)
                if len(groups[i]) > 1:
                    turn(i, 1)
                pe.wait_ge(o_free, NT * h + i + 1)
                for k, (n, part) in enumerate(groups[i]):
                    pe.wait_ge(probT_ready[n % 2], count(h, n))
                    for j, (_, vb) in enumerate(part):
                        last = nc.tensor.matmul(p_o[i % o_bufs][:, 0:HD], probT[n % 2][:, j, :], v[:, vb, bass.ds(h * HD, HD)],
                                                start=(k == 0 and j == 0), stop=(k * GROUP + j == len(blocks[i]) - 1))
                    if k + 2 < len(groups[i]):
                        turn(i, k + 2)
                last.then_inc(o_ready, 1)

            for s in range(2):
                pe.sem_inc(q_free[s], 1)
            pe.wait_ge(const_in, n_consts)
            with pe.Fori(0, nh) as h:
                for i in range(s_bufs):
                    scores(h, i)
                for i in range(NT):
                    tile(h, i)

        def copies(eng, copy, h, i, parities):
            def step(n, part):
                eng.wait_ge(t_ready[n % 2], count(h, n))
                copy(probT[n % 2][:, 0:len(part), :], p_t[n % 2][:, 0:len(part), :]).then_inc(probT_ready[n % 2], 1)
            return [(step, n, part) for n, part in groups[i] if n % 2 in parities]

        @block.scalar
        def _(act):
            def exps(h, i):
                act.wait_ge(top_ready, NT * h + i + 1)
                if i >= s_bufs:
                    n = groups[i - s_bufs][-1][0]
                    act.wait_ge(t_ready[n % 2], count(h, n))
                nc.scalar.activation(prob[i % s_bufs][:, 0:s_cols[i]], scores_of(i), ACT.Exp, bias=neg_top[i % s_bufs][:],
                                     accum_out=total[i % (s_bufs + 1)][:]).then_inc(prob_ready, 1)

            with act.Fori(0, nh) as h:
                for i in range(s_bufs):
                    exps(h, i)
                for i in range(NT):
                    todo = copies(act, lambda o, i: nc.scalar.activation(o, i, ACT.Copy), h, i, turned_by_scalar)
                    for step, n, part in todo:
                        step(n, part)
                    if i + s_bufs < NT:
                        exps(h, i + s_bufs)

        @block.vector
        def _(dve):
            def maxima(h, i):
                dve.wait_ge(s_ready, NT * h + i + 1)
                if bias is not None:
                    bias(dve, h, order[i], scores_of(i))
                    dve.drain()
                nc.vector.tensor_reduce(top[i % s_bufs][:], scores_of(i), AX.X, ALU.max)
                dve.drain()
                nc.vector.tensor_scalar(neg_top[i % s_bufs][:], top[i % s_bufs][:], -1.0, None, ALU.mult).then_inc(top_ready, 1)

            def normalise(h, i):
                dve.wait_ge(prob_ready, NT * h + i + 1)
                nc.vector.reciprocal(inv[:], total[i % (s_bufs + 1)][:])
                dve.drain()
                dve.wait_ge(o_ready, NT * h + i + 1)
                s = halves[i]
                if i == first_of[s]:
                    dve.wait_ge(y_stored[s], 16 * (h + 1))
                nc.vector.tensor_scalar(y[s][:, order[i] % HALF, :], p_o[i % o_bufs][:, 0:HD], inv[:], None, ALU.mult)\
                    .then_inc(y_ready[s], 1)
                dve.drain().then_inc(o_free, 1)

            dve.sem_inc(o_free, o_bufs)
            dve.wait_ge(const_in, n_consts)
            with dve.Fori(0, nh) as h:
                for i in range(s_bufs):
                    maxima(h, i)
                for i in range(NT):
                    todo = copies(dve, nc.vector.tensor_copy, h, i, [p for p in range(2) if p not in turned_by_scalar])
                    if i > 0:
                        normalise(h, i - 1)
                    for step, n, part in todo[:1]:
                        step(n, part)
                    if i + s_bufs < NT:
                        maxima(h, i + s_bufs)
                    for step, n, part in todo[1:]:
                        step(n, part)
                normalise(h, NT - 1)
    ph.close()


def load_twice(sp, q, src, q_in):
    for part in range(2):
        for half in range(2):
            sp.dma_start(raw(q[part][half * HD:(half + 1) * HD]), src(part)).then_inc(q_in, 16)


def head_tiles(dram, first):
    def at(h, s):
        return dram.rearrange("(s u p) c -> p s u c", s=2, p=P)[:, s, :, bass.ds(h * HD + first, HD)]
    return at


def fox_attention(nc, d, g):
    ph = Phase(nc, "fox")
    kT, v, tri = ph.sb("kT", [P, GH, T], F32R), ph.sb("v", [P, NT, GW]), ph.sb("tri", [P, P])
    k_x = ph.sb("k_x", [4, GH, T], F32R)

    def load(sp, const_in):
        for part in range(2):
            sp.dma_start(raw(kT[part * HD:(part + 1) * HD]), d["qkmT"][part, GW:2 * GW].rearrange("(h e) t -> e h t", e=HD))\
                .then_inc(const_in, 16)
        sp.dma_start(raw(k_x[:]), d["fox_rows"][GH:2 * GH].rearrange("h e t -> e h t")).then_inc(const_in, 16)
        sp.dma_start(v[:], d["fox_v"].rearrange("(n p) c -> p n c", p=P)).then_inc(const_in, 16)

    def load_q(sp, h, s, q, q_x, q_in):
        cols = slice(s * HALF * P, (s + 1) * HALF * P)
        load_twice(sp, q, lambda part: d["qkmT"][part, bass.ds(h * HD, HD), cols], q_in)
        sp.dma_start(raw(q_x[:]), d["fox_rows"][bass.ds(h, 1), :, cols].rearrange("h e t -> (h e) t")).then_inc(q_in, 16)

    def bias_consts(pool, const_in):
        nc.gpsimd.memset(tri[:], 0.0)
        pool.drain()
        nc.gpsimd.affine_select(out=tri[:], in_=tri[:], compare_op=ALU.is_ge, fill=MASKED, base=0, pattern=[[-1, P]],
                                channel_multiplier=1).then_inc(const_in, 1)

    def bias(dve, h, u, s):
        nc.vector.tensor_tensor(s[:, u * P:(u + 1) * P], s[:, u * P:(u + 1) * P], tri[:], ALU.add)

    Q = NT // 4
    order = [u for long, short in ((3 * Q, 0), (2 * Q, Q)) for i in range(Q) for u in (long + i, short + i)]

    def s_at(i):
        return 0 if i % 2 == 0 else (4 if order[i] < Q else 3) * BANK

    attention(nc, d, g, ph, GH, kT, k_x, v, load, load_q, 5, lambda u: [(b * P, b) for b in range(u + 1)], 16 * 4 + 1,
              head_tiles(d["y1"], GW), 2, s_at, bias, bias_consts, order, turned_by_scalar=(0, 1), o_bufs=1)


def mem_attention(nc, d, g):
    ph = Phase(nc, "mem")
    kT, v = ph.sb("kT", [P, GH, NMEM], F32R), ph.sb("v", [P, NMEM // P, GW])

    def load(sp, const_in):
        for part in range(2):
            sp.dma_start(raw(kT[part * HD:(part + 1) * HD]), d["mem_kT"][part].rearrange("(h e) t -> e h t", e=HD))\
                .then_inc(const_in, 16)
        sp.dma_start(v[:], d["mem_v"].rearrange("(n p) c -> p n c", p=P)).then_inc(const_in, 16)

    def load_q(sp, h, s, q, q_x, q_in):
        load_twice(sp, q, lambda part: d["qkmT"][part, bass.ds(2 * GW + h * HD, HD), s * HALF * P:(s + 1) * HALF * P], q_in)

    attention(nc, d, g, ph, GH, kT, None, v, load, load_q, 4, lambda u: [(b * P, b) for b in range(NMEM // P)], 16 * 3,
              head_tiles(d["y1"], 3 * GW), 4, lambda i: i % 4 * BANK, turned_by_scalar=(0, 1))


D2 = 512
H2 = D2 // HD
GRID_W = 64
WIN_R, WIN_C = 8, 16
REL_C = 2 * WIN_C - 1
REL_R = 2 * WIN_R - 1
TK2 = T + NMEM


def modulation(nc, d, g, block, ph, p_mod, p_gate, scales_ready):
    sb, sem = ph.sb, ph.sem
    W_BUFS = 4
    w = [sb(f"w{b}", [P, KB, BANK]) for b in range(W_BUFS)]
    cond, cond_x = sb("cond", [P, KB, 2]), sb("cond_x", [P, KB, P])
    b_cols, g_cols, mod, b_gate = sb("b_cols", [P, 2 * KB]), sb("g_cols", [P, KB]), sb("mod", [P, 2 * KB, 2]), sb("b_gate", [P, DM])
    const_in, cond_ready, wide_ready, mod_ready, gate_ready = (
        sem(n) for n in ("const_in", "cond_ready", "wide_ready", "mod_ready", "gate_ready"))
    w_in, w_used = [sem(f"w{b}_in") for b in range(W_BUFS)], sem("w_used")
    CHUNKS, GATE_CHUNKS = 3 * DM // BANK, DM // BANK

    def load_consts(sp):
        for dst, src in ((cond, d["cond"]), (b_cols, d["b_ada_cols"]), (g_cols, d["norm_g2"])):
            sp.dma_start(dst[:], src).then_inc(const_in, 16)
        sp.dma_start(b_gate[:], d["b_ada_gate"].partition_broadcast(P)).then_inc(const_in, 16)

    def load_chunk(sp, c):
        if c >= W_BUFS:
            sp.wait_ge(w_used, c - W_BUFS + 1)
        sp.dma_start(w[c % W_BUFS][:], d["w_ada"].rearrange("(k p) c -> p k c", p=P)[
            :, :, (c - GATE_CHUNKS) % CHUNKS * BANK:((c - GATE_CHUNKS) % CHUNKS + 1) * BANK]).then_inc(w_in[c % W_BUFS], 16)

    def load(sp):
        load_consts(sp)
        for c in range(W_BUFS):
            load_chunk(sp, c)

    def load_rest(sp):
        for c in range(W_BUFS, CHUNKS):
            load_chunk(sp, c)

    @block.scalar
    def _(act):
        act.wait_ge(const_in, 64)
        nc.scalar.activation(cond[:], cond[:], ACT.Silu).then_inc(cond_ready, 1)

    def project(pe):
        pe.wait_ge(cond_ready, 1)
        pe.wait_ge(wide_ready, 1)
        for c in range(GATE_CHUNKS):
            pe.wait_ge(w_in[c % W_BUFS], 16)
            for k in range(KB):
                last = nc.tensor.matmul(p_gate[:, c, :], cond_x[:, k, :], w[c % W_BUFS][:, k, :],
                                        start=(k == 0), stop=(k == KB - 1))
            last.then_inc(w_used, 1)
        pe.drain().then_inc(gate_ready, 1)
        for c in range(GATE_CHUNKS, CHUNKS):
            pe.wait_ge(w_in[c % W_BUFS], 16 * (c // W_BUFS + 1))
            for n in range(BANK // P):
                for k in range(KB):
                    last = nc.tensor.matmul(p_mod[:, (c - GATE_CHUNKS) * (BANK // P) + n, :],
                                            w[c % W_BUFS][:, k, n * P:(n + 1) * P], cond[:, k, :],
                                            start=(k == 0), stop=(k == KB - 1))
        last.then_inc(mod_ready, 1)

    @block.vector
    def _(dve):
        dve.wait_ge(const_in, 64)
        dve.wait_ge(cond_ready, 1)
        nc.vector.tensor_copy(cond_x[:], cond[:, :, 0:1].to_broadcast([P, KB, P])).then_inc(wide_ready, 1)

    def finish(dve):
        dve.wait_ge(gate_ready, 1)
        nc.vector.tensor_tensor(g.gate_x[:], p_gate[:].rearrange("p n c -> p (n c)"), b_gate[:], ALU.add)
        dve.wait_ge(mod_ready, 1)
        nc.vector.tensor_tensor(mod[:], p_mod[:], along(b_cols[:], 2), ALU.add)
        dve.drain()
        for i, (scale, shift) in enumerate(((g.scale_x, g.shift_x), (g.scale_c, g.shift_c))):
            nc.vector.tensor_copy(shift[:], mod[:, 0:KB, i])
            nc.vector.scalar_tensor_tensor(scale[:], mod[:, KB:2 * KB, i], 1.0, g_cols[:], ALU.add, ALU.mult)
        dve.drain().then_inc(scales_ready, 1)
    return load, load_rest, project, finish


def relative_bias(nc, d, block, ph, p_out):
    sb, sem = ph.sb, ph.sem
    R = 33
    HR = H2 * REL_R
    rel, hot, out = sb("rel", [R, HR]), sb("hot", [R, GRID_W, GRID_W]), sb("out", [HR, GRID_W * GRID_W])
    zeroed, rel_in, hot_ready, out_ready, copied, stored = (
        sem(n) for n in ("zeroed", "rel_in", "hot_ready", "out_ready", "copied", "stored"))
    low, high = WIN_C // 2, GRID_W - WIN_C // 2

    def load(sp):
        sp.wait_ge(zeroed, 1)
        sp.dma_start(rel[0:REL_C, :], d["rel_bias"]).then_inc(rel_in, 16)

    def store(sp):
        sp.wait_ge(copied, GRID_W * GRID_W // BANK)
        sp.dma_start(d["rel_table"], out[:]).then_inc(stored, 16)
        sp.wait_ge(stored, 16)

    @block.gpsimd
    def _(pool):
        nc.gpsimd.memset(rel[0:32, :], 0.0)
        pool.drain()
        nc.gpsimd.memset(rel[32:33, :], MASKED)
        pool.drain()
        nc.gpsimd.memset(hot[:], 0.0)
        pool.drain().then_inc(zeroed, 1)
        nc.gpsimd.affine_select(out=hot[0:32], in_=hot[0:32], compare_op=ALU.not_equal, fill=1.0, base=WIN_C - 1,
                                pattern=[[-1, GRID_W], [1, GRID_W]], channel_multiplier=-1)
        pool.drain()
        far = hot[32:33]
        nc.gpsimd.memset(far[:, 0:low, WIN_C:], 1.0)
        pool.drain()
        nc.gpsimd.memset(far[:, high:, 0:GRID_W - WIN_C], 1.0)
        pool.drain()
        mid = far[:, low:high, :]
        for sign in (1, -1):
            nc.gpsimd.affine_select(out=mid, in_=mid, compare_op=ALU.is_ge, fill=1.0,
                                    base=0 if sign > 0 else WIN_C - 1,
                                    pattern=[[-sign, high - low], [sign, GRID_W]], channel_multiplier=0)
            pool.drain()
        pool.drain().then_inc(hot_ready, 1)

    def select(pe):
        pe.wait_ge(rel_in, 16)
        pe.wait_ge(hot_ready, 1)
        flat = hot[:].rearrange("p q k -> p (q k)")
        for n in range(GRID_W * GRID_W // BANK):
            if n >= 2:
                pe.wait_ge(copied, n - 1)
            nc.tensor.matmul(p_out[0:HR, n % 2, :], rel[:], flat[:, n * BANK:(n + 1) * BANK], start=True, stop=True)\
                .then_inc(out_ready, 1)
        pe.wait_ge(copied, GRID_W * GRID_W // BANK)

    def copy(act):
        for n in range(GRID_W * GRID_W // BANK):
            act.wait_ge(out_ready, n + 1)
            nc.scalar.activation(out[:, n * BANK:(n + 1) * BANK], p_out[0:HR, n % 2, :], ACT.Copy).then_inc(copied, 1)
    return load, select, copy, store


def side_inputs(nc, d, g):
    phs = [Phase(nc, n) for n in ("side", "rel", "ada", "mem_kv", "ctx_kv")]
    side, rel, ada, mem_kv, ctx_kv = phs
    mem_scale = side.sb("mem_scale", [P, KB])
    banks = [side.ps(n, shape) for n, shape in (("xT", [P, KB, P]), ("k", [P, BANK]), ("v", [P, BANK]), ("kT", [P, GROUP, P]))]
    p_mod, p_wide = side.ps("mod", [P, 2 * KB, 2]), side.ps("wide", [P, 2, BANK])
    mem_scale_in, scales_ready = side.sem("mem_scale_in"), side.sem("scales_ready")
    with nc.Block() as block:
        @block.scalar
        def _(act):
            act.dma_start(mem_scale[:], d["mem_norm_g"]).then_inc(mem_scale_in, 16)

        load_rel, select_rel, copy_rel, store_rel = relative_bias(nc, d, block, rel, p_wide)
        load_ada, load_ada_rest, project_ada, finish_ada = modulation(nc, d, g, block, ada, p_mod, p_wide, scales_ready)
        load_mem, store_mem = keys_values(nc, g, block, mem_kv, banks, d["mem"], d["mem_w_kv"], GH, d["mem_k_g"], mem_scale,
                                          None, lambda act: act.wait_ge(mem_scale_in, 16), d["mem_kT"], d["mem_v"])

        @block.tensor
        def _(pe):
            select_rel(pe)
            project_ada(pe)

        @block.scalar
        def _(act):
            copy_rel(act)

        @block.vector
        def _(dve):
            finish_ada(dve)

        load_ctx, store_ctx = keys_values(nc, g, block, ctx_kv, banks, d["ctx"], d["ctx_w_kv"], H2, d["ctx_k_g"], g.scale_c,
                                          g.shift_c, lambda act: act.wait_ge(scales_ready, 1), d["ctx_kT"], d["ctx_v"])

        @block.sync
        def _(sp):
            load_rel(sp)
            load_mem(sp)
            load_ada(sp)
            store_mem(sp)
            load_ada_rest(sp)
            load_ctx(sp)
            store_rel(sp)
            store_ctx(sp)
    for ph in phs[::-1]:
        ph.close()


def tile_pass_2(nc, d, g):
    ph = Phase(nc, "p2")
    sb, ps, sem = ph.sb, ph.ps, ph.sem
    MB = 5 * GW // P
    PAIRS = NT // 2
    w_parts = [sb(f"w_{part}", [P, MB, DM], F32R) for part in ("high", "low")]
    staging = [sb(f"staging{b}", [P, DM]) for b in range(2)]
    y, z, mix = sb("y", [P, MB * P]), sb("z", [P, MB, P]), sb("mix", [P, MB, P])
    x = [sb(f"x{b}", [P, DM]) for b in range(2)]
    mix_parts = [[sb(f"mix{b}_{part}", [P, MB, P], F32R) for part in ("high", "low")] for b in range(2)]
    xs, slot = sb("xs", [P, DM]), sb("slot", [P, KB, P])
    x_sq, x_var, x_rstd = sb("x_sq", [P, 1]), sb("x_var", [P, 1]), sb("x_rstd", [P, 1])
    p_y, p_x, p_o = ps("y", [P, 12, P]), ps("x", [P, KB, P]), ps("o", [P, DM])
    w_in, w_high_ready, w_ready = [sem(f"w{b}_in") for b in range(2)], sem("w_high_ready"), sem("w_ready")
    yz_in, slot_stored = sem("yz_in"), sem("slot_stored")
    x_in, gated, high_ready, mix_ready, x1_ready, x1_stored = (
        [sem(f"{n}{b}") for b in range(2)] for n in (
            "x_in", "gated", "high_ready", "mix_ready", "x1_ready", "x1_stored"))
    yT_ready, o_ready, x_sq_ready, x_rstd_ready, xs_ready, xT_ready, x_filled, taken = (
        sem(n) for n in ("yT_ready", "o_ready", "x_sq_ready", "x_rstd_ready", "xs_ready", "xT_ready", "x_filled", "taken"))

    def tiles(eng, tile):
        tile(0, 0, first=True, last=False)
        tile(0, 1, first=False, last=False, second=True)
        with eng.Fori(1, PAIRS - 1) as j:
            for b in range(2):
                tile(j, b, first=False, last=False)
        for b in range(2):
            tile(PAIRS - 1, b, first=False, last=True)

    with nc.Block() as block:
        @block.sync
        def _(sp):
            def load_yz(i):
                sp.dma_start(y[:], tile_of(d["y1"], i)).then_inc(yz_in, 16)
                sp.dma_start(z[:], cols_of(d["z1T"], i)).then_inc(yz_in, 16)

            def load_w(k):
                sp.dma_start(staging[k % 2][:], d["w_out1"][k * P:(k + 1) * P, :]).then_inc(w_in[k % 2], 16)

            def move(i):
                wait_apart(sp, x_filled, i + 1, taken)
                sp.dma_start(cols_of(d["x2T"], i), slot[:]).then_inc(slot_stored, 16)

            def load_x(j, b):
                sp.dma_start(x[b][:], tile_of(d["x"], 2 * j + b)).then_inc(x_in[b], 16)

            def tile(j, b, first, last, second=False):
                i = 2 * j + b
                if not last:
                    sp.wait_ge(gated[1 - b], j + b + 1)
                    load_yz(i + 2)
                sp.wait_ge(x1_ready[b], j + 1)
                sp.dma_start(tile_of(d["x1"], 2 * j + b), x[b][:]).then_inc(x1_stored[b], 16)
                if first:
                    load_x(0, 1)
                elif b == 0:
                    wait_apart(sp, xs_ready, 2 * j, taken)
                    sp.wait_ge(x1_stored[1], 16 * j)
                    load_x(j, 1)
                elif not last:
                    wait_apart(sp, xs_ready, 2 * j + 1, taken)
                    sp.wait_ge(x1_stored[0], 16 * (j + 1))
                    load_x(j + 1, 0)
                if not first:
                    move(i - 1)

            sp.sem_inc(slot_stored, 16)
            load_yz(0)
            for k in range(2):
                load_w(k)
            load_x(0, 0)
            sp.wait_ge(gated[0], 1)
            load_yz(1)
            for k in range(2, MB):
                sp.wait_ge(w_ready, k - 1)
                load_w(k)
            tiles(sp, tile)
            move(NT - 1)
            sp.wait_ge(slot_stored, 16 * (NT + 1))
            for b in range(2):
                sp.wait_ge(x1_stored[b], 16 * PAIRS)

        @block.tensor
        def _(pe):
            def turn_y(j, b, first=False):
                pe.wait_ge(yz_in, 32 * (2 * j + b + 1))
                if not first:
                    pe.wait_ge(gated[1 - b], j + b)
                for k in range(MB):
                    last = nc.tensor.transpose(p_y[:, k, :], y[:, k * P:(k + 1) * P], g.ident[:])
                last.then_inc(yT_ready, 1)

            def turn_x(i, first=False):
                pe.wait_ge(xs_ready, i + 1)
                if not first:
                    pe.wait_ge(x_filled, i)
                for k in range(KB):
                    last = nc.tensor.transpose(p_x[:, k, :], xs[:, k * P:(k + 1) * P], g.ident[:])
                last.then_inc(xT_ready, 1)

            def tile(j, b, first, last, second=False):
                pe.wait_ge(mix_ready[b], j + 1)
                if not first:
                    pe.wait_ge(x1_ready[1 - b], j + b)
                for n in range(DM // BANK):
                    for k in range(MB):
                        pe.wait_ge(w_ready, k + 1)
                        for i, (w_part, x_part) in enumerate(PASSES):
                            end = nc.tensor.matmul(p_o[:, n * BANK:(n + 1) * BANK], mix_parts[b][x_part][:, k, :],
                                                   w_parts[w_part][:, k, n * BANK:(n + 1) * BANK],
                                                   start=(k == 0 and i == 0), stop=(k == MB - 1 and i == len(PASSES) - 1))
                end.then_inc(o_ready, 1)
                if not last:
                    turn_y(j + 1, b)
                if not first:
                    turn_x(2 * j + b - 1, first=second)

            turn_y(0, 0, first=True)
            turn_y(0, 1)
            tiles(pe, tile)
            turn_x(NT - 1)

        @block.scalar
        def _(act):
            def high(j, b):
                act.wait_ge(gated[b], j + 1)
                nc.scalar.activation(mix_parts[b][0][:], mix[:], ACT.Copy).then_inc(high_ready[b], 1)

            def fill(i):
                act.wait_ge(xT_ready, i + 1)
                act.wait_ge(slot_stored, 16 * (i + 1))
                for k in range(KB):
                    nc.scalar.activation(slot[:, k, :], p_x[:, k, :], ACT.Identity, scale=g.scale_x[:, k:k + 1],
                                         bias=g.shift_x[:, k:k + 1])
                act.drain().then_inc(x_filled, 1)

            def tile(j, b, first, last, second=False):
                i = 2 * j + b
                act.wait_ge(x1_ready[b], j + 1)
                if not first:
                    act.wait_ge(xT_ready, i)
                nc.scalar.activation(xs[:], x[b][:], ACT.Square, scale=DM ** -0.5, accum_out=x_sq[:]).then_inc(x_sq_ready, 1)
                if not last:
                    high(j + 1, b)
                if not first:
                    fill(i - 1)

            for b in range(2):
                high(0, b)
            for k in range(MB):
                act.wait_ge(w_in[k % 2], 16 * (k // 2 + 1))
                nc.scalar.activation(w_parts[0][:, k], staging[k % 2][:], ACT.Copy).then_inc(w_high_ready, 1)
            tiles(act, tile)
            fill(NT - 1)

        @block.gpsimd
        def _(pool):
            def low(j, b):
                pool.wait_ge(high_ready[b], j + 1)
                nc.gpsimd.tensor_tensor(mix_parts[b][1][:], mix[:], mix_parts[b][0][:], ALU.subtract).then_inc(mix_ready[b], 1)

            def tile(j, b, first, last, second=False):
                pool.wait_ge(x_sq_ready, 2 * j + b + 1)
                nc.gpsimd.tensor_tensor(x_var[:], x_sq[:], g.eps[:], ALU.add)
                pool.drain()
                nc.gpsimd.tensor_tensor(x_rstd[:], x_var[:], g.neg_half[:], ALU.pow).then_inc(x_rstd_ready, 1)
                if not last:
                    low(j + 1, b)

            for b in range(2):
                low(0, b)
            for k in range(MB):
                pool.wait_ge(w_high_ready, k + 1)
                nc.gpsimd.tensor_tensor(w_parts[1][:, k], staging[k % 2][:], w_parts[0][:, k], ALU.subtract).then_inc(w_ready, 1)
            tiles(pool, tile)

        @block.vector
        def _(dve):
            def gate(j, b, first=False):
                dve.wait_ge(yT_ready, 2 * j + b + 1)
                if not first:
                    dve.wait_ge(mix_ready[1 - b], j + b)
                nc.vector.tensor_tensor(mix[:], p_y[:, 0:MB, :], z[:], ALU.mult).then_inc(gated[b], 1)

            def tile(j, b, first, last, second=False):
                i = 2 * j + b
                dve.wait_ge(o_ready, i + 1)
                dve.wait_ge(x_in[b], 16 * (j + 1))
                nc.vector.tensor_tensor(x[b][:], p_o[:], x[b][:], ALU.add).then_inc(x1_ready[b], 1)
                if not last:
                    gate(j + 1, b)
                dve.wait_ge(x_rstd_ready, i + 1)
                nc.vector.tensor_scalar(xs[:], x[b][:], x_rstd[:], None, ALU.mult).then_inc(xs_ready, 1)

            gate(0, 0, first=True)
            gate(0, 1)
            tiles(dve, tile)
    ph.close()


def feature_pass_2(nc, d, g):
    ph = Phase(nc, "f2")
    sb, ps, sem = ph.sb, ph.ps, ph.sem
    row = [sb(f"row{b}", [P, T]) for b in range(2)]
    work = [sb(f"work{b}", [P, T]) for b in range(2)]
    fp = FeaturePass(ph, [*row, *work])
    high = sb("high", [P, T], F32R)
    ones, gain = sb("ones", [P, P]), sb("gain", [P, 2])
    const_in, ones_ready, v_ready, high_stored = sem("const_in"), sem("ones_ready"), sem("v_ready"), sem("high_stored")
    sq_ready, sum_ready, rms_ready, high_ready, qk_ready, qk_stored, vT_ready, v_turned, v_out, v_stored, out_ready, stored = (
        [sem(f"{n}{b}") for b in range(2)] for n in (
            "sq_ready", "sum_ready", "rms_ready", "high_ready", "qk_ready", "qk_stored", "vT_ready", "v_turned", "v_out",
            "v_stored", "out_ready", "stored"))
    QK, V, IN, GATE = (n // P // 2 for n in (2 * D2, D2, D2, 2 * D2))
    FIRST_V, FIRST_IN, FIRST_GATE, PAIRS = QK, QK + V, QK + V + IN, QK + V + IN + GATE

    def rows_of(dram, block):
        return dram[bass.ds(block * P, P), :]

    with nc.Block() as block:
        @block.sync
        def _(sp):
            def next_pair(j):
                for b in range(2):
                    sp.wait_ge(fp.w_ready[b], j + 1)
                    fp.load(sp, d["w_fm2"], j + 1, b)

            def store(j, b, dst):
                sp.wait_ge(out_ready[b], j - FIRST_IN + 1)
                sp.dma_start(dst, row[b][:]).then_inc(stored[b], 16)

            sp.dma_start(gain[:], d["qk_gain2"]).then_inc(const_in, 16)
            sp.sem_inc(high_stored, 16)
            for b in range(2):
                fp.load(sp, d["w_fm2"], 0, b)
                for s in (qk_stored[b], v_stored[b], stored[b]):
                    sp.sem_inc(s, 16)
            fp.load_input(sp, d["x2T"])
            with sp.Fori(0, FIRST_V) as j:
                next_pair(j)
                for b in range(2):
                    sp.wait_ge(high_ready[b], j + 1)
                    sp.dma_start(rows_of(d["qk2T"][0], 2 * j + b), raw(high[:])).then_inc(high_stored, 16)
                    sp.wait_ge(qk_ready[b], j + 1)
                    sp.dma_start(rows_of(d["qk2T"][1], 2 * j + b), row[b][:]).then_inc(qk_stored[b], 16)
            with sp.Fori(FIRST_V, FIRST_IN) as j:
                next_pair(j)
                for b in range(2):
                    sp.wait_ge(v_out[b], j - FIRST_V + 1)
                    sp.dma_start(d["v2"].rearrange("(n p) c -> p n c", p=P)[:, :, bass.ds((2 * (j - FIRST_V) + b) * P, P)],
                                 work[b][:].rearrange("p (n c) -> p n c", c=P)).then_inc(v_stored[b], 16)
            with sp.Fori(FIRST_IN, FIRST_GATE) as j:
                next_pair(j)
                for b in range(2):
                    store(j, b, rows_of(d["f_inT"], 2 * (j - FIRST_IN) + b))
            with sp.Fori(FIRST_GATE, PAIRS - 1) as j:
                next_pair(j)
                for b in range(2):
                    store(j, b, rows_of(d["z2T"], 2 * (j - FIRST_GATE) + b))
            for b in range(2):
                store(PAIRS - 1, b, rows_of(d["z2T"], 2 * (GATE - 1) + b))
            sp.wait_ge(high_stored, 16 * (2 * QK + 1))
            for b in range(2):
                sp.wait_ge(qk_stored[b], 16 * (QK + 1))
                sp.wait_ge(v_stored[b], 16 * (V + 1))
                sp.wait_ge(stored[b], 16 * (IN + GATE + 1))

        @block.tensor
        def _(pe):
            def project(j, b):
                fp.project(nc, pe, j, b)

            def sums(j, b):
                pe.wait_ge(sq_ready[b], j + 1)
                for c in range(0, T, BANK):
                    last = nc.tensor.matmul(fp.p_out[b][:, c:c + BANK], ones[:], work[b][:, c:c + BANK], start=True, stop=True)
                last.then_inc(sum_ready[b], 1)

            def turn_v(j, b):
                pe.wait_ge(vT_ready[b], j - FIRST_V + 1)
                for n in range(NT):
                    last = nc.tensor.transpose(fp.p_out[b][:, n * P:(n + 1) * P], row[b][:, n * P:(n + 1) * P], g.ident[:])
                last.then_inc(v_turned[b], 1)

            def pairs(first, end, second):
                with pe.Fori(first, end) as j:
                    project(j, 1)
                    second(j, 0)
                    project(j + 1, 0)
                    second(j, 1)

            pe.wait_ge(ones_ready, 1)
            project(0, 0)
            pairs(0, FIRST_V, sums)
            pairs(FIRST_V, FIRST_IN, turn_v)
            project(FIRST_IN, 1)
            with pe.Fori(FIRST_IN + 1, PAIRS) as j:
                for b in range(2):
                    project(j, b)

        @block.gpsimd
        def _(pool):
            same_head(nc, pool, ones)
            pool.drain().then_inc(ones_ready, 1)
            for b in range(2):
                fp.split_weights(nc, pool, 0, b, first=True)
            with pool.Fori(1, PAIRS) as j:
                for b in range(2):
                    fp.split_weights(nc, pool, j, b)

        @block.scalar
        def _(act):
            def empty_qk(j, b):
                act.wait_ge(fp.p_ready[b], j + 1)
                act.wait_ge(qk_stored[b], 16 * (j + 1))
                nc.scalar.activation(row[b][:], fp.p_out[b][:], ACT.Copy)
                nc.scalar.activation(work[b][:], fp.p_out[b][:], ACT.Square)
                act.drain().then_inc(sq_ready[b], 1)

            def rms(j, b):
                act.wait_ge(sum_ready[b], j + 1)
                nc.scalar.activation(work[b][:], fp.p_out[b][:], ACT.Sqrt, scale=1.0 / HD, bias=g.eps[:]).then_inc(rms_ready[b], 1)
                act.drain().then_inc(fp.p_free[b], 1)

            def empty_v(j, b):
                act.wait_ge(fp.p_ready[b], j + 1)
                act.wait_ge(qk_stored[b], 16 * (QK + 1))
                nc.scalar.activation(row[b][:], fp.p_out[b][:], ACT.Copy).then_inc(vT_ready[b], 1)

            for b in range(2):
                act.sem_inc(fp.p_free[b], 1)
            fp.round_input(nc, act)
            empty_qk(0, 0)
            with act.Fori(0, FIRST_V - 1) as j:
                empty_qk(j, 1)
                rms(j, 0)
                empty_qk(j + 1, 0)
                rms(j, 1)
            empty_qk(FIRST_V - 1, 1)
            rms(FIRST_V - 1, 0)
            empty_v(FIRST_V, 0)
            rms(FIRST_V - 1, 1)
            empty_v(FIRST_V, 1)
            with act.Fori(FIRST_V + 1, FIRST_IN) as j:
                for b in range(2):
                    empty_v(j, b)
            for first, end, func in ((FIRST_IN, FIRST_GATE, ACT.Copy), (FIRST_GATE, PAIRS, ACT.Silu)):
                with act.Fori(first, end) as j:
                    for b in range(2):
                        act.wait_ge(fp.p_ready[b], j + 1)
                        act.wait_ge(stored[b], 16 * (j - FIRST_IN + 1))
                        nc.scalar.activation(row[b][:], fp.p_out[b][:], func).then_inc(out_ready[b], 1)
                        act.drain().then_inc(fp.p_free[b], 1)

        @block.vector
        def _(dve):
            def norm(j, b, is_key):
                dve.wait_ge(rms_ready[b], j + 1)
                nc.vector.reciprocal(work[b][:], work[b][:])
                dve.drain()
                nc.vector.scalar_tensor_tensor(row[b][:], row[b][:], gain[:, is_key:is_key + 1], work[b][:], ALU.mult, ALU.mult)
                dve.drain()
                dve.wait_ge(high_stored, 16 * (2 * j + b + 1))
                nc.vector.tensor_copy(high[:], row[b][:]).then_inc(high_ready[b], 1)
                dve.drain()
                nc.vector.tensor_tensor(row[b][:].bitcast(F32R), row[b][:], high[:], ALU.subtract).then_inc(qk_ready[b], 1)

            fp.rest_of_input(nc, dve)
            dve.wait_ge(const_in, 16)
            nc.vector.tensor_scalar(gain[:, 0:1], gain[:, 0:1], HD ** -0.5, None, ALU.mult)
            dve.drain()
            for first, end, is_key in ((0, FIRST_V // 2, 0), (FIRST_V // 2, FIRST_V, 1)):
                with dve.Fori(first, end) as j:
                    for b in range(2):
                        norm(j, b, is_key)
            with dve.Fori(FIRST_V, FIRST_IN) as j:
                for b in range(2):
                    dve.wait_ge(v_turned[b], j - FIRST_V + 1)
                    dve.wait_ge(v_stored[b], 16 * (j - FIRST_V + 1))
                    nc.vector.tensor_copy(work[b][:], fp.p_out[b][:]).then_inc(v_out[b], 1)
                    dve.drain().then_inc(fp.p_free[b], 1)
    ph.close()


RADIX = 4
TF = T // RADIX
NF_T = TF // P
FG = 4
FK = D2 // P


def fourier(nc, d, g, tables):
    ph = Phase(nc, "four")
    sb, ps, sem = ph.sb, ph.ps, ph.sem
    u = sb("u", [P, FK, T])
    ch = sb("ch", [P, 2, P])
    w4, wcs = sb("w4", [P, FK, D2]), sb("wcs", [P, 2, FK, D2])
    e0, e1 = sb("e0", [P, FK, P]), sb("e1", [P, FK, P])
    fold = sb("fold", [P, 4, FK, P])
    d1w = sb("d1w", [P, 2, D2])
    zz = sb("zz", [P, NF_T, RADIX, 2, D2])
    cs = [sb(f"cs{b}", [P, NF_T, 2, P]) for b in range(2)]
    out = [sb(f"out{b}", [P, D2]) for b in range(2)]
    p_b = [ps(f"b{n}", [P, BANK]) for n in range(8)]
    names = ("const_in", "u_in", "w_ready", "w_copied", "fold_ready", "f_ready", "s_copied", "d1_copied", "d_done", "y_ready",
             "y_out")
    const_in, u_in, w_ready, w_copied, fold_ready, f_ready, s_copied, d1_copied, d_done, y_ready, y_out = (sem(n) for n in names)
    tables_blank, tables_in = sem("tables_blank"), sem("tables_in")
    cs_in, out_ready, stored = ([sem(f"{n}{b}") for b in range(2)] for n in ("cs_in", "out_ready", "stored"))

    with nc.Block() as block:
        @block.sync
        def _(sp):
            sp.dma_start(ch[:], d["dft_channels"]).then_inc(const_in, 16)
            sp.dma_start(w4[:], d["w_four"].rearrange("(k p) c -> p k c", p=P)).then_inc(const_in, 16)
            sp.dma_start(u[:], d["f_inT"].rearrange("(k p) t -> p k t", p=P)).then_inc(u_in, 16)
            for b in range(2):
                sp.sem_inc(stored[b], 16)

            def load(j, m):
                sp.dma_start(cs[m % 2][:].rearrange("p n s m -> p (n s m)"),
                             d["dft_tokens"][bass.ds(j * NF_T + m, 1)].rearrange("a p c -> (a p) c")).then_inc(cs_in[m % 2], 16)

            load(0, 0)
            load(0, 1)
            sp.wait_ge(tables_blank, 1)
            load_bias_tables(sp, d, tables, tables_in)

            def turn(j, m, more):
                if more:
                    sp.wait_ge(y_ready, NF_T * j + m + 1)
                    load(j + (m + 2) // NF_T, (m + 2) % NF_T)
                sp.wait_ge(out_ready[m % 2], NF_T // 2 * j + m // 2 + 1)
                sp.dma_start(d["y2"].rearrange("(m j) c -> j m c", j=RADIX)[bass.ds(j, 1), m * P:(m + 1) * P, 0:D2]
                             .rearrange("a m c -> (a m) c"), out[m % 2][:]).then_inc(stored[m % 2], 16)

            with sp.Fori(0, RADIX - 1) as j:
                for m in range(NF_T):
                    turn(j, m, True)
            for m in range(NF_T):
                turn(RADIX - 1, m, m + 2 < NF_T)
            sp.wait_ge(tables_in, 16 * 4 * H2)
            for b in range(2):
                sp.wait_ge(stored[b], 16 * (RADIX * NF_T // 2 + 1))

        @block.gpsimd
        def _(pool):
            nc.gpsimd.memset(tables[0][:], MASKED).then_inc(tables_blank, 1)

        @block.tensor
        def _(pe):
            pe.wait_ge(const_in, 32)
            for i in range(2):
                for k in range(FK):
                    last = nc.tensor.matmul(p_b[i * FK + k][:], ch[:, i, :], w4[:, k, :], start=True, stop=True)
            last.then_inc(w_ready, 1)
            pe.wait_ge(w_copied, 1)

            def fold_products(n):
                pe.wait_ge(fold_ready, n + 1)
                pe.wait_ge(d_done, n + 1)
                for f in range(4):
                    for i in range(2):
                        for k in range(FK):
                            last = nc.tensor.matmul(p_b[2 * f + i][:], fold[:, f, k, :], wcs[:, i, k, :],
                                                    start=(k == 0), stop=(k == FK - 1))
                        last.then_inc(f_ready, 1)

            with pe.Fori(0, NF_T) as n:
                fold_products(n)
            pe.wait_ge(s_copied, NF_T)
            pe.wait_ge(d_done, NF_T + 1)
            with pe.Fori(0, RADIX) as j:
                for m in range(NF_T):
                    pe.wait_ge(cs_in[m % 2], 16 * (NF_T // 2 * j + m // 2 + 1))
                    pe.wait_ge(y_out, NF_T * j + m + 1)
                    for n in range(NF_T):
                        for i in range(2):
                            last = nc.tensor.matmul(p_b[m % 2][:], cs[m % 2][:, n, i, :],
                                                    zz[:, n, bass.ds(j, 1), i, :].rearrange("p a c -> p (a c)"),
                                                    start=(n == 0 and i == 0), stop=(n == NF_T - 1 and i == 1))
                    last.then_inc(y_ready, 1)

        @block.scalar
        def _(act):
            act.wait_ge(w_ready, 1)
            for i in range(2):
                for k in range(FK):
                    nc.scalar.activation(wcs[:, i, k, :], p_b[i * FK + k][:], ACT.Copy)
            act.drain().then_inc(w_copied, 1)
            with act.Fori(0, NF_T) as n:
                for f in range(2):
                    for i in range(2):
                        act.wait_ge(f_ready, 8 * n + 2 * f + i + 1)
                        nc.scalar.activation(zz[:, bass.ds(n, 1), 2 * f, i, :].rearrange("p a c -> p (a c)"), p_b[2 * f + i][:], ACT.Copy)
                act.drain().then_inc(s_copied, 1)
                act.wait_ge(f_ready, 8 * (n + 1))
                act.wait_ge(d_done, n + 1)
                for i in range(2):
                    nc.scalar.activation(d1w[:, i, :], p_b[6 + i][:], ACT.Copy)
                act.drain().then_inc(d1_copied, 1)
            act.sem_inc(y_out, 2)
            with act.Fori(0, RADIX) as j:
                for m in range(NF_T):
                    act.wait_ge(y_ready, NF_T * j + m + 1)
                    act.wait_ge(stored[m % 2], 16 * (NF_T // 2 * j + m // 2 + 1))
                    nc.scalar.activation(out[m % 2][:], p_b[m % 2][:], ACT.Copy).then_inc(out_ready[m % 2], 1)
                    act.drain().then_inc(y_out, 1)

        @block.vector
        def _(dve):
            dve.wait_ge(u_in, 16)
            dve.sem_inc(d_done, 1)
            with dve.Fori(0, NF_T) as n:
                q = [u[:, :, bass.ds(i * TF + n * P, P)] for i in range(RADIX)]
                nc.vector.tensor_tensor(e0[:], q[0], q[2], ALU.add)
                nc.vector.tensor_tensor(e1[:], q[1], q[3], ALU.add)
                nc.vector.tensor_tensor(fold[:, 2], q[0], q[2], ALU.subtract)
                nc.vector.tensor_tensor(fold[:, 3], q[1], q[3], ALU.subtract)
                dve.drain()
                nc.vector.tensor_tensor(fold[:, 0], e0[:], e1[:], ALU.add)
                nc.vector.tensor_tensor(fold[:, 1], e0[:], e1[:], ALU.subtract)
                dve.drain().then_inc(fold_ready, 1)
                dve.wait_ge(d1_copied, n + 1)
                for residue, at_c, at_s in ((1, ALU.subtract, ALU.add), (3, ALU.add, ALU.subtract)):
                    for i, op in enumerate((at_c, at_s)):
                        nc.vector.tensor_tensor(zz[:, bass.ds(n, 1), residue, i, :].rearrange("p a c -> p (a c)"), p_b[4 + i][:],
                                                d1w[:, 1 - i, :], op)
                dve.drain().then_inc(d_done, 1)
    ph.close()


SPAN = 10
EDGE = REL_R - 1


def load_bias_tables(sp, d, tables, tables_in):
    inner, edge = tables
    table = d["rel_table"].rearrange("(h r) (q k) -> q h r k", r=REL_R, k=GRID_W)
    for e in range(2):
        at = slice(e * GRID_W, (e + 1) * GRID_W)
        for h in range(H2):
            sp.dma_start(inner[at, h, e:e + WIN_R, :], table[:, h, 3:3 + WIN_R, :]).then_inc(tables_in, 16)
            sp.dma_start(edge[at, h, :, :], table[:, h, 1 - e:1 - e + EDGE, :]).then_inc(tables_in, 16)


def neighbourhood(nc, d, g, tables):
    ph = Phase(nc, "nbr")
    kT, v = ph.sb("kT", [P, H2, TK2], F32R), ph.sb("v", [P, TK2 // P, D2])
    inner, edge = tables
    first_inner, last_inner = 2, NT - 3
    win = WIN_R * GRID_W // P

    def key_cols(u):
        if u < first_inner:
            local = range(win)
        elif u > last_inner:
            local = range(NT - win, NT)
        else:
            local = range(u - 2, u - 2 + SPAN * GRID_W // P)
        return [(b * P, b) for b in [*local, *range(NT, TK2 // P)]]

    def load(sp, const_in):
        for part in range(2):
            at = slice(part * HD, (part + 1) * HD)
            sp.dma_start(raw(kT[at, :, 0:T]), d["qk2T"][part, D2:2 * D2].rearrange("(h e) t -> e h t", e=HD)).then_inc(const_in, 16)
            sp.dma_start(raw(kT[at, :, T:TK2]), d["ctx_kT"][part].rearrange("(h e) t -> e h t", e=HD)).then_inc(const_in, 16)
        sp.dma_start(v[:, 0:NT, :], d["v2"].rearrange("(n p) c -> p n c", p=P)).then_inc(const_in, 16)
        sp.dma_start(v[:, NT:, :], d["ctx_v"].rearrange("(n p) c -> p n c", p=P)).then_inc(const_in, 16)

    def load_q(sp, h, s, q, q_x, q_in):
        load_twice(sp, q, lambda part: d["qk2T"][part, bass.ds(h * HD, HD), s * HALF * P:(s + 1) * HALF * P], q_in)

    def bias(dve, h, u, s):
        if first_inner <= u <= last_inner:
            n, table = SPAN * GRID_W, inner[:, bass.ds(h, 1)]
        else:
            top = 0 if u < first_inner else 2 * NT - WIN_R
            j = top - 2 * u + WIN_R - 1 - 1
            n, table = WIN_R * GRID_W, edge[:, bass.ds(h, 1), j:j + WIN_R, :]
        nc.vector.tensor_tensor(s[:, 0:n], s[:, 0:n], table.rearrange("p a r k -> p (a r k)"), ALU.add)

    attention(nc, d, g, ph, H2, kT, None, v, load, load_q, 4, key_cols, 16 * 6, head_tiles(d["y2"], D2), 2,
              lambda i: i % 2 * 2 * BANK, bias, turned_by_scalar=(0, 1))


def final_pass(nc, d, g):
    ph = Phase(nc, "fin")
    sb, ps, sem = ph.sb, ph.ps, ph.sem
    w = sb("w", [P, KB, DM])
    w_parts = [sb(f"w_{part}", [P, KB, DM], F32R) for part in ("high", "low")]
    y, z, x1, mix, out = ([sb(f"{n}{b}", shape) for b in range(2)] for n, shape in
                          (("y", [P, DM]), ("z", [P, KB, P]), ("x1", [P, DM]), ("mix", [P, KB, P]), ("out", [P, DM])))
    mix_parts = [[sb(f"mix{b}_{part}", [P, KB, P], F32R) for part in ("high", "low")] for b in range(2)]
    scaled = [sb(f"scaled{b}", [P, DM]) for b in range(2)]
    p_t = [ps(f"t{b}", [P, KB, P]) for b in range(2)]
    p_o = [ps(f"o{b}", [P, DM]) for b in range(2)]
    const_in, w_high_ready, w_ready = sem("const_in"), sem("w_high_ready"), sem("w_ready")
    yz_in, x1_in, t_ready, gated, high_ready, mix_ready, o_ready, out_ready, stored = (
        [sem(f"{n}{b}") for b in range(2)] for n in (
            "yz_in", "x1_in", "t_ready", "gated", "high_ready", "mix_ready", "o_ready", "out_ready", "stored"))
    PAIRS = NT // 2

    with nc.Block() as block:
        @block.sync
        def _(sp):
            def load_yz(j, b):
                sp.dma_start(y[b][:], tile_of(d["y2"], 2 * j + b)).then_inc(yz_in[b], 16)
                sp.dma_start(z[b][:], cols_of(d["z2T"], 2 * j + b)).then_inc(yz_in[b], 16)

            def load_x1(j, b):
                sp.dma_start(x1[b][:], tile_of(d["x1"], 2 * j + b)).then_inc(x1_in[b], 16)

            def next_yz(j, b):
                sp.wait_ge(gated[b], j + 1)
                load_yz(j + 1, b)

            def store(j, b):
                sp.wait_ge(out_ready[b], j + 1)
                sp.dma_start(tile_of(d["out"], 2 * j + b), out[b][:]).then_inc(stored[b], 16)

            for b in range(2):
                sp.sem_inc(stored[b], 16)
                load_yz(0, b)
            for k in range(KB):
                sp.dma_start(w[:, k, :], d["w_out2"][k * P:(k + 1) * P, :]).then_inc(const_in, 16)
            for b in range(2):
                load_x1(0, b)
            next_yz(0, 0)
            with sp.Fori(0, PAIRS - 2) as j:
                next_yz(j, 1)
                store(j, 0)
                load_x1(j + 1, 0)
                next_yz(j + 1, 0)
                store(j, 1)
                load_x1(j + 1, 1)
            next_yz(PAIRS - 2, 1)
            for b in range(2):
                store(PAIRS - 2, b)
                load_x1(PAIRS - 1, b)
            for b in range(2):
                store(PAIRS - 1, b)
            for b in range(2):
                sp.wait_ge(stored[b], 16 * (PAIRS + 1))

        @block.tensor
        def _(pe):
            def turn(j, b):
                pe.wait_ge(yz_in[b], 32 * (j + 1))
                for k in range(KB):
                    last = nc.tensor.transpose(p_t[b][:, k, :], y[b][:, k * P:(k + 1) * P], g.ident[:])
                last.then_inc(t_ready[b], 1)

            def project(j, b):
                pe.wait_ge(mix_ready[b], j + 1)
                for n in range(DM // BANK):
                    for k in range(KB):
                        pe.wait_ge(w_ready, k + 1)
                        for i, (w_part, x_part) in enumerate(PASSES):
                            last = nc.tensor.matmul(p_o[b][:, n * BANK:(n + 1) * BANK], mix_parts[b][x_part][:, k, :],
                                                    w_parts[w_part][:, k, n * BANK:(n + 1) * BANK],
                                                    start=(k == 0 and i == 0), stop=(k == KB - 1 and i == len(PASSES) - 1))
                last.then_inc(o_ready[b], 1)

            turn(0, 0)
            with pe.Fori(0, PAIRS - 1) as j:
                turn(j, 1)
                project(j, 0)
                turn(j + 1, 0)
                project(j, 1)
            turn(PAIRS - 1, 1)
            project(PAIRS - 1, 0)
            project(PAIRS - 1, 1)

        def halves(eng, part):
            with eng.Fori(0, PAIRS) as j:
                for b in range(2):
                    part(j, b)

        @block.scalar
        def _(act):
            def high(j, b):
                act.wait_ge(gated[b], j + 1)
                nc.scalar.activation(mix_parts[b][0][:], mix[b][:], ACT.Copy).then_inc(high_ready[b], 1)

            act.wait_ge(const_in, 16 * KB)
            for k in range(KB):
                nc.scalar.activation(w_parts[0][:, k], w[:, k], ACT.Copy).then_inc(w_high_ready, 1)
            halves(act, high)

        @block.gpsimd
        def _(pool):
            def low(j, b):
                pool.wait_ge(high_ready[b], j + 1)
                nc.gpsimd.tensor_tensor(mix_parts[b][1][:], mix[b][:], mix_parts[b][0][:], ALU.subtract).then_inc(mix_ready[b], 1)

            for k in range(KB):
                pool.wait_ge(w_high_ready, k + 1)
                nc.gpsimd.tensor_tensor(w_parts[1][:, k], w[:, k], w_parts[0][:, k], ALU.subtract).then_inc(w_ready, 1)
            halves(pool, low)

        @block.vector
        def _(dve):
            def gate(j, b):
                dve.wait_ge(t_ready[b], j + 1)
                nc.vector.tensor_tensor(mix[b][:], p_t[b][:], z[b][:], ALU.mult).then_inc(gated[b], 1)

            def residual(j, b):
                dve.wait_ge(o_ready[b], j + 1)
                nc.vector.tensor_tensor(scaled[b][:], p_o[b][:], g.gate_x[:], ALU.mult)
                dve.drain()
                dve.wait_ge(stored[b], 16 * (j + 1))
                dve.wait_ge(x1_in[b], 16 * (j + 1))
                nc.vector.tensor_tensor(out[b][:], scaled[b][:], x1[b][:], ALU.add).then_inc(out_ready[b], 1)

            gate(0, 0)
            with dve.Fori(0, PAIRS - 1) as j:
                gate(j, 1)
                residual(j, 0)
                gate(j + 1, 0)
                residual(j, 1)
            gate(PAIRS - 1, 1)
            residual(PAIRS - 1, 0)
            residual(PAIRS - 1, 1)
    ph.close()


def mlstm(nc, d, g):
    ph = Phase(nc, "mlstm")
    sb, ps, sem = ph.sb, ph.ps, ph.sem
    VW = HD + 1
    NB = GW // P
    qk = [sb(f"qk{b}", [P, 2 * NB, P]) for b in range(2)]
    va = [sb(f"va{b}", [P, GH, VW]) for b in range(2)]
    o_in = [sb(f"o{b}", [P, GW]) for b in range(2)]
    rows = [sb(f"rows{b}", [4 * GH, P]) for b in range(2)]
    k_pad = sb("k_pad", [P, GH, P])
    sel = sb("sel", [GH, GH, P])
    past = sb("past", [P, P])
    run_max, carry_row = sb("run_max", [GH, T]), sb("carry_row", [GH, NT])
    carry = sb("carry", [P, GH, NT])
    cols = sb("cols", [P, 4 * GH])
    kw = sb("kw", [P, GW])
    arg, e, sm = sb("arg", [P, GH, P]), sb("e", [P, GH, P]), sb("sm", [P, GH, P])
    state = sb("state", [P, NB, 2 * VW])
    nd, nd2 = sb("nd", [P, GH, VW]), sb("nd2", [P, GH, VW])
    den, den2, inv = sb("den", [P, GH]), sb("den2", [P, GH]), sb("inv", [P, GH])
    gate, gate2, h1, h2, y_out = sb("gate", [P, GW]), sb("gate2", [P, GW]), sb("h1", [P, GW]), sb("h2", [P, GW]), sb("y", [P, GW])
    o_gate, h_tmp = sb("o_gate", [P, GW]), sb("h_tmp", [P, GW])
    h_sq, h_var, h_rstd, gain = sb("h_sq", [P, GH]), sb("h_var", [P, GH]), sb("h_rstd", [P, GH]), sb("gain", [P, GW])
    p_t, p_st, p_max = ps("t", [P, BANK]), ps("st", [P, GH, P]), ps("max", [P, GH, P])
    p_num, p_inter, p_state = ps("num", [P, BANK]), ps("inter", [P, BANK]), ps("state", [P, BANK])
    const_in, zeroed, sel_ready, carry_ready = (sem(n) for n in ("const_in", "zeroed", "sel_ready", "carry_ready"))
    slot_in = [sem(f"slot{b}_in") for b in range(2)]
    names = ("pe_done", "o_used", "pad_ready", "t_ready", "cols_ready", "st_ready", "max_ready", "arg_ready", "e_ready",
             "mask_ready", "sm_ready", "kw_ready", "num_ready", "inter_ready", "state_out", "state_ready", "nd_done",
             "gate_in", "gate_ready", "gate_free", "h_sq_ready", "h_rstd_ready", "h_in", "y_ready", "y_stored")
    (pe_done, o_used, pad_ready, t_ready, cols_ready, st_ready, max_ready, arg_ready, e_ready, mask_ready, sm_ready,
     kw_ready, num_ready, inter_ready, state_out, state_ready, nd_done, gate_in, gate_ready, gate_free, h_sq_ready, h_rstd_ready,
     h_in, y_ready, y_stored) = (sem(n) for n in names)
    LOADS = 4

    def pairs(eng, chunk):
        with eng.Fori(0, NT // 2) as j:
            for b in range(2):
                chunk(2 * j + b, b, j)

    with nc.Block() as block:
        @block.sync
        def _(sp):
            def load(c, b):
                sp.dma_start(qk[b][:], cols_of(d["mlstm_qkT"], c)).then_inc(slot_in[b], 16)
                sp.dma_start(va[b][:, :, 0:HD], heads(tile_of(d["mlstm_vo"], c)[:, 0:GW])).then_inc(slot_in[b], 16)
                sp.dma_start(o_in[b][:], tile_of(d["mlstm_vo"], c)[:, GW:2 * GW]).then_inc(slot_in[b], 16)
                sp.dma_start(rows[b][:], d["mlstm_rows"][:, bass.ds(c * P, P)]).then_inc(slot_in[b], 16)

            def store(c):
                sp.wait_ge(y_ready, c + 1)
                sp.dma_start(tile_of(d["y1"], c)[:, 2 * GW:3 * GW], y_out[:]).then_inc(y_stored, 16)

            sp.sem_inc(y_stored, 16)
            sp.dma_start(run_max[:], d["mlstm_max"]).then_inc(const_in, 16)
            sp.dma_start(carry_row[:], d["mlstm_carry"]).then_inc(const_in, 16)
            sp.dma_start(gain[:], d["mlstm_out_g"].partition_broadcast(P)).then_inc(const_in, 16)
            sp.wait_ge(zeroed, 1)
            load(0, 0)
            load(1, 1)
            with sp.Fori(0, NT // 2 - 1) as j:
                for b in range(2):
                    c = 2 * j + b
                    sp.wait_ge(pe_done, c + 1)
                    sp.wait_ge(o_used, c + 1)
                    load(c + 2, b)
                    store(c)
            store(NT - 2)
            store(NT - 1)
            sp.wait_ge(y_stored, 16 * (NT + 1))

        @block.gpsimd
        def _(pool):
            nc.gpsimd.memset(sel[:], 0.0)
            nc.gpsimd.memset(k_pad[:], 0.0)
            nc.gpsimd.memset(state[:], 0.0)
            for b in range(2):
                nc.gpsimd.memset(va[b][:], 1.0)
            nc.gpsimd.memset(past[:], 1.0)
            pool.drain().then_inc(zeroed, 1)
            nc.gpsimd.affine_select(out=past[:], in_=past[:], compare_op=ALU.is_ge, fill=0.0, base=0, pattern=[[1, P]],
                                    channel_multiplier=-1)
            pool.drain()
            nc.gpsimd.affine_select(out=sel[:], in_=sel[:], compare_op=ALU.not_equal, fill=-1.0, base=0,
                                    pattern=[[-1, GH], [0, P]], channel_multiplier=1).then_inc(sel_ready, 1)

            def chunk(c, b, j):
                pool.wait_ge(e_ready, c + 1)
                nc.gpsimd.tensor_tensor(e[:], e[:], past[:].unsqueeze(1).to_broadcast([P, GH, P]), ALU.mult)\
                    .then_inc(mask_ready, 1)
                pool.wait_ge(gate_in, c + 1)
                nc.gpsimd.tensor_tensor(gate2[:], gate[:], g.one[:].to_broadcast([P, GW]), ALU.add).then_inc(gate_ready, 1)
                pool.drain().then_inc(gate_free, 1)
                pool.wait_ge(h_in, c + 1)
                nc.gpsimd.tensor_tensor(h2[:], h1[:], h1[:], ALU.mult).then_inc(h_sq_ready, 1)
                pool.wait_ge(nd_done, c + 1)
                nc.gpsimd.tensor_tensor(h_var[:], h_sq[:], g.head_eps[:].to_broadcast([P, GH]), ALU.add)
                pool.drain()
                nc.gpsimd.tensor_tensor(h_rstd[:], h_var[:], g.neg_half[:].to_broadcast([P, GH]), ALU.pow)\
                    .then_inc(h_rstd_ready, 1)

            pool.sem_inc(gate_free, 1)
            pairs(pool, chunk)

        @block.scalar
        def _(act):
            act.sem_inc(st_ready, 1)
            act.wait_ge(zeroed, 1)
            act.wait_ge(carry_ready, 1)
            nc.scalar.activation(carry[:], p_max[:, :, 0:NT], ACT.Copy, scale=-1.0).then_inc(carry_ready, 1)

            def chunk(c, b, j):
                act.wait_ge(slot_in[b], 16 * LOADS * (j + 1))
                act.wait_ge(st_ready, c + 1)
                for half in range(2):
                    at = slice(half * HD, (half + 1) * HD)
                    nc.scalar.activation(k_pad[at, half::2, :], qk[b][at, NB:2 * NB, :], ACT.Copy)
                act.drain().then_inc(pad_ready, 1)
                act.wait_ge(gate_free, c + 1)
                nc.scalar.activation(gate[:], o_in[b][:], ACT.Exp, scale=-1.0).then_inc(gate_in, 1)
                act.drain().then_inc(o_used, 1)
                act.wait_ge(arg_ready, c + 1)
                nc.scalar.activation(e[:], arg[:], ACT.Exp).then_inc(e_ready, 1)

            pairs(act, chunk)

        @block.tensor
        def _(pe):
            pe.wait_ge(const_in, 48)
            pe.wait_ge(sel_ready, 1)
            for h in range(GH):
                last = nc.tensor.matmul(p_max[:, h, 0:NT], sel[:, h, :], carry_row[:], start=True, stop=True)
            last.then_inc(carry_ready, 1)
            pe.wait_ge(carry_ready, 2)

            def chunk(c, b, j):
                pe.wait_ge(slot_in[b], 16 * LOADS * (j + 1))
                pe.wait_ge(kw_ready, c + 1)
                for n in range(NB):
                    nc.tensor.transpose(p_t[:, n * P:(n + 1) * P], qk[b][:, NB + n, :], g.ident[:])
                nc.tensor.transpose(p_t[:, GW:GW + 4 * GH], rows[b][:], g.ident[0:4 * GH, 0:4 * GH]).then_inc(t_ready, 1)
                for h in range(GH):
                    last = nc.tensor.matmul(p_max[:, h, :], sel[:, h, :], run_max[:, bass.ds(c * P, P)],
                                            start=True, stop=True)
                last.then_inc(max_ready, 1)
                pe.wait_ge(pad_ready, c + 1)
                for h in range(GH):
                    last = nc.tensor.matmul(p_st[:, h, :], k_pad[:, h, :], qk[b][:, h // 2, :], start=True, stop=True)
                last.then_inc(st_ready, 1)
                pe.wait_ge(state_ready, c + 1)
                for n in range(NB):
                    last = nc.tensor.matmul(p_inter[:, n * 2 * VW:(n + 1) * 2 * VW], qk[b][:, n, :], state[:, n, :],
                                            start=True, stop=True)
                last.then_inc(inter_ready, 1)
                pe.wait_ge(kw_ready, c + 2)
                for n in range(NB):
                    last = nc.tensor.matmul(p_state[:, n * 2 * VW:(n + 1) * 2 * VW], kw[:, n * P:(n + 1) * P],
                                            va[b][:, 2 * n:2 * n + 2, :].rearrange("p h d -> p (h d)"),
                                            start=True, stop=True)
                last.then_inc(state_out, 1)
                pe.wait_ge(sm_ready, c + 1)
                for h in range(GH):
                    last = nc.tensor.matmul(p_num[:, h * VW:(h + 1) * VW], sm[:, h, :], va[b][:, h, :],
                                            start=True, stop=True)
                last.then_inc(num_ready, 1)
                pe.drain().then_inc(pe_done, 1)

            pairs(pe, chunk)

        @block.vector
        def _(dve):
            def chunk(c, b, j):
                dve.wait_ge(t_ready, c + 1)
                nc.vector.tensor_copy(cols[:], p_t[:, GW:GW + 4 * GH])
                dve.drain()
                a, w_inter, w_new, e_neg_m = (cols[:, n * GH:(n + 1) * GH] for n in range(4))
                nc.vector.scalar_tensor_tensor(heads(kw[:]), heads(p_t[:, 0:GW]), HD ** -0.5, along(w_new, HD),
                                               ALU.mult, ALU.mult).then_inc(kw_ready, 1)
                dve.wait_ge(max_ready, c + 1)
                for h in range(GH):
                    nc.vector.tensor_scalar(arg[:, h, :], p_max[:, h, :], a[:, h:h + 1], 0.0, ALU.add, ALU.min)
                dve.drain().then_inc(arg_ready, 1)
                dve.wait_ge(inter_ready, c + 1)
                nc.vector.tensor_tensor(nd[:], p_inter[:, 0:GH * VW].rearrange("p (h d) -> p h d", d=VW), along(w_inter, VW),
                                        ALU.mult)
                dve.wait_ge(state_out, c + 1)
                for n in range(NB):
                    for half in range(2):
                        at, h = slice(half * HD, (half + 1) * HD), 2 * n + half
                        cs = slice(half * VW, (half + 1) * VW)
                        nc.vector.scalar_tensor_tensor(state[at, n, cs], state[at, n, cs], carry[at, h, bass.ds(c, 1)],
                                                       p_state[at, n * 2 * VW + half * VW:n * 2 * VW + (half + 1) * VW],
                                                       ALU.mult, ALU.add)
                dve.drain().then_inc(state_ready, 1)
                dve.wait_ge(st_ready, c + 2)
                dve.wait_ge(mask_ready, c + 1)
                nc.vector.scalar_tensor_tensor(sm[:], p_st[:], HD ** -0.5, e[:], ALU.mult, ALU.mult).then_inc(sm_ready, 1)
                dve.wait_ge(num_ready, c + 1)
                nc.vector.tensor_tensor(nd2[:], nd[:], p_num[:, 0:GH * VW].rearrange("p (h d) -> p h d", d=VW), ALU.add)
                dve.drain()
                nc.vector.scalar_tensor_tensor(den[:], nd2[:, :, HD], -1.0, nd2[:, :, HD], ALU.mult, ALU.max)
                dve.drain()
                nc.vector.tensor_tensor(den2[:], den[:], e_neg_m, ALU.max)
                dve.drain()
                nc.vector.reciprocal(inv[:], den2[:])
                dve.wait_ge(gate_ready, c + 1)
                nc.vector.reciprocal(o_gate[:], gate2[:])
                dve.drain()
                nc.vector.tensor_tensor(heads(h_tmp[:]), nd2[:, :, 0:HD], along(inv[:], HD), ALU.mult)
                dve.drain()
                nc.vector.tensor_tensor(h1[:], h_tmp[:], o_gate[:], ALU.mult).then_inc(h_in, 1)
                dve.wait_ge(h_sq_ready, c + 1)
                nc.vector.tensor_reduce(h_sq[:], heads(h2[:]), AX.X, ALU.add).then_inc(nd_done, 1)
                dve.wait_ge(h_rstd_ready, c + 1)
                nc.vector.tensor_tensor(heads(h_tmp[:]), heads(h1[:]), along(h_rstd[:], HD), ALU.mult)
                dve.drain()
                dve.wait_ge(y_stored, 16 * (c + 1))
                nc.vector.tensor_tensor(y_out[:], h_tmp[:], gain[:], ALU.mult).then_inc(y_ready, 1)

            dve.wait_ge(const_in, 48)
            nc.vector.tensor_scalar(gain[:], gain[:], HD ** 0.5, None, ALU.mult)
            dve.wait_ge(zeroed, 1)
            dve.wait_ge(carry_ready, 2)
            dve.sem_inc(kw_ready, 1)
            dve.sem_inc(state_ready, 1)
            pairs(dve, chunk)
    ph.close()


F_B, F_K, F_KK, F_R, F_V, F_RK = range(6)
NF = 6
NB = GW // P
RANK = 16
DECAY = float(np.exp(-0.5))


def rwkv_factors(nc, d, g, big, to_next):
    ph = Phase(nc, "rfac")
    sb, ps, sem = ph.sb, ph.ps, ph.sem
    low = [sb(f"low{n}", [RANK, 1 + T]) for n in range(2)]
    low_s = [sb(f"low_s{n}", [RANK, T]) for n in range(2)]
    low_mu = sb("low_mu", [RANK, 2])
    up = sb("up", [RANK, 2, GW])
    cols = sb("cols", [P, NB, 5])
    head_ones = sb("head_ones", [P, P])
    not_first = sb("not_first", [P, T])
    r, k, sg, a, kk, cum, tmp = (sb(n, [P, T]) for n in ("r", "k", "sg", "a", "kk", "cum", "tmp"))
    mid = sb("mid", [P, NB, NT])
    p_w, p_a = ps("w", [P, T]), ps("a", [P, T])
    const_in, rk_in, v_in, consts_ready, shifted, tanh_ready, w_ready, a_ready, sg_ready, a_done = (
        sem(n) for n in ("const_in", "rk_in", "v_in", "consts_ready", "shifted", "tanh_ready", "w_ready", "a_ready",
                         "sg_ready", "a_done"))
    sq_ready, sum_ready, clamped, norm_ready, arg_ready, exp_ready, block_done, pad_ready = (
        sem(n) for n in ("sq_ready", "sum_ready", "clamped", "norm_ready", "arg_ready", "exp_ready", "block_done",
                         "pad_ready"))

    def chunks(ap):
        return ap.rearrange("p (c t) -> p c t", t=P)

    with nc.Block() as block:
        @block.sync
        def _(sp):
            sp.wait_ge(pad_ready, 1)
            sp.dma_start(low[0][:, 1:], d["lowT"][0:RANK, :]).then_inc(const_in, 16)
            sp.dma_start(low[1][:, 1:], d["lowT"][32:32 + RANK, :]).then_inc(const_in, 16)
            sp.dma_start(low_mu[:], d["rwkv_low_mu"]).then_inc(const_in, 16)
            sp.dma_start(up[:], d["rwkv_up"]).then_inc(const_in, 16)
            sp.dma_start(cols[:], d["rwkv_cols"]).then_inc(const_in, 16)
            for n in range(NB):
                if n:
                    sp.wait_ge(block_done, n)
                sp.dma_start(r[:], d["rwkv_T"][n * P:(n + 1) * P, :]).then_inc(rk_in, 16)
                sp.dma_start(k[:], d["rwkv_T"][GW + n * P:GW + (n + 1) * P, :]).then_inc(rk_in, 16)
                sp.dma_start(big[:, n, F_V, :], d["rwkv_T"][2 * GW + n * P:2 * GW + (n + 1) * P, :]).then_inc(v_in, 16)
            sp.wait_ge(v_in, 16 * NB)

        @block.gpsimd
        def _(pool):
            for n in range(2):
                nc.gpsimd.memset(low[n][:, 0:1], 0.0)
            pool.drain().then_inc(pad_ready, 1)
            nc.gpsimd.memset(not_first[:], 1.0)
            nc.gpsimd.memset(to_next[:], 1.0)
            pool.drain()
            nc.gpsimd.memset(chunks(not_first[:])[:, :, 0:1], 0.0)
            same_head(nc, pool, head_ones)
            pool.drain().then_inc(consts_ready, 1)

        @block.tensor
        def _(pe):
            pe.wait_ge(consts_ready, 1)
            pe.wait_ge(shifted, 1)
            pe.wait_ge(tanh_ready, 1)
            for n in range(NB):
                if n:
                    pe.wait_ge(clamped, n)
                    pe.wait_ge(a_done, n)
                for out, i, ready in ((p_w, 0, w_ready), (p_a, 1, a_ready)):
                    for c in range(0, T, BANK):
                        last = nc.tensor.matmul(out[:, c:c + BANK], up[:, i, n * P:(n + 1) * P], low_s[i][:, c:c + BANK],
                                                start=True, stop=True)
                    last.then_inc(ready, 1)
                pe.wait_ge(sg_ready, n + 1)
                pe.wait_ge(sq_ready, n + 1)
                for c in range(0, T, BANK):
                    last = nc.tensor.matmul(p_w[:, c:c + BANK], head_ones[:], tmp[:, c:c + BANK], start=True, stop=True)
                last.then_inc(sum_ready, 1)

        @block.scalar
        def _(act):
            act.wait_ge(shifted, 1)
            nc.scalar.activation(low_s[0][:], low_s[0][:], ACT.Tanh).then_inc(tanh_ready, 1)
            for n in range(NB):
                act.wait_ge(w_ready, n + 1)
                if n:
                    act.wait_ge(block_done, n)
                nc.scalar.activation(sg[:], p_w[:], ACT.Sigmoid, bias=cols[:, n, 0:1]).then_inc(sg_ready, 1)
                act.wait_ge(a_ready, n + 1)
                nc.scalar.activation(a[:], p_a[:], ACT.Sigmoid, bias=cols[:, n, 1:2]).then_inc(a_done, 1)
                act.wait_ge(clamped, n + 1)
                nc.scalar.activation(tmp[:], tmp[:], ACT.Sqrt).then_inc(norm_ready, 1)
                for i, (src, scale) in enumerate(((cum, -DECAY), (tmp, -DECAY), (cum, DECAY))):
                    act.wait_ge(arg_ready, 4 * n + i + 1)
                    nc.scalar.activation(tmp[:], src[:], ACT.Exp, scale=scale).then_inc(exp_ready, 1)
                act.wait_ge(arg_ready, 4 * n + 4)
                nc.scalar.activation(mid[:, n, :], mid[:, n, :], ACT.Exp, scale=-DECAY).then_inc(exp_ready, 1)

        @block.vector
        def _(dve):
            dve.wait_ge(const_in, 16 * 5)
            dve.wait_ge(pad_ready, 1)
            for i in range(2):
                x, previous = low[i][:, 1:], low[i][:, 0:T]
                nc.vector.tensor_tensor(low_s[i][:], previous, x, ALU.subtract)
                dve.drain()
                nc.vector.scalar_tensor_tensor(low_s[i][:], low_s[i][:], low_mu[:, i:i + 1], x, ALU.mult, ALU.add)
            dve.drain().then_inc(shifted, 1)
            dve.wait_ge(consts_ready, 1)
            for n in range(NB):
                f = [big[:, n, i, :] for i in range(NF)]
                k_k, k_a, r_k = (cols[:, n, i:i + 1] for i in (2, 3, 4))
                dve.wait_ge(rk_in, 32 * (n + 1))
                nc.vector.tensor_scalar(kk[:], k[:], k_k, None, ALU.mult)
                dve.drain()
                nc.vector.tensor_tensor(tmp[:], kk[:], kk[:], ALU.mult).then_inc(sq_ready, 1)
                dve.wait_ge(sum_ready, n + 1)
                nc.vector.tensor_scalar(tmp[:], p_w[:], 1e-24, None, ALU.max).then_inc(clamped, 1)
                dve.wait_ge(a_done, n + 1)
                nc.vector.tensor_scalar(f[F_RK], a[:], 1.0, k_a, ALU.subtract, ALU.mult)
                dve.drain()
                nc.vector.scalar_tensor_tensor(f[F_K], f[F_RK], 1.0, k[:], ALU.add, ALU.mult)
                dve.drain()
                nc.vector.scalar_tensor_tensor(f[F_RK], r[:], r_k, f[F_K], ALU.mult, ALU.mult)
                dve.wait_ge(norm_ready, n + 1)
                nc.vector.reciprocal(tmp[:], tmp[:])
                dve.drain()
                nc.vector.tensor_tensor(kk[:], kk[:], tmp[:], ALU.mult)
                dve.drain()
                nc.vector.tensor_tensor(f[F_B], kk[:], a[:], ALU.mult)
                dve.wait_ge(sg_ready, n + 1)
                nc.vector.tensor_tensor_scan(cum[:], not_first[:], sg[:], 0.0, ALU.mult, ALU.add)
                dve.drain()
                nc.vector.tensor_copy(mid[:, n, :], chunks(cum[:])[:, :, P // 2 - 1])
                dve.drain()
                nc.vector.tensor_tensor(chunks(cum[:]), chunks(cum[:]), along(mid[:, n, :], P), ALU.subtract)\
                    .then_inc(arg_ready, 1)
                dve.wait_ge(exp_ready, 4 * n + 1)
                nc.vector.tensor_tensor(f[F_R], r[:], tmp[:], ALU.mult)
                nc.vector.tensor_copy(to_next[:, n, :], chunks(tmp[:])[:, :, P - 1])
                dve.drain()
                nc.vector.tensor_tensor(tmp[:], cum[:], sg[:], ALU.subtract).then_inc(arg_ready, 1)
                dve.wait_ge(exp_ready, 4 * n + 2)
                nc.vector.tensor_tensor(f[F_KK], kk[:], tmp[:], ALU.mult)
                dve.drain().then_inc(arg_ready, 1)
                dve.wait_ge(exp_ready, 4 * n + 3)
                nc.vector.tensor_tensor(f[F_B], f[F_B], tmp[:], ALU.mult)
                nc.vector.tensor_tensor(f[F_K], f[F_K], tmp[:], ALU.mult)
                dve.drain().then_inc(arg_ready, 1)
                dve.wait_ge(exp_ready, 4 * n + 4)
                nc.vector.tensor_tensor(to_next[:, n, 0:NT - 1], to_next[:, n, 0:NT - 1], mid[:, n, 1:NT], ALU.mult)
                dve.drain().then_inc(block_done, 1)
    ph.close()


def rwkv_chunks(nc, d, g, big, to_next):
    ph = Phase(nc, "rwkv")
    sb, ps, sem = ph.sb, ph.ps, ph.sem
    LEVELS = 7
    slots = [sb(f"slot{b}", [P, NB, NF, P]) for b in range(2)]
    pads = [sb(f"pad{b}", [P, GH, F_KK + 1, P]) for b in range(2)]
    keep = sb("keep", [P, 4, P], U32)
    keep_low = sb("keep_low", [P, GH, P], U32)
    level = sb("level", [P, LEVELS, P])
    level0 = sb("level0", [P, P])
    tri = sb("tri", [P, GH, P])
    prod = sb("prod", [P, GH, 4, P])
    a_low = sb("a_low", [P, GH, P])
    lt = sb("lt", [P, LEVELS, GH, P])
    x = sb("x", [P, 2, 2, 2, P])
    xl = sb("xl", [P, LEVELS - 1, 2, 2, P])
    tok = sb("tok", [P, 2, GW])
    v = sb("v", [P, GW])
    head_sel = sb("head_sel", [P, 2])
    bonus = sb("bonus", [P, GH])
    state = sb("state", [P, NB, P])
    u, removed, y, y2, y3, y4, y_out = (sb(n, [P, GW]) for n in ("u", "removed", "y", "y2", "y3", "y4", "y_out"))
    y_sq, y_var, y_rstd, gain = sb("y_sq", [P, GH]), sb("y_var", [P, GH]), sb("y_rstd", [P, GH]), sb("gain", [P, GW])
    p_b = [ps(f"b{n}", [P, BANK]) for n in range(8)]
    P_A, P_TOK, P_V, P_U = 4, 5, 6, 7
    names = ("const_in", "zeroed", "masks_ready", "slot_ready", "slot_free", "prod_out", "a_out", "tok_out", "v_out",
             "prod_ready", "a_ready", "tok_ready", "v_ready", "lt_ready", "x_first", "taken", "u_out", "u_ready", "removed_out",
             "removed_ready", "y_out_ready", "state_out", "state_ready", "y_ready", "y_sq_ready", "y_sum_ready", "y_rstd_ready",
             "bonus_ready", "bonus_free", "out_ready", "stored", "tok_free")
    (const_in, zeroed, masks_ready, slot_ready, slot_free, prod_out, a_out, tok_out, v_out, prod_ready, a_ready, tok_ready,
     v_ready, lt_ready, x_first, taken, u_out, u_ready, removed_out, removed_ready, y_done, state_out, state_ready, y_ready,
     y_sq_ready, y_sum_ready, y_rstd_ready, bonus_ready, bonus_free, out_ready, stored, tok_free) = (sem(n) for n in names)
    xl_out, xl_ready, x_out, x_ready = ([sem(f"{n}{p}") for p in range(2)] for n in ("xl_out", "xl_ready", "x_out", "x_ready"))
    UP = LEVELS - 1

    def chunk_of(c):
        return big[:, :, :, bass.ds(c * P, P)]

    def pair_of(ap):
        return ap.rearrange("p (h c) -> p h c", h=2)

    def half(ap, i, which):
        return ap.rearrange("p h (b a n) -> p h b a n", a=2, n=2 << i)[:, :, :, which, :]

    with nc.Block() as block:
        @block.sync
        def _(sp):
            sp.sem_inc(stored, 16)
            sp.dma_start(gain[:], d["rwkv_ln_g"].partition_broadcast(P)).then_inc(const_in, 16)
            with sp.Fori(0, NT) as c:
                sp.wait_ge(out_ready, c + 1)
                sp.dma_start(tile_of(d["y1"], c)[:, 4 * GW:5 * GW], y_out[:]).then_inc(stored, 16)
            sp.wait_ge(stored, 16 * (NT + 1))

        @block.gpsimd
        def _(pool):
            for pad in pads:
                nc.gpsimd.memset(pad[:], 0.0)
            nc.gpsimd.memset(xl[:], 0.0)
            nc.gpsimd.memset(state[:], 0.0)
            nc.gpsimd.memset(prod[:], 0.0)
            nc.gpsimd.memset(a_low[:], 0.0)
            pool.drain().then_inc(zeroed, 1)
            nc.gpsimd.memset(tri[:], 1.0)
            nc.gpsimd.memset(level[:], 1.0)
            nc.gpsimd.memset(level0[:], 1.0)
            nc.gpsimd.memset(head_sel[:], 1.0)
            pool.drain()

            def where(ap, base, pattern, mult):
                nc.gpsimd.affine_select(out=ap, in_=ap, compare_op=ALU.is_ge, fill=0.0, base=base, pattern=pattern,
                                        channel_multiplier=mult)
                pool.drain()

            where(tri[:, 0::2, :], -1, [[0, 2], [1, P]], -1)
            where(tri[:, 1::2, :], 0, [[0, 2], [1, P]], -1)
            nc.gpsimd.tensor_copy(keep[:], tri[:])
            pool.drain()
            nc.gpsimd.memset(tri[:], 1.0)
            pool.drain()
            where(tri[:], -1, [[0, GH], [-1, P]], 1)
            nc.gpsimd.tensor_copy(keep_low[:], tri[:])
            where(head_sel[:, 0:1], HD - 1, [[0, 1]], -1)
            where(head_sel[:, 1:2], -HD, [[0, 1]], 1)
            for i in range(LEVELS):
                n = 1 << i
                ap = level[:, i, :].rearrange("p (b t) -> p b t", t=2 * n)
                nc.gpsimd.memset(ap[:, :, 0:n], 0.0)
                pool.drain()
                where(ap, 0, [[-2 * n, P // (2 * n)], [0, 2 * n]], 1)
                where(ap, n - 1, [[2 * n, P // (2 * n)], [0, 2 * n]], -1)
            ap = level0[:].rearrange("p (b s) -> p b s", s=2)
            nc.gpsimd.memset(ap[:, :, 1:2], 0.0)
            pool.drain()
            where(ap, -1, [[-2, P // 2], [-1, 2]], 1)
            where(ap, 1, [[2, P // 2], [1, 2]], -1)
            pool.drain().then_inc(masks_ready, 1)

            def norm(c):
                pool.wait_ge(y_ready, c + 1)
                nc.gpsimd.tensor_tensor(y2[:], y[:], y[:], ALU.mult).then_inc(y_sq_ready, 1)
                pool.wait_ge(y_sum_ready, c + 1)
                nc.gpsimd.tensor_tensor(y_var[:], y_sq[:], g.head_eps[:].to_broadcast([P, GH]), ALU.add)
                pool.drain()
                nc.gpsimd.tensor_tensor(y_rstd[:], y_var[:], g.neg_half[:].to_broadcast([P, GH]), ALU.pow)\
                    .then_inc(y_rstd_ready, 1)

            def levels(c):
                pool.wait_ge(prod_ready, c + 1)
                pool.wait_ge(slot_free, c + 2)
                for i in range(LEVELS):
                    nc.gpsimd.tensor_tensor(lt[:, i], prod[:, :, 0, :], level[:, i:i + 1, :].to_broadcast([P, GH, P]),
                                            ALU.mult).then_inc(lt_ready, 1)
                pool.wait_ge(v_ready, c + 1)
                pool.wait_ge(bonus_free, c + 1)
                nc.gpsimd.tensor_tensor(heads(y4[:]), heads(v[:]), along(bonus[:], HD), ALU.mult).then_inc(bonus_ready, 1)

            levels(0)
            with pool.Fori(1, NT) as c:
                norm(c - 1)
                levels(c)
            norm(NT - 1)

        @block.scalar
        def _(act):
            act.wait_ge(zeroed, 1)

            def fill(c, b):
                act.wait_ge(slot_free, c + 1)
                nc.scalar.activation(slots[b][:], chunk_of(c), ACT.Copy)
                for first in range(2):
                    at = slice(first * HD, (first + 1) * HD)
                    nc.scalar.activation(pads[b][at, first::2], chunk_of(c)[at, :, 0:F_KK + 1], ACT.Copy)
                act.drain().then_inc(slot_ready, 1)

            def chunk(c, b, last):
                act.wait_ge(tok_out, c + 1)
                nc.scalar.activation(tok[:].rearrange("p a c -> p (a c)"), p_b[P_TOK][:], ACT.Copy).then_inc(tok_ready, 1)
                if not last:
                    fill(c + 1, 1 - b)
                act.wait_ge(v_out, c + 1)
                act.wait_ge(bonus_ready, c + 1)
                nc.scalar.activation(v[:], p_b[P_V][:, 0:GW], ACT.Copy)
                nc.scalar.activation(bonus[:], p_b[P_V][:, GW:GW + GH], ACT.Copy)
                act.drain().then_inc(v_ready, 1)
                for i in range(UP):
                    for p in range(2):
                        act.wait_ge(xl_out[p], UP * c + i + 1)
                        nc.scalar.activation(half(xl[:, i, p], i, 0), half(pair_of(p_b[p][:, 0:2 * P]), i, 0), ACT.Copy)\
                            .then_inc(xl_ready[p], 1)
                act.wait_ge(u_out, c + 1)
                nc.scalar.activation(u[:], p_b[P_U][:, 0:GW], ACT.Copy).then_inc(u_ready, 1)
                act.wait_ge(removed_out, c + 1)
                nc.scalar.activation(removed[:], p_b[P_A][:, 0:GW], ACT.Copy, scale=-1.0).then_inc(removed_ready, 1)
                act.wait_ge(y_done, c + 1)
                nc.scalar.activation(y[:], p_b[P_TOK][:, 0:GW], ACT.Copy).then_inc(y_ready, 1)
                act.drain().then_inc(tok_free, 1)

            act.sem_inc(tok_free, 1)
            act.sem_inc(bonus_ready, 1)
            fill(0, 0)
            with act.Fori(0, NT // 2 - 1) as pair:
                for b in range(2):
                    chunk(2 * pair + b, b, last=False)
            for b in range(2):
                chunk(NT - 2 + b, b, last=b > 0)

        @block.tensor
        def _(pe):
            pe.wait_ge(zeroed, 1)
            pe.wait_ge(masks_ready, 1)
            pe.sem_inc(slot_free, 2)

            def products(c, slot, pad):
                pe.wait_ge(slot_ready, c + 1)
                for h in range(GH):
                    rhs = slot[:, h // 2, F_KK:F_R + 1, :].rearrange("p f t -> p (f t)")
                    for i, f in enumerate((F_B, F_K)):
                        last = nc.tensor.matmul(p_b[h][:, i * 2 * P:(i + 1) * 2 * P], pad[:, h, f, :], rhs,
                                                start=True, stop=True)
                    last.then_inc(prod_out, 1)
                for h in range(GH):
                    last = nc.tensor.matmul(p_b[P_A][:, h * P:(h + 1) * P], pad[:, h, F_KK, :], slot[:, h // 2, F_B, :],
                                            start=True, stop=True)
                last.then_inc(a_out, 1)
                pe.wait_ge(tok_free, c + 1)
                for i, f in enumerate((F_B, F_K)):
                    for n in range(NB):
                        at = i * GW + n * P
                        last = nc.tensor.transpose(p_b[P_TOK][:, at:at + P], slot[:, n, f, :], g.ident[:])
                last.then_inc(tok_out, 1)
                pe.wait_ge(state_ready, c + 1)
                for n in range(NB):
                    nc.tensor.transpose(p_b[P_V][:, n * P:(n + 1) * P], slot[:, n, F_V, :], g.ident[:])
                for n in range(NB):
                    last = nc.tensor.matmul(p_b[P_V][:, GW + 2 * n:GW + 2 * n + 2], slot[:, n, F_RK, :], head_sel[:],
                                            start=True, stop=True)
                last.then_inc(v_out, 1)

            def inverse(c):
                pe.wait_ge(x_first, c + 1)
                for i in range(UP):
                    pe.wait_ge(lt_ready, LEVELS * c + i + 2)
                    for p in range(2):
                        if i:
                            pe.wait_ge(x_ready[p], UP * c + i)
                        for j in range(2):
                            last = nc.tensor.matmul(p_b[p][:, j * P:(j + 1) * P], lt[:, i + 1, 2 * p + j, :],
                                                    x[:, p, 0, j, :], start=True, stop=True)
                        last.then_inc(xl_out[p], 1)
                    for p in range(2):
                        pe.wait_ge(xl_ready[p], UP * c + i + 1)
                        for j in range(2):
                            if i < UP - 1:
                                nc.tensor.matmul(p_b[2 + p][:, j * P:(j + 1) * P], x[:, p, 1, j, :], xl[:, i, p, j, :],
                                                 start=True, stop=True)
                            last = nc.tensor.matmul(p_b[2 + p][:, (2 + j) * P:(3 + j) * P], xl[:, i, p, j, :],
                                                    x[:, p, 1, j, :], start=True, stop=True)
                        last.then_inc(x_out[p], 1)

            def through_state(c, slot):
                pe.wait_ge(v_ready, c + 1)
                for n in range(NB):
                    nc.tensor.matmul(p_b[P_U][:, n * P:(n + 1) * P], slot[:, n, F_KK, :], state[:, n, :], start=True, stop=False)
                    for h in (2 * n, 2 * n + 1):
                        last = nc.tensor.matmul(p_b[P_U][:, h * HD:(h + 1) * HD], prod[:, h, 2, :], v[:, h * HD:(h + 1) * HD],
                                                start=False, stop=(h % 2 == 1))
                last.then_inc(u_out, 1)
                pe.wait_ge(u_ready, c + 1)
                for p in range(2):
                    pe.wait_ge(x_ready[p], UP * (c + 1))
                for h in range(GH):
                    last = nc.tensor.matmul(p_b[P_A][:, h * HD:(h + 1) * HD], x[:, h // 2, 1, h % 2, :],
                                            u[:, h * HD:(h + 1) * HD], start=True, stop=True)
                last.then_inc(removed_out, 1)
                pe.wait_ge(tok_ready, c + 1)
                pe.wait_ge(removed_ready, c + 1)
                for n in range(NB):
                    cs = slice(n * P, (n + 1) * P)
                    nc.tensor.matmul(p_b[P_V][:, cs], g.ident[:], state[:, n, :], start=True, stop=False)
                    nc.tensor.matmul(p_b[P_V][:, cs], tok[:, 1, cs], v[:, cs], start=False, stop=False)
                    last = nc.tensor.matmul(p_b[P_V][:, cs], tok[:, 0, cs], removed[:, cs], start=False, stop=True)
                last.then_inc(state_out, 1)
                for n in range(NB):
                    nc.tensor.matmul(p_b[P_TOK][:, n * P:(n + 1) * P], slot[:, n, F_R, :], state[:, n, :], start=True, stop=False)
                    for h in (2 * n, 2 * n + 1):
                        hs = slice(h * HD, (h + 1) * HD)
                        nc.tensor.matmul(p_b[P_TOK][:, hs], prod[:, h, 3, :], v[:, hs], start=False, stop=False)
                        last = nc.tensor.matmul(p_b[P_TOK][:, hs], prod[:, h, 1, :], removed[:, hs], start=False,
                                                stop=(h % 2 == 1))
                last.then_inc(y_done, 1)
                pe.drain().then_inc(slot_free, 1)

            with pe.Fori(0, NT // 2) as pair:
                for b in range(2):
                    c = 2 * pair + b
                    products(c, slots[b], pads[b])
                    inverse(c)
                    through_state(c, slots[b])

        @block.vector
        def _(dve):
            dve.wait_ge(const_in, 16)
            nc.vector.tensor_scalar(gain[:], gain[:], HD ** 0.5, None, ALU.mult)
            dve.wait_ge(zeroed, 1)
            dve.wait_ge(masks_ready, 1)
            dve.sem_inc(bonus_free, 1)
            dve.sem_inc(state_ready, 1)

            def mask(c, some):
                for h in some:
                    wait_apart(dve, prod_out, GH * c + h + 1, taken)
                    nc.vector.copy_predicated(prod[:, h].rearrange("p f t -> p (f t)"), keep[:].rearrange("p f t -> p (f t)"),
                                              p_b[h][:])

            def sum_squares(c):
                dve.wait_ge(y_sq_ready, c + 1)
                nc.vector.tensor_reduce(y_sq[:], heads(y2[:]), AX.X, ALU.add).then_inc(y_sum_ready, 1)

            def norm(c):
                dve.wait_ge(y_rstd_ready, c + 1)
                nc.vector.tensor_tensor(heads(y3[:]), heads(y[:]), along(y_rstd[:], HD), ALU.mult)
                dve.drain()
                nc.vector.tensor_tensor(y3[:], y3[:], gain[:], ALU.mult)
                dve.drain()
                dve.wait_ge(bonus_ready, c + 2)
                dve.wait_ge(stored, 16 * (c + 1))
                nc.vector.tensor_tensor(y_out[:], y3[:], y4[:], ALU.add).then_inc(out_ready, 1)
                dve.drain().then_inc(bonus_free, 1)

            def chunk(c, first=False):
                dve.wait_ge(slot_free, c + 2)
                mask(c, (0, 1))
                if not first:
                    sum_squares(c - 1)
                mask(c, (2, 3))
                dve.drain().then_inc(prod_ready, 1)
                wait_apart(dve, a_out, c + 1, taken)
                nc.vector.copy_predicated(a_low[:].rearrange("p h s -> p (h s)"), keep_low[:].rearrange("p h s -> p (h s)"),
                                          p_b[P_A][:])
                dve.drain()
                ident = g.ident[:].unsqueeze(1).to_broadcast([P, 2, P])
                for p in range(2):
                    nc.vector.tensor_tensor(x[:, p, 0], a_low[:, 2 * p:2 * p + 2, :],
                                            level0[:].unsqueeze(1).to_broadcast([P, 2, P]), ALU.mult)
                dve.wait_ge(lt_ready, LEVELS * c + 1)
                for p in range(2):
                    nc.vector.tensor_tensor(x[:, p, 1], ident, lt[:, 0, 2 * p:2 * p + 2, :], ALU.subtract)
                dve.drain()
                for p in range(2):
                    nc.vector.tensor_tensor(x[:, p, 0], ident, x[:, p, 0], ALU.subtract)
                dve.drain().then_inc(x_first, 1)
                if not first:
                    norm(c - 1)
                for i in range(UP):
                    for p in range(2):
                        dve.wait_ge(x_out[p], UP * c + i + 1)
                        for a in range(1 if i == UP - 1 else 0, 2):
                            part = half(x[:, p, a], i, a)
                            less = half(pair_of(p_b[2 + p][:, a * 2 * P:(a + 1) * 2 * P]), i, a)
                            last = nc.vector.tensor_tensor(part, part, less, ALU.subtract)
                        last.then_inc(x_ready[p], 1)
                dve.drain()
                dve.wait_ge(state_out, c + 1)
                dve.wait_ge(y_done, c + 1)
                for n in range(NB):
                    for low in (0, HD):
                        at = slice(low, low + HD)
                        nc.vector.tensor_scalar(state[at, n, at], p_b[P_V][at, n * P + low:n * P + low + HD],
                                                to_next[at, n, bass.ds(c, 1)], None, ALU.mult)
                dve.drain().then_inc(state_ready, 1)

            chunk(0, first=True)
            with dve.Fori(1, NT) as c:
                chunk(c)
            sum_squares(NT - 1)
            norm(NT - 1)
    ph.close()


def rwkv(nc, d, g):
    with nc.sbuf_tensor("rwkv_big", [P, NB, NF, T], F32) as big, nc.sbuf_tensor("rwkv_to_next", [P, NB, NT], F32) as to_next:
        rwkv_factors(nc, d, g, big, to_next)
        rwkv_chunks(nc, d, g, big, to_next)


SCRATCH = {
    "y1": (T, 5 * GW),
    "z1T": (5 * GW, T),
    "qkmT": (2, 3 * GW, T),
    "fox_v": (T, GW),
    "mlstm_vo": (T, 2 * GW),
    "mlstm_qkT": (2 * GW, T),
    "rwkv_T": (3 * GW, T),
    "fox_rows": (2 * GH, 4, T),
    "mlstm_rows": (4 * GH, T),
    "mlstm_max": (GH, T),
    "mlstm_carry": (GH, NT),
    "mem_kT": (2, GW, NMEM),
    "mem_v": (NMEM, GW),
    "lowT": (P, T),
    "hT": (DM, T),
    "x2T": (DM, T),
    "x1": (T, DM),
    "rel_table": (H2 * REL_R, GRID_W * GRID_W),
    "qk2T": (2, 2 * D2, T),
    "v2": (T, D2),
    "f_inT": (D2, T),
    "z2T": (2 * D2, T),
    "y2": (T, DM),
    "ctx_kT": (2, D2, NMEM),
    "ctx_v": (NMEM, D2),
}


class OnChip:
    pass


def build(nc, arrays, phases):
    scratch = {n: nc.dram_tensor(f"scratch_{n}", shape, F32, kind="Internal").ap() for n, shape in SCRATCH.items()}
    d, g = {**arrays, **scratch}, OnChip()
    with ExitStack() as ctx:
        def sb(name, shape):
            return ctx.enter_context(nc.sbuf_tensor(name, shape, F32))

        g.ident = sb("ident", [P, P])
        g.neg_half, g.eps, g.head_eps, g.one = (sb(n, [P, 1]) for n in ("neg_half", "eps", "head_eps", "one"))
        g.scale_x, g.shift_x, g.scale_c, g.shift_c = (sb(n, [P, KB]) for n in ("scale_x", "shift_x", "scale_c", "shift_c"))
        g.gate_x = sb("gate_x", [P, DM])
        phases(nc, d, g, sb)


def all_phases(nc, d, g, sb):
    consts_phase(nc, g)
    side_inputs(nc, d, g)
    tile_pass_1(nc, d, g)
    feature_pass_1(nc, d, g)
    gates_phase(nc, d, g)
    fox_attention(nc, d, g)
    mlstm(nc, d, g)
    rwkv(nc, d, g)
    mem_attention(nc, d, g)
    tile_pass_2(nc, d, g)
    feature_pass_2(nc, d, g)
    with nc.sbuf_tensor("nbr_inner", [P, H2, SPAN, GRID_W], F32) as inner, \
            nc.sbuf_tensor("nbr_edge", [P, H2, EDGE, GRID_W], F32) as edge:
        fourier(nc, d, g, (inner, edge))
        neighbourhood(nc, d, g, (inner, edge))
    final_pass(nc, d, g)


PHASES = all_phases


def kernel(**inputs):
    import concourse.bacc as bacc
    from concourse.bass_utils import run_bass_kernel_spmd

    a = {n: np.asarray(v) for n, v in inputs.items()}
    at = {}
    col = 0
    for name, width in (("au", GW), ("av", GW), ("az", GW), ("bq", GW), ("bk", GW), ("bv", GW), ("bf", GH), ("bz", GW),
                        ("cq", GW), ("ck", GW), ("cv", GW), ("ci", GH), ("cf", GH), ("co", GW), ("cz", GW),
                        ("dr", GW), ("dw", 16), ("dk", GW), ("dv", GW), ("da", 16), ("dz", GW), ("mq", GW), ("mz", GW)):
        at[name] = slice(col, col + width)
        col += width
    w_in = a["w_in"][0]

    def columns(*names):
        return np.concatenate([w_in[:, at[n]] for n in names], axis=1)

    def blocks(w):
        k, c = w.shape[0] // P, w.shape[1] // P
        return w.reshape(k, P, c, P).transpose(2, 1, 0, 3).reshape(c, P, k * P)

    low = np.zeros((DM, P), np.float32)
    for first, name in ((0, "dw"), (32, "da"), (64, "bf"), (68, "ci"), (72, "cf")):
        n = at[name].stop - at[name].start
        low[:, first:first + n] = w_in[:, at[name]]

    def col_blocks(v):
        return v.reshape(-1, P).T

    def row(*vs):
        return np.concatenate(vs)

    w_out = a["w_out"][0]
    w_in_2 = a["w_in_2"][0]
    b_ada = a["b_ada_2"][0]
    channel = np.arange(P)
    angle_c = 2 * np.pi / P * np.outer(channel, channel)
    token, position = np.arange(TF), np.arange(T)
    angle_t = 2 * np.pi / T * (np.outer(token, position) % T)
    waves = np.stack([np.cos(angle_t), -np.sin(angle_t)]) * (T * P) ** -0.5
    waves = waves.reshape(2, NF_T, P, NF_T, P, RADIX).transpose(5, 3, 2, 1, 0, 4)

    arrays = {
        "x": a["x"][0],
        "norm_g": a["norm_g"][0],
        "w_tok1": columns("au", "av", "bq", "bk", "mq", "bv", "cv", "co"),
        "w_fm1": blocks(np.concatenate([columns("az", "bz", "cz", "mz", "cq", "ck", "dr", "dk", "dv", "dz"), low], 1)),
        "sgu_norm_g": a["sgu_norm_g"][0],
        "sgu_wT": a["sgu_w"][0].transpose(2, 0, 1),
        "sgu_b": a["sgu_b"][0].T,
        "conv_w": a["mlstm_conv_w"][0].reshape(4, 4, P).transpose(2, 1, 0),
        "conv_b": col_blocks(a["mlstm_conv_b"][0]),
        "rwkv_mu": col_blocks(row(*[a["rwkv_mu"][0][at[n].start - at["dr"].start:at[n].stop - at["dr"].start]
                                    for n in ("dr", "dk", "dv", "dz")])),
        "f_bias": row(a["fox_f_b"][0], a["mlstm_f_b"][0])[:, None],
        "i_bias": a["mlstm_i_b"][0][:, None],
        "mem": a["mem"][0],
        "mem_norm_g": col_blocks(a["mem_norm_g"][0]),
        "mem_w_kv": a["mem_w_kv"][0],
        "mem_k_g": row(*[a["mem_k_g"][0]] * GH),
        "mlstm_out_g": a["mlstm_out_g"][0],
        "rwkv_low_mu": np.stack([a["rwkv_mu"][0][at[n].start - at["dr"].start:at[n].stop - at["dr"].start]
                                 for n in ("dw", "da")], axis=1),
        "rwkv_up": np.stack([a["rwkv_w2"][0], a["rwkv_a2"][0]], axis=1),
        "rwkv_cols": np.stack([col_blocks(v) for v in (a["rwkv_w0"][0], a["rwkv_a0"][0], a["rwkv_k_k"][0],
                                                       a["rwkv_k_a"][0], a["rwkv_r_k"][0].reshape(-1))], axis=2),
        "rwkv_ln_g": a["rwkv_ln_g"][0],
        "qkm_g": row(*[a["fox_q_g"][0]] * GH, *[a["fox_k_g"][0]] * GH, *[a["mem_q_g"][0]] * GH),
        "w_out1": np.concatenate([w_out[n * GW:(n + 1) * GW] for n in (0, 1, 2, 4, 3)]),
        "cond": np.stack([col_blocks(a["c_2"][0]), col_blocks(a["c_ctx_2"])], axis=2),
        "w_ada": a["w_ada_2"][0],
        "b_ada_cols": col_blocks(b_ada[:2 * DM]),
        "b_ada_gate": b_ada[2 * DM:],
        "norm_g2": col_blocks(a["norm_g_2"][0]),
        "rel_bias": a["rel_bias_2"][0].reshape(-1, REL_C).T,
        "ctx": a["ctx_2"][0],
        "ctx_w_kv": w_in_2[:, 3 * D2:5 * D2],
        "ctx_k_g": row(*[a["k_norm_g_2"][0]] * H2),
        "qk_gain2": np.stack([row(*[a[n][0]] * (P // HD)) for n in ("q_norm_g_2", "k_norm_g_2")], axis=1),
        "w_fm2": blocks(np.concatenate([w_in_2[:, n * D2:(n + 1) * D2] for n in (2, 3, 4, 0, 1, 5)], axis=1)),
        "w_four": a["w_four_2"][0],
        "w_out2": a["w_out_2"][0],
        "dft_channels": np.stack([np.cos(angle_c), np.sin(angle_c)], axis=1).astype(np.float32),
        "dft_tokens": waves.reshape(RADIX * NF_T, P, NF_T * 2 * P).astype(np.float32),
    }
    arrays = {n: np.ascontiguousarray(v) for n, v in arrays.items()}
    nc = bacc.Bacc("TRN2", target_bir_lowering=False, num_devices=1)
    dram = {n: nc.dram_tensor(f"in_{n}", v.shape, F32, kind="ExternalInput").ap() for n, v in arrays.items()}
    dram["out"] = nc.dram_tensor("out", (T, DM), F32, kind="ExternalOutput").ap()
    build(nc, dram, PHASES)
    r = run_bass_kernel_spmd(nc, [{f"in_{n}": v for n, v in arrays.items()}], core_ids=[0])
    return r.results[0]["out"].reshape(1, T, DM)
```
